# Optimizing a Trainium2 kernel written in Bass

```python
import jax, jax.numpy as jnp
from jax import lax
import numpy as np

D_MODEL = 1024
BATCH = 1
SEQ = 1024
DEPTH = 1

GRID_W = 64
CTX_LEN = 256
EPS = 1e-6
N_MOD = 6
RET_HEADS = 4
RET_DK = 256
RET_DV = 256
RET_CHUNK = 128
ROPE_BASE = 10000.0
RET_QK_W = RET_HEADS * RET_DK
RET_V_W = RET_HEADS * RET_DV
CONV_CH = D_MODEL
CONV_WIDTH = 31
IN_WIDTH = 2 * RET_QK_W + 2 * RET_V_W + 2 * CONV_CH + 2 * D_MODEL
IN_SPLITS = (RET_QK_W, 2 * RET_QK_W, 2 * RET_QK_W + RET_V_W, 2 * RET_QK_W + 2 * RET_V_W,
             2 * RET_QK_W + 2 * RET_V_W + CONV_CH, 2 * RET_QK_W + 2 * RET_V_W + 2 * CONV_CH,
             2 * RET_QK_W + 2 * RET_V_W + 2 * CONV_CH + D_MODEL)
PEER_HEADS = 8
PEER_N_KEYS = 128
PEER_N_EXPERTS = PEER_N_KEYS * PEER_N_KEYS
PEER_DK = 256
PEER_DK_HALF = PEER_DK // 2
PEER_TOPK = 16
PEER_BLOCK = 128

kernel_name = "hybrid_retention_conformer_peer_dit_layer"

def _rms_norm(x, gain):
    x32 = x.astype(jnp.float32)
    y = x32 * lax.rsqrt(jnp.mean(x32 * x32, axis=-1, keepdims=True) + EPS)
    return (y * gain.astype(jnp.float32)).astype(x.dtype)

def _layer_norm(x, gain, bias):
    x32 = x.astype(jnp.float32)
    mu = jnp.mean(x32, axis=-1, keepdims=True)
    xc = x32 - mu
    y = xc * lax.rsqrt(jnp.mean(xc * xc, axis=-1, keepdims=True) + EPS)
    return (y * gain.astype(jnp.float32) + bias.astype(jnp.float32)).astype(x.dtype)

def _modulate(h, shift, scale):
    return h * (1.0 + scale) + shift

def _heads(t, n_heads, d_head):
    b, l, _ = t.shape
    return t.reshape(b, l, n_heads, d_head).transpose(0, 2, 1, 3)

def _axial_rotary(n_rows):
    rows = jnp.repeat(jnp.arange(n_rows, dtype=jnp.float32), GRID_W)
    cols = jnp.tile(jnp.arange(GRID_W, dtype=jnp.float32), n_rows)
    quarter = RET_DK // 4
    inv = ROPE_BASE ** (-jnp.arange(quarter, dtype=jnp.float32) / quarter)
    ang = jnp.concatenate([rows[:, None] * inv, cols[:, None] * inv], axis=-1)
    return jnp.cos(ang), jnp.sin(ang)

def _rotary(t, cos, sin):
    t1, t2 = jnp.split(t, 2, axis=-1)
    cos = cos.astype(t.dtype)
    sin = sin.astype(t.dtype)
    return jnp.concatenate([t1 * cos - t2 * sin, t1 * sin + t2 * cos], axis=-1)

def _retention_scan(q, k, v, log_gamma, state0):
    out_dtype = v.dtype
    q = q.astype(jnp.float32)
    k = k.astype(jnp.float32)
    v = v.astype(jnp.float32)
    b, h, l, dk = q.shape
    dv = v.shape[-1]
    nc = l // RET_CHUNK
    lg = log_gamma.astype(jnp.float32)
    pos = jnp.arange(RET_CHUNK, dtype=jnp.float32)
    diff = pos[:, None] - pos[None, :]
    decay_in = jnp.where(diff >= 0, jnp.exp(lg[:, None, None] * jnp.maximum(diff, 0.0)), 0.0)
    q_dec = jnp.exp(lg[:, None] * (pos + 1.0))[:, :, None]
    k_dec = jnp.exp(lg[:, None] * (RET_CHUNK - 1.0 - pos))[:, :, None]
    chunk_dec = jnp.exp(lg * RET_CHUNK)[:, None, None]

    def to_chunks(t):
        return jnp.moveaxis(t.reshape(b, h, nc, RET_CHUNK, t.shape[-1]), 2, 0)

    def step(state, inp):
        qi, ki, vi = inp
        scores = jnp.einsum('bhnd,bhmd->bhnm', qi, ki) * decay_in
        y = jnp.einsum('bhnm,bhme->bhne', scores, vi) + jnp.einsum('bhnd,bhde->bhne', qi * q_dec, state)
        state = state * chunk_dec + jnp.einsum('bhmd,bhme->bhde', ki * k_dec, vi)
        return state, y

    _, ys = lax.scan(step, state0.astype(jnp.float32), (to_chunks(q), to_chunks(k), to_chunks(v)))
    return jnp.moveaxis(ys, 0, 2).reshape(b, h, l, dv).astype(out_dtype)

def _context_states(hc, w_in, log_gamma):
    kv = hc @ w_in[:, IN_SPLITS[0]:IN_SPLITS[2]]
    k, v = jnp.split(kv, [RET_QK_W], axis=-1)
    k = (_heads(k, RET_HEADS, RET_DK) * RET_DK ** -0.5).astype(jnp.float32)
    v = _heads(v, RET_HEADS, RET_DV).astype(jnp.float32)
    l = k.shape[2]
    pos = jnp.arange(l, dtype=jnp.float32)
    lg = log_gamma.astype(jnp.float32)
    w_f = jnp.exp(lg[0][:, None] * (l - 1.0 - pos))
    w_b = jnp.exp(lg[1][:, None] * pos)
    st_f = jnp.einsum('bhld,bhle,hl->bhde', k, v, w_f)
    st_b = jnp.einsum('bhld,bhle,hl->bhde', k, v, w_b)
    return st_f, st_b

def _depthwise_conv(t, w, b):
    ch = t.shape[-1]
    y = lax.conv_general_dilated(t, w[:, None, :].astype(t.dtype), window_strides=(1,),
                                 padding=[(CONV_WIDTH // 2, CONV_WIDTH // 2)],
                                 dimension_numbers=('NWC', 'WIO', 'NWC'), feature_group_count=ch)
    return y + b

def _mixer(h, w_in, log_gamma, w_ret_o, conv_w, conv_b, conv_norm_g, conv_norm_b, w_conv_o, w_out,
           rope, state_f, state_b):
    bsz, l, _ = h.shape
    proj = h @ w_in
    q, k, v, g_ret, glu_a, glu_b, gate_a, gate_b = jnp.split(proj, IN_SPLITS, axis=-1)
    q = _heads(q, RET_HEADS, RET_DK)
    k = _heads(k, RET_HEADS, RET_DK)
    v = _heads(v, RET_HEADS, RET_DV)
    if rope is not None:
        q = _rotary(q, *rope)
        k = _rotary(k, *rope)
    k = k * RET_DK ** -0.5
    y_f = _retention_scan(q, k, v, log_gamma[0], state_f)
    y_b = _retention_scan(jnp.flip(q, axis=2), jnp.flip(k, axis=2), jnp.flip(v, axis=2), log_gamma[1], state_b)
    y = (y_f + jnp.flip(y_b, axis=2)).astype(jnp.float32)
    y = y * lax.rsqrt(jnp.mean(y * y, axis=-1, keepdims=True) + EPS)
    y = y.transpose(0, 2, 1, 3).reshape(bsz, l, RET_V_W).astype(h.dtype)
    branch_a = (y * jax.nn.silu(g_ret)) @ w_ret_o
    u = glu_a * jax.nn.sigmoid(glu_b)
    u = _depthwise_conv(u, conv_w, conv_b)
    u = jax.nn.silu(_layer_norm(u, conv_norm_g, conv_norm_b))
    branch_b = u @ w_conv_o
    merged = jax.nn.sigmoid(gate_a) * branch_a + jax.nn.sigmoid(gate_b) * branch_b
    return merged @ w_out

def _peer(h, w_query, sub_keys, expert_u, expert_v):
    bsz, l, d = h.shape
    blocks = h.reshape(bsz * l // PEER_BLOCK, PEER_BLOCK, d)

    def block(xb):
        q = (xb @ w_query).reshape(PEER_BLOCK, PEER_HEADS, 2, PEER_DK_HALF)
        s = jnp.einsum('thpd,hpnd->thpn', q, sub_keys)
        s_top, i_top = lax.top_k(s, PEER_TOPK)
        cand = s_top[:, :, 0, :, None] + s_top[:, :, 1, None, :]
        cand_idx = i_top[:, :, 0, :, None] * PEER_N_KEYS + i_top[:, :, 1, None, :]
        best, sel = lax.top_k(cand.reshape(PEER_BLOCK, PEER_HEADS, PEER_TOPK * PEER_TOPK), PEER_TOPK)
        experts = jnp.take_along_axis(cand_idx.reshape(PEER_BLOCK, PEER_HEADS, PEER_TOPK * PEER_TOPK), sel, axis=-1)
        g = jax.nn.softmax(best.astype(jnp.float32), axis=-1).astype(xb.dtype)
        act = jax.nn.gelu(jnp.einsum('thkd,td->thk', expert_u[experts], xb))
        return jnp.einsum('thk,thkd->td', g * act, expert_v[experts])

    return lax.map(block, blocks).reshape(bsz, l, d)

def setup_inputs(seed: int = 0) -> dict:
    key = jax.random.key(seed)
    ks = jax.random.split(key, 20)
    f32 = jnp.float32
    d = D_MODEL
    nrm = lambda k, shape, s: jax.random.normal(k, shape, f32) * s
    base_decay = jnp.log(2.0 ** (-5.0 - jnp.arange(RET_HEADS, dtype=f32)))
    return {
        "x": nrm(ks[0], (BATCH, SEQ, d), 1.0),
        "c": nrm(ks[1], (BATCH, d), 1.0),
        "ctx": nrm(ks[2], (BATCH, CTX_LEN, d), 1.0),
        "c_ctx": nrm(ks[3], (d,), 1.0),
        "w_mod": nrm(ks[4], (DEPTH, d, N_MOD * d), 0.5 * d ** -0.5),
        "b_mod": nrm(ks[5], (DEPTH, N_MOD * d), 0.02),
        "norm_gain": 1.0 + nrm(ks[6], (DEPTH, 4, d), 0.05),
        "w_in": nrm(ks[7], (DEPTH, d, IN_WIDTH), d ** -0.5),
        "ret_decay_raw": jnp.broadcast_to(base_decay, (DEPTH, 2, RET_HEADS)) + nrm(ks[8], (DEPTH, 2, RET_HEADS), 0.05),
        "w_ret_o": nrm(ks[9], (DEPTH, RET_V_W, d), RET_V_W ** -0.5),
        "conv_w": nrm(ks[10], (DEPTH, CONV_WIDTH, CONV_CH), CONV_WIDTH ** -0.5),
        "conv_b": nrm(ks[11], (DEPTH, CONV_CH), 0.02),
        "conv_norm_g": 1.0 + nrm(ks[12], (DEPTH, CONV_CH), 0.05),
        "conv_norm_b": nrm(ks[13], (DEPTH, CONV_CH), 0.02),
        "w_conv_o": nrm(ks[14], (DEPTH, CONV_CH, d), CONV_CH ** -0.5),
        "w_out": nrm(ks[15], (DEPTH, d, d), d ** -0.5),
        "peer_wq": nrm(ks[16], (DEPTH, d, PEER_HEADS * PEER_DK), d ** -0.5),
        "peer_keys": nrm(ks[17], (DEPTH, PEER_HEADS, 2, PEER_N_KEYS, PEER_DK_HALF), PEER_DK_HALF ** -0.5),
        "peer_u": nrm(ks[18], (DEPTH, PEER_N_EXPERTS, d), d ** -0.5),
        "peer_v": nrm(ks[19], (DEPTH, PEER_N_EXPERTS, d), (PEER_HEADS * PEER_TOPK) ** -0.5),
    }

def reference(x, c, ctx, c_ctx, w_mod, b_mod, norm_gain, w_in, ret_decay_raw, w_ret_o, conv_w, conv_b,
              conv_norm_g, conv_norm_b, w_conv_o, w_out, peer_wq, peer_keys, peer_u, peer_v):
    lat, cx = x, ctx
    n_lat = lat.shape[1]
    n_rows = n_lat // GRID_W
    rope = _axial_rotary(n_rows)
    for layer in range(DEPTH):
        last = layer == DEPTH - 1
        gain = norm_gain[layer]
        mod_lat = (jax.nn.silu(c) @ w_mod[layer] + b_mod[layer])[:, None, :]
        mod_ctx = (jax.nn.silu(c_ctx) @ w_mod[layer] + b_mod[layer])[None, None, :]
        sh1, sc1, g1, sh2, sc2, g2 = jnp.split(mod_lat, N_MOD, axis=-1)
        csh1, csc1, cg1, csh2, csc2, cg2 = jnp.split(mod_ctx, N_MOD, axis=-1)
        log_gamma = -jax.nn.softplus(ret_decay_raw[layer])
        mixer_w = (w_in[layer], log_gamma, w_ret_o[layer], conv_w[layer], conv_b[layer],
                   conv_norm_g[layer], conv_norm_b[layer], w_conv_o[layer], w_out[layer])
        peer_w = (peer_wq[layer], peer_keys[layer], peer_u[layer], peer_v[layer])
        hc = _modulate(_rms_norm(cx, gain[0]), csh1, csc1)
        st_f, st_b = _context_states(hc, w_in[layer], log_gamma)
        h = _modulate(_rms_norm(lat, gain[0]), sh1, sc1)
        y = _mixer(h, *mixer_w, rope, st_f, st_b)
        lat = lat + g1 * _rms_norm(y, gain[1])
        h = _modulate(_rms_norm(lat, gain[2]), sh2, sc2)
        lat = lat + g2 * _rms_norm(_peer(h, *peer_w), gain[3])
        if not last:
            zeros = jnp.zeros((cx.shape[0], RET_HEADS, RET_DK, RET_DV), jnp.float32)
            yc = _mixer(hc, *mixer_w, None, zeros, zeros)
            cx = cx + cg1 * _rms_norm(yc, gain[1])
            hc2 = _modulate(_rms_norm(cx, gain[2]), csh2, csc2)
            cx = cx + cg2 * _rms_norm(_peer(hc2, *peer_w), gain[3])
    return lat


_drawn_inputs = setup_inputs


def setup_inputs(seed=0):
    import zlib

    import numpy as np

    out = dict(_drawn_inputs(seed))
    spreads = {}
    factors = {}
    for name, (base, spread) in spreads.items():
        noise = np.random.default_rng([zlib.crc32(name.encode()), seed]).standard_normal(out[name].shape)
        drawn = base * np.exp(spread * noise) if base else spread * noise
        out[name] = __import__('jax').numpy.asarray(drawn.astype(out[name].dtype))
    for name, factor in factors.items():
        out[name] = (out[name] * factor).astype(out[name].dtype)
    return out
```

```python
import numpy as np
from contextlib import ExitStack

import concourse.bass as bass
from concourse import mybir
from concourse.alu_op_type import AluOpType as ALU

ACT = mybir.ActivationFunctionType
AX = mybir.AxisListType
F32 = mybir.dt.float32
F32R = mybir.dt.float32r
BF16 = mybir.dt.bfloat16
I32 = mybir.dt.int32
U32 = mybir.dt.uint32

P = 128
SEQ = 1024
CTX = 256
D = 1024
KT = D // P
TT = SEQ // P
CT = CTX // P
HALF = 512
NB = 512
EPS = 1e-6
HEADS = 4
DK = 256
GRID_W = 64
CONV_W = 31


class Pool:

    def __init__(self, nc, ctx, side="left"):
        self.nc, self.ctx, self.side, self.sems = nc, ctx, side, []
        ctx.callback(self.give_back)

    def give_back(self):
        if self.sems:
            self.nc.clear_and_free_semaphores(self.sems)
            self.nc.all_engine_barrier()

    def sem(self, name):
        self.sems.append(self.nc.alloc_semaphore(name))
        return self.sems[-1]

    def sb(self, name, shape, dt=F32):
        return self.ctx.enter_context(self.nc.sbuf_tensor(name, shape, dt, side=self.side))

    def ps(self, name, shape, dt=F32):
        return self.ctx.enter_context(self.nc.psum_tensor(name, shape, dt))


class Chain:

    def __init__(self, eng, sem, base=0, per_turn=0, i=0):
        self.eng, self.sem, self.base, self.per_turn, self.i, self.taken = eng, sem, base, per_turn, i, 0

    def step(self, instruction):
        self.taken += 1
        instruction.then_inc(self.sem, 1)
        count = self.base + self.taken
        self.eng.wait_ge(self.sem, self.i * self.per_turn + count if self.per_turn else count)


def f32(ap):
    return ap.bitcast(F32)


def split_matmuls(nc, out, pairs):
    last = None
    for n, ((s_hi, s_lo), (m_hi, m_lo)) in enumerate(pairs):
        nc.tensor.matmul(out, s_hi, m_hi, start=(n == 0), stop=False)
        nc.tensor.matmul(out, s_hi, m_lo, start=False, stop=False)
        last = nc.tensor.matmul(out, s_lo, m_hi, start=False, stop=(n == len(pairs) - 1))
    return last

BLOCKS = ["glu_a", "glu_b", "glu_a", "glu_b", "q", "q", "k", "k",
          "gate_a", "gate_a", "gate_b", "gate_b", "v", "v", "g_ret", "g_ret"]
W_IN_ORDER = [8, 10, 9, 11, 0, 1, 2, 3, 12, 13, 14, 15, 4, 5, 6, 7]
FM_ROWS = 12 * NB


def input_projection(nc, w_blocks, h_hi, h_lo, hc_hi, hc_lo, fm, tm, ctx_kv, conv_w, conv_b, conv):
    with ExitStack() as ctx:
        p = Pool(nc, ctx)
        RING = 4
        raw = p.sb("ip_raw", [P, KT * NB])
        w_hi = [p.sb(f"ip_w_hi{b}", [P, KT * NB], F32R) for b in range(2)]
        w_lo = [p.sb(f"ip_w_lo{b}", [P, KT * NB], F32R) for b in range(2)]
        stage = p.sb("ip_stage", [P, RING, HALF])
        bank = [p.ps(f"ip_bank{b}", [P, HALF]) for b in range(RING)]

        glu = p.sb("ip_glu", [P, 2, SEQ])
        PAD = CONV_W // 2
        padded = [p.sb(f"ip_padded{b}", [P, SEQ + 2 * PAD]) for b in range(2)]
        convolved = p.sb("ip_convolved", [P, 2, SEQ])
        taps = p.sb("ip_taps", [P, KT, CONV_W])
        conv_bias = p.sb("ip_conv_bias", [P, KT])

        taps_loaded = p.sem("ip_taps_loaded")
        glu_loaded = p.sem("ip_glu_loaded")
        sigmoid_ready = p.sem("ip_sigmoid_ready")
        glu_ready = p.sem("ip_glu_ready")
        conv_chain = p.sem("ip_conv_chain")
        conv_ready = p.sem("ip_conv_ready")
        conv_stored = [p.sem(f"ip_conv_stored{b}") for b in range(2)]
        raw_loaded = p.sem("ip_raw_loaded")
        hi_ready = p.sem("ip_hi_ready")
        lo_ready = p.sem("ip_lo_ready")
        group_done = p.sem("ip_group_done")
        evacuated = p.sem("ip_evacuated")
        stored = [p.sem(f"ip_stored{r}") for r in range(RING)]

        SEGMENTS = [(0, 2, False, False, True), (4, 1, False, False, False), (6, 1, False, True, False),
                    (8, 2, False, False, True), (12, 1, True, True, False), (14, 1, True, False, False)]
        N_BLOCKS = 16
        CONV_FIRST = 4

        def walk(eng, visit):
            group = 0
            for first, pairs, token_major, context, rolled in SEGMENTS:
                per_block = 8 + (CT if context else 0)
                if rolled:
                    with eng.Fori(0, pairs, 1) as i:
                        for b in range(2):
                            visit(first + b, i, b, group + b * per_block, 2 * per_block,
                                  token_major, context, True, True)
                else:
                    for b in range(2):
                        blk = first + b
                        visit(blk, 0, b, group + b * per_block, 0, token_major, context,
                              blk + 1 < N_BLOCKS, blk + 2 < N_BLOCKS)
                group += 2 * pairs * per_block

        block = ctx.enter_context(nc.Block())

        @block.sync
        def _(sp):
            for r in range(RING):
                sp.sem_inc(stored[r], 16)
            sp.dma_start(raw[:], w_blocks[0]).then_inc(raw_loaded, 16)
            sp.dma_start(taps[:], conv_w).then_inc(taps_loaded, 16)
            sp.dma_start(conv_bias[:], conv_b).then_inc(taps_loaded, 16)
            for b in range(2):
                sp.sem_inc(conv_stored[b], 16)
            sp.sem_inc(conv_ready, 2)
            sp.wait_ge(lo_ready, 1)
            sp.dma_start(raw[:], w_blocks[1]).then_inc(raw_loaded, 16)

            def visit(blk, i, b, group, step, token_major, context, ahead, load):
                if load:
                    sp.wait_ge(lo_ready, blk + 2 + 2 * i)
                    src = w_blocks[bass.ds(blk + 2 + 2 * i, 1)] if step else w_blocks[blk + 2:blk + 3]
                    sp.dma_start(raw[:], src.rearrange("o p n -> (o p) n")).then_inc(raw_loaded, 16)
                tile = blk - CONV_FIRST
                if 0 <= tile < KT:
                    if tile == 0:
                        for r in range(RING):
                            sp.wait_ge(stored[r], 16 * (CONV_FIRST * 8 // RING + 1))
                    else:
                        sp.wait_ge(glu_ready, tile + 2 * i)
                    row = tile * P + (tile // 4) * NB
                    rows = fm[bass.ds(row + 2 * P * i, P + NB), :] if step else fm[row:row + P + NB, :]
                    for j in range(2):
                        sp.dma_start(glu[:, j, :], rows[j * NB:j * NB + P, :]).then_inc(glu_loaded, 16)
                if 0 < tile <= KT:
                    store_tile(tile - 1, i if step else 0, step)
                for g in range(8 + (CT if context else 0)):
                    sp.wait_ge(evacuated, group + g + 1 + RING + step * i)
                    slot = (group + g) % RING
                    if g >= 8:
                        j = (blk - 6) if blk < 8 else (blk - 12 + 2)
                        dst = ctx_kv[2 * j:2 * j + 2, (g - 8) * P:(g - 7) * P, :].rearrange("e t d -> t e d")
                    elif token_major:
                        h = 2 * (blk - 12)
                        dst = tm[h:h + 2, g * P:(g + 1) * P, :].rearrange("e t d -> t e d")
                    else:
                        row = blk * NB + (g // 2) * P
                        cols = slice((g % 2) * HALF, (g % 2 + 1) * HALF)
                        dst = fm[bass.ds(row + 2 * NB * i, P), cols] if step else fm[row:row + P, cols]
                    src = stage[:, slot, :]
                    if g >= 8 or token_major:
                        src = src.rearrange("p (e d) -> p e d", e=2)
                    sp.dma_start(dst, src).then_inc(stored[slot], 16)

            def store_tile(tile, i, step):
                sp.wait_ge(conv_ready, tile + 3 + 2 * i)
                dst = conv[bass.ds(tile * P + 2 * P * i, P), :] if step else conv[tile * P:(tile + 1) * P, :]
                sp.dma_start(dst, convolved[:, tile % 2, :]).then_inc(conv_stored[tile % 2], 16)

            walk(sp, visit)
            for b in range(2):
                sp.wait_ge(conv_stored[b], 16 * (KT // 2 + 1))
            total = 16 * 8 + 4 * CT
            for r in range(RING):
                sp.wait_ge(stored[r], 16 * (total // RING + 1))

        @block.scalar
        def _(act):
            def split(blk, i, b):
                act.wait_ge(raw_loaded, 16 * (blk + 1) + 32 * i)
                nc.scalar.activation(w_hi[b][:], raw[:], ACT.Copy).then_inc(hi_ready, 1)

            split(0, 0, 0)

            def visit(blk, i, b, group, step, token_major, context, ahead, load):
                if ahead:
                    split(blk + 1, i, 1 - b)
                tile = blk - CONV_FIRST
                for g in range(8 + (CT if context else 0)):
                    if g == 1 and 0 <= tile < KT:
                        act.wait_ge(glu_loaded, 32 * (tile + 1) + 64 * i)
                        nc.scalar.activation(glu[:, 1, :], glu[:, 1, :], ACT.Sigmoid).then_inc(sigmoid_ready, 1)
                    slot = (group + g) % RING
                    act.wait_ge(group_done, group + g + 1 + step * i)
                    act.wait_ge(stored[slot], 16 * ((group + g) // RING + 1) + 16 * (step // RING) * i)
                    nc.scalar.activation(stage[:, slot, :], bank[slot][:], ACT.Copy).then_inc(evacuated, 1)

            walk(act, visit)

        @block.vector
        def _(dve):
            def visit(blk, i, b, group, step, token_major, context, ahead, load):
                tile = blk - CONV_FIRST
                if 0 <= tile < KT:
                    chain = Chain(dve, conv_chain, (CONV_W - 1) * tile, 2 * (CONV_W - 1) if step else 0, i)
                    out = convolved[:, tile % 2, :]
                    tap = taps[:, bass.ds(tile + 2 * i, 1), :] if step else taps[:, tile:tile + 1, :]
                    tap = tap.rearrange("p o w -> p (o w)")
                    bias = conv_bias[:, bass.ds(tile + 2 * i, 1)] if step else conv_bias[:, tile:tile + 1]
                    dve.wait_ge(glu_ready, tile + 1 + 2 * i)
                    dve.wait_ge(conv_stored[tile % 2], 16 * (tile // 2 + 1) + 16 * i)
                    chain.step(nc.vector.tensor_scalar(out, padded[tile % 2][:, 0:SEQ], tap[:, 0:1], bias, ALU.mult, ALU.add))
                    for w in range(1, CONV_W):
                        add = nc.vector.scalar_tensor_tensor(out=out, in0=padded[tile % 2][:, w:w + SEQ], scalar=tap[:, w:w + 1],
                                                             in1=out, op0=ALU.mult, op1=ALU.add)
                        if w < CONV_W - 1:
                            chain.step(add)
                        else:
                            add.then_inc(conv_ready, 1)

            dve.wait_ge(taps_loaded, 32)
            walk(dve, visit)

        @block.gpsimd
        def _(pool):
            def low_part(blk, i, b):
                pool.wait_ge(hi_ready, blk + 1 + 2 * i)
                nc.gpsimd.tensor_tensor(w_lo[b][:], raw[:], f32(w_hi[b][:]), ALU.subtract).then_inc(lo_ready, 1)

            for b in range(2):
                nc.gpsimd.memset(padded[b][:, 0:PAD], 0.0)
                nc.gpsimd.memset(padded[b][:, SEQ + PAD:], 0.0)
            low_part(0, 0, 0)

            def visit(blk, i, b, group, step, token_major, context, ahead, load):
                if ahead:
                    low_part(blk + 1, i, 1 - b)
                tile = blk - CONV_FIRST
                if 0 <= tile < KT:
                    pool.wait_ge(sigmoid_ready, tile + 1 + 2 * i)
                    pool.wait_ge(conv_ready, tile + 1 + 2 * i)
                    nc.gpsimd.tensor_tensor(padded[tile % 2][:, PAD:PAD + SEQ], glu[:, 0, :], glu[:, 1, :],
                                            ALU.mult).then_inc(glu_ready, 1)

            walk(pool, visit)

        @block.tensor
        def _(pe):
            pe.sem_inc(evacuated, RING)

            def visit(blk, i, b, group, step, token_major, context, ahead, load):
                pe.wait_ge(lo_ready, blk + 1 + 2 * i)
                wh = w_hi[b][:].rearrange("p (k n) -> p k n", k=KT)
                wl = w_lo[b][:].rearrange("p (k n) -> p k n", k=KT)
                for g in range(8 + (CT if context else 0)):
                    slot = (group + g) % RING
                    pe.wait_ge(evacuated, group + g + 1 + step * i)
                    if g >= 8:
                        c = slice((g - 8) * P, (g - 7) * P)
                        pairs = [((hc_hi[:, k, c], hc_lo[:, k, c]), (wh[:, k, :], wl[:, k, :])) for k in range(KT)]
                    elif token_major:
                        c = slice(g * P, (g + 1) * P)
                        pairs = [((h_hi[:, k, c], h_lo[:, k, c]), (wh[:, k, :], wl[:, k, :])) for k in range(KT)]
                    else:
                        n = slice((g // 2) * P, (g // 2 + 1) * P)
                        c = slice((g % 2) * HALF, (g % 2 + 1) * HALF)
                        pairs = [((wh[:, k, n], wl[:, k, n]), (h_hi[:, k, c], h_lo[:, k, c])) for k in range(KT)]
                    split_matmuls(nc, bank[slot][:], pairs).then_inc(group_done, 1)

            walk(pe, visit)


def rsqrt_of_mean(nc, chain, act_sqrt, out, sums, scratch, n):
    v = nc.vector
    mean, root, y2 = scratch
    chain.step(v.tensor_scalar(mean, sums, 1.0 / n, EPS, ALU.mult, ALU.add))
    act_sqrt(root, mean)
    chain.step(v.reciprocal(out, root))
    chain.step(v.tensor_tensor(y2, out, out, ALU.mult))
    chain.step(v.tensor_tensor(y2, y2, mean, ALU.mult))
    chain.step(v.tensor_scalar(y2, y2, -0.5, 1.5, ALU.mult, ALU.add))
    chain.step(v.tensor_tensor(out, out, y2, ALU.mult))

SH1, SC1, G1, SH2, SC2, G2 = range(6)


def conditioning(nc, c_cols, w_mod_blocks, b_mod_cols, gain_cols, mod, rows, ones, ident):
    NBLK = 12
    with ExitStack() as ctx:
        p = Pool(nc, ctx)
        w = [p.sb(f"cd_w{b}", [P, KT, NB]) for b in range(3)]
        c2 = p.sb("cd_c", [P, KT, 2])
        c2s = p.sb("cd_cs", [P, KT, 2])
        bias = p.sb("cd_bias", [P, 6, KT])
        gain = p.sb("cd_gain", [P, 4, KT])
        lat = p.sb("cd_lat", [P, 6, KT])
        cmod = p.sb("cd_cmod", [P, 2, KT])
        g12 = p.sb("cd_g12", [P, 2, KT])
        diag = p.sb("cd_diag", [P, 2, D])
        row2 = p.sb("cd_row2", [2, 6 * D])
        row_bank = [p.ps(f"cd_row_bank{b}", [2, NB]) for b in range(2)]
        acc = p.ps("cd_acc", [P, 6 * KT, 2])
        spread = [p.ps(f"cd_spread{n}", [P, HALF]) for n in range(4)]
        small_loaded = p.sem("cd_small_loaded")
        w_loaded = [p.sem(f"cd_w_loaded{b}") for b in range(3)]
        w_used = p.sem("cd_w_used")
        silu_ready = p.sem("cd_silu_ready")
        row_copied = p.sem("cd_row_copied")
        turned = p.sem("cd_turned")
        chained = p.sem("cd_chained")
        diag_ready = p.sem("cd_diag_ready")
        spread_done = p.sem("cd_spread_done")
        block = ctx.enter_context(nc.Block())

        @block.sync
        def _(sp):
            sp.dma_start(c2[:], c_cols).then_inc(small_loaded, 16)
            sp.dma_start(bias[:], b_mod_cols).then_inc(small_loaded, 16)
            sp.dma_start(gain[:], gain_cols).then_inc(small_loaded, 16)
            for n in range(NBLK):
                if n >= 3:
                    sp.wait_ge(w_used, n - 2)
                sp.dma_start(w[n % 3][:].rearrange("p k n -> p (k n)"), w_mod_blocks[n]).then_inc(w_loaded[n % 3], 16)

        @block.scalar
        def _(act):
            act.wait_ge(small_loaded, 48)
            nc.scalar.activation(c2s[:], c2[:], ACT.Silu).then_inc(silu_ready, 1)
            for n in range(NBLK):
                act.wait_ge(w_used, n + 1)
                nc.scalar.activation(row2[:, n * NB:(n + 1) * NB], row_bank[n % 2][:], ACT.Copy).then_inc(row_copied, 1)

        @block.tensor
        def _(pe):
            pe.wait_ge(silu_ready, 1)
            for n in range(NBLK):
                pe.wait_ge(w_loaded[n % 3], 16 * (n // 3 + 1))
                if n >= 2:
                    pe.wait_ge(row_copied, n - 1)
                for k in range(KT):
                    mm = nc.tensor.matmul(row_bank[n % 2][:], c2s[:, k, :], w[n % 3][:, k, :],
                                          start=(k == 0), stop=(k == KT - 1))
                mm.then_inc(w_used, 1)
            pe.wait_ge(row_copied, NBLK)
            for m in range(6 * KT):
                tr = nc.tensor.transpose(acc[:, m, :], row2[:, m * P:(m + 1) * P], ident[0:2, 0:2])
            tr.then_inc(turned, 1)
            pe.wait_ge(diag_ready, 1)
            for n in range(4):
                mm = nc.tensor.matmul(spread[n][:], ones, diag[:, n // 2, (n % 2) * HALF:(n % 2 + 1) * HALF],
                                      start=True, stop=True)
            mm.then_inc(spread_done, 1)

        @block.vector
        def _(dve):
            v = nc.vector
            chain = Chain(dve, chained)
            dve.wait_ge(small_loaded, 48)
            dve.wait_ge(turned, 1)
            sums = acc[:].rearrange("p (m k) c -> p m k c", m=6)
            chain.step(v.tensor_tensor(lat[:], sums[:, :, :, 0], bias[:], ALU.add))
            chain.step(v.tensor_tensor(cmod[:], sums[:, 0:2, :, 1], bias[:, 0:2, :], ALU.add))
            for a, b, source, sh, sc, g in (("a1", "b1", lat, SH1, SC1, 0), ("a2", "b2", lat, SH2, SC2, 2),
                                            ("ac", "bc", cmod, SH1, SC1, 0)):
                chain.step(v.scalar_tensor_tensor(out=mod[a][:], in0=source[:, sc, :], scalar=1.0, in1=gain[:, g, :],
                                                  op0=ALU.add, op1=ALU.mult))
                chain.step(v.tensor_copy(mod[b][:], source[:, sh, :]))
            chain.step(v.tensor_tensor(g12[:, 0, :], lat[:, G1, :], gain[:, 1, :], ALU.mult))
            chain.step(v.tensor_tensor(g12[:, 1, :], lat[:, G2, :], gain[:, 3, :], ALU.mult))
            for m in range(2):
                for k in range(KT):
                    last = v.tensor_scalar(diag[:, m, k * P:(k + 1) * P], ident, g12[:, m, k:k + 1], None, ALU.mult)
            last.then_inc(diag_ready, 1)
            dve.wait_ge(spread_done, 1)
            for m, row in enumerate((rows["g1"], rows["g2"])):
                for half in range(2):
                    v.tensor_copy(row[:, half * HALF:(half + 1) * HALF], spread[2 * m + half][:])


def normalise(nc, name, sources, groups, ident):
    with ExitStack() as ctx:
        p = Pool(nc, ctx)
        RING = 4
        tiles = sum(x.shape[1] for x, _ in sources)
        at = [sum(x.shape[1] for x, _ in sources[:n]) for n in range(len(sources))]
        squares = p.sb(name + "_squares", [P, D])
        sums = p.sb(name + "_sums", [P, tiles])
        rstd = p.sb(name + "_rstd", [P, tiles])
        scratch = [p.sb(f"{name}_scratch{n}", [P, tiles]) for n in range(3)]
        value = p.sb(name + "_value", [P, RING, HALF])
        bank = [p.ps(f"{name}_bank{b}", [P, HALF]) for b in range(RING)]
        loaded = [p.sem(f"{name}_loaded{n}") for n in range(len(sources))]
        summed = p.sem(name + "_summed")
        mean_ready = p.sem(name + "_mean_ready")
        root_ready = p.sem(name + "_root_ready")
        chained = p.sem(name + "_chained")
        scaled = p.sem(name + "_scaled")
        turned = p.sem(name + "_turned")
        valued = p.sem(name + "_valued")
        high = p.sem(name + "_high")
        low = p.sem(name + "_low")
        block = ctx.enter_context(nc.Block())

        @block.sync
        def _(sp):
            for n, (x, dram) in enumerate(sources):
                if dram is not None:
                    sp.dma_start(x, dram).then_inc(loaded[n], 16)

        @block.scalar
        def _(act):
            for n, (x, dram) in enumerate(sources):
                if dram is not None:
                    act.wait_ge(loaded[n], 16)
                for t in range(x.shape[1]):
                    c = at[n] + t
                    if c:
                        act.wait_ge(summed, c)
                    nc.scalar.activation(squares[:], x[:, t, :], ACT.Square, accum_out=sums[:, c:c + 1]).then_inc(summed, 1)
            act.wait_ge(mean_ready, 1)
            nc.scalar.activation(scratch[1][:], scratch[0][:], ACT.Sqrt).then_inc(root_ready, 1)
            for g, (_, _, m, _, _, _, hi, _) in enumerate(groups):
                act.wait_ge(valued, g + 1)
                nc.scalar.activation(hi, value[:, g % RING, 0:m * P], ACT.Copy).then_inc(high, 1)

        @block.vector
        def _(dve):
            v = nc.vector
            chain = Chain(dve, chained)
            dve.wait_ge(summed, tiles)

            def act_sqrt(root, mean):
                v.tensor_copy(scratch[2][:], mean).then_inc(mean_ready, 1)
                dve.wait_ge(root_ready, 1)

            rsqrt_of_mean(nc, chain, act_sqrt, rstd[:], sums[:], (scratch[0][:], scratch[1][:], scratch[2][:]), D)
            for n, (x, _) in enumerate(sources):
                for t in range(x.shape[1]):
                    v.tensor_scalar(x[:, t, :], x[:, t, :], rstd[:, at[n] + t:at[n] + t + 1], None, ALU.mult).then_inc(scaled, 1)

            def low_part(g):
                m, lo, hi = groups[g][2], groups[g][7], groups[g][6]
                dve.wait_ge(high, g + 1)
                v.tensor_tensor(lo, value[:, g % RING, 0:m * P], f32(hi), ALU.subtract).then_inc(low, 1)

            for g, (_, _, m, _, a, b, _, _) in enumerate(groups):
                dve.wait_ge(turned, g + 1)
                if g >= RING:
                    dve.wait_ge(low, g - RING + 1)
                v.tensor_scalar(value[:, g % RING, 0:m * P], bank[g % RING][:, 0:m * P], a, b,
                                ALU.mult, ALU.add).then_inc(valued, 1)
                if g >= 1:
                    low_part(g - 1)
            low_part(len(groups) - 1)

        @block.tensor
        def _(pe):
            pe.wait_ge(scaled, tiles)
            for g, (n, first, m, k, _, _, _, _) in enumerate(groups):
                if g >= RING:
                    pe.wait_ge(valued, g - RING + 1)
                for t in range(m):
                    tr = nc.tensor.transpose(bank[g % RING][:, t * P:(t + 1) * P],
                                             sources[n][0][:, first + t, k * P:(k + 1) * P], ident)
                tr.then_inc(turned, 1)


def constants(nc, ones, ident):
    with ExitStack() as ctx:
        p = Pool(nc, ctx)
        zeroed = p.sem("cs_zeroed")
        block = ctx.enter_context(nc.Block())

        @block.gpsimd
        def _(pool):
            nc.gpsimd.memset(ones[:], 1.0)
            nc.gpsimd.memset(ident[:], 0.0).then_inc(zeroed, 1)
            pool.wait_ge(zeroed, 1)
            nc.gpsimd.affine_select(out=ident[:], in_=ident[:], compare_op=ALU.not_equal, fill=1.0, base=0,
                                    pattern=[[-1, P]], channel_multiplier=1)

CHUNK = 128
NC_ = SEQ // CHUNK
Q_ROW, K_ROW = 4 * NB, 6 * NB

ROTATE_STEPS = 3


def rotate(engine, chain, out, raw, cos_sin, tmp, done):
    cos, sin = cos_sin[:, 0, :], cos_sin[:, 1, :]
    engine.tensor_tensor(out[:, 0, :], raw[:, 0, :], cos, ALU.mult)
    engine.tensor_tensor(out[:, 1, :], raw[:, 0, :], sin, ALU.mult)
    chain.step(engine.tensor_tensor(tmp[:], raw[:, 1, :], sin, ALU.mult))
    chain.step(engine.tensor_tensor(out[:, 0, :], out[:, 0, :], tmp[:], ALU.subtract))
    chain.step(engine.tensor_tensor(tmp[:], raw[:, 1, :], cos, ALU.mult))
    engine.tensor_tensor(out[:, 1, :], out[:, 1, :], tmp[:], ALU.add).then_inc(done, 1)


def retention(nc, fm, tm, ctx_kv, decay_raw, cos_sin, yg_hi, yg_lo, ident):
    with ExitStack() as ctx:
        p = Pool(nc, ctx)
        q_raw = p.sb("rt_q_raw", [P, 2, SEQ])
        k_raw = p.sb("rt_k_raw", [P, 2, SEQ])
        q = p.sb("rt_q", [P, 2, SEQ])
        k = p.sb("rt_k", [P, 2, SEQ])
        v = p.sb("rt_v", [P, NC_, DK])
        gate = p.sb("rt_gate", [P, NC_, DK])
        kc = p.sb("rt_kc", [P, CT, DK])
        vc = p.sb("rt_vc", [P, CT, DK])
        kcd = [p.sb(f"rt_kcd{d}", [P, CT, DK]) for d in range(2)]
        kd = [p.sb(f"rt_kd{d}", [P, NC_, DK]) for d in range(2)]
        state = [p.sb(f"rt_state{d}", [P, 2, DK]) for d in range(2)]
        y = p.sb("rt_y", [P, NC_, DK])
        weights = p.sb("rt_weights", [P, NC_, CHUNK])
        cs = p.sb("rt_cos_sin", [P, 2, SEQ])
        tmp_q = p.sb("rt_tmp_q", [P, SEQ])
        tmp_k = p.sb("rt_tmp_k", [P, SEQ])
        value = p.sb("rt_value", [P, 2, HALF])
        dist = p.sb("rt_dist", [P, 2, CHUNK])
        side = p.sb("rt_side", [P, 2, CHUNK])
        delta = p.sb("rt_delta", [P, CHUNK])
        powers = p.sb("rt_powers", [P, 2, 5])
        power_i = p.sb("rt_power_i", [P, 2, 5], I32)
        delta_i = p.sb("rt_delta_i", [P, CHUNK], I32)
        dec = p.sb("rt_dec", [P, 2, 5])
        mask2 = p.sb("rt_mask2", [P, 2, CHUNK])
        mask = p.sb("rt_mask", [P, CHUNK])
        raw_all = p.sb("rt_raw_all", [P, 2, HEADS])
        raw_dec = p.sb("rt_raw_dec", [P, 2])
        lg = p.sb("rt_lg", [P, 2])
        small = [p.sb(f"rt_small{n}", [P, 2]) for n in range(6)]
        square = p.sb("rt_square", [P, DK])
        sums = p.sb("rt_sums", [P, NC_])
        rstd = p.sb("rt_rstd", [P, NC_])
        scratch = [p.sb(f"rt_scratch{n}", [P, NC_]) for n in range(3)]

        work = [p.ps(f"rt_work{b}", [P, HALF]) for b in range(2)]
        upd = [p.ps(f"rt_upd{d}", [P, 2, DK]) for d in range(2)]
        cross = [[p.ps(f"rt_cross{d}{b}", [P, DK]) for b in range(2)] for d in range(2)]

        tables_loaded = p.sem("rt_tables_loaded")
        made = p.sem("rt_made")
        decay_loaded = p.sem("rt_decay_loaded")
        q_loaded, k_loaded, kc_loaded, vc_loaded, v_loaded, g_loaded = (
            p.sem(f"rt_{x}_loaded") for x in ("q", "k", "kc", "vc", "v", "g"))
        q_rotated = p.sem("rt_q_rotated")
        k_rotated = p.sem("rt_k_rotated")
        pool_chain = p.sem("rt_pool_chain")
        dve_chain = p.sem("rt_dve_chain")
        lg_exp = p.sem("rt_lg_exp")
        lg_asked = p.sem("rt_lg_asked")
        lg_ready = p.sem("rt_lg_ready")
        decays = p.sem("rt_decays")
        kc_scaled = p.sem("rt_kc_scaled")
        ctx_done = p.sem("rt_ctx_done")
        state_set = p.sem("rt_state_set")
        kt_done, kt_read = p.sem("rt_kt_done"), p.sem("rt_kt_read")
        sc_done, sc_read = p.sem("rt_sc_done"), p.sem("rt_sc_read")
        in_done, in_read = p.sem("rt_in_done"), p.sem("rt_in_read")
        yt_done, yt_read = p.sem("rt_yt_done"), p.sem("rt_yt_read")
        stepped = p.sem("rt_stepped")
        advanced = p.sem("rt_advanced")
        y_summed = p.sem("rt_y_summed")
        squared = p.sem("rt_squared")
        root_asked = p.sem("rt_root_asked")
        root_ready = p.sem("rt_root_ready")
        silu_ready = p.sem("rt_silu_ready")
        gated = p.sem("rt_gated")
        high = p.sem("rt_high")
        low = p.sem("rt_low")

        block = ctx.enter_context(nc.Block())

        @block.sync
        def _(sp):
            sp.sem_inc(q_rotated, 1)
            sp.dma_start(raw_all[:].rearrange("p d h -> p (d h)"),
                         decay_raw.rearrange("(o d) h -> o (d h)", o=1).to_broadcast([P, 2 * HEADS])).then_inc(decay_loaded, 16)
            sp.dma_start(cs[:], cos_sin).then_inc(tables_loaded, 16)
            with sp.Fori(0, HEADS, 1) as i:
                q_row, k_row = sp.snap(i * DK + Q_ROW), sp.snap(i * DK + K_ROW)
                v_head, g_head = sp.snap(i * 1), sp.snap(i + HEADS)
                sp.wait_ge(q_rotated, i + 1)
                sp.dma_start(q_raw[:], fm[bass.ds(q_row, DK), :].rearrange("(j p) t -> p j t", p=P)).then_inc(q_loaded, 16)
                sp.wait_ge(k_rotated, i + 1)
                sp.dma_start(k_raw[:], fm[bass.ds(k_row, DK), :].rearrange("(j p) t -> p j t", p=P)).then_inc(k_loaded, 16)
                sp.wait_ge(ctx_done, i + 1)
                sp.dma_start(kc[:], ctx_kv[bass.ds(i, 1)].rearrange("o (c p) d -> p (o c) d", p=P)).then_inc(kc_loaded, 16)
                sp.dma_start(vc[:], ctx_kv[bass.ds(g_head, 1)].rearrange("o (c p) d -> p (o c) d", p=P)).then_inc(vc_loaded, 16)
                sp.wait_ge(stepped, i * 16 + 16)
                sp.dma_start(v[:], tm[bass.ds(i, 1)].rearrange("o (c p) d -> p (o c) d", p=P)).then_inc(v_loaded, 16)
                sp.wait_ge(gated, i + 1)
                sp.dma_start(gate[:], tm[bass.ds(g_head, 1)].rearrange("o (c p) d -> p (o c) d", p=P)).then_inc(g_loaded, 16)

        @block.gpsimd
        def _(pool):
            g = nc.gpsimd
            pool.sem_inc(k_rotated, 1)
            for d, cols in enumerate((((1, 1), (-1, CHUNK - 1), (0, CHUNK), (-1, CTX - 1), (-1, CTX - 1 - P)),
                                      ((-1, CHUNK), (1, 0), (0, CHUNK), (1, 0), (1, P)))):
                for c, (mult, base) in enumerate(cols):
                    g.iota(power_i[:, d, c:c + 1], pattern=[[0, 1]], base=base, channel_multiplier=mult)
            g.iota(delta_i[:], pattern=[[1, CHUNK]], base=0, channel_multiplier=-1).then_inc(made, 1)
            pool.wait_ge(tables_loaded, 16)
            with pool.Fori(0, HEADS, 1) as i:
                pool.wait_ge(k_loaded, 16 * i + 16)
                chain = Chain(pool, pool_chain, 0, ROTATE_STEPS, i)
                pool.wait_ge(sc_done, i * 2 + 2)
                rotate(g, chain, k, k_raw, cs, tmp_k, k_rotated)

        @block.scalar
        def _(act):
            s = nc.scalar
            with act.Fori(0, HEADS, 1) as i:
                act.wait_ge(lg_asked, 2 * i + 1)
                s.activation(small[1][:], small[0][:], ACT.Exp).then_inc(lg_exp, 1)
                act.wait_ge(lg_asked, 2 * i + 2)
                s.activation(small[3][:], small[2][:], ACT.Ln).then_inc(lg_exp, 1)
                act.wait_ge(lg_ready, i + 1)
                for d in range(2):
                    s.activation(dec[:, d, :], powers[:, d, :], ACT.Exp, scale=lg[:, d:d + 1])
                    last = s.activation(mask2[:, d, :], dist[:, d, :], ACT.Exp, scale=lg[:, d:d + 1])
                last.then_inc(decays, 1)
                act.wait_ge(ctx_done, i + 2)
                for d in range(2):
                    last = s.activation(state[d][:], upd[d][:], ACT.Copy)
                last.then_inc(state_set, 1)
                for n in range(4):
                    act.wait_ge(in_done, 4 * i + n + 1)
                    s.activation(y[:, 2 * n:2 * n + 2, :].rearrange("p c d -> p (c d)"), work[n % 2][:], ACT.Copy).then_inc(in_read, 1)
                act.wait_ge(g_loaded, 16 * i + 16)
                s.activation(gate[:], gate[:], ACT.Silu).then_inc(silu_ready, 1)
                act.wait_ge(y_summed, i + 1)
                for c in range(NC_):
                    if c:
                        act.wait_ge(squared, NC_ * i + c)
                    s.activation(square[:], y[:, c, :], ACT.Square, accum_out=sums[:, c:c + 1]).then_inc(squared, 1)
                act.wait_ge(root_asked, i + 1)
                s.activation(scratch[1][:], scratch[2][:], ACT.Sqrt).then_inc(root_ready, 1)
                for n in range(4):
                    act.wait_ge(yt_read, 4 * i + 4 + n + 1)
                    s.activation(yg_hi[:, bass.ds(2 * i + n // 2, 1), (n % 2) * HALF:(n % 2 + 1) * HALF].rearrange("p o t -> p (o t)"),
                                 value[:, n % 2, :], ACT.Copy).then_inc(high, 1)

        @block.vector
        def _(dve):
            vv = nc.vector
            chain = Chain(dve, dve_chain)
            dve.wait_ge(made, 1)
            chain.step(vv.tensor_copy(powers[:], power_i[:]))
            chain.step(vv.tensor_copy(delta[:], delta_i[:]))
            chain.step(vv.tensor_scalar(dist[:, 0, :], delta[:], 0.0, None, ALU.max))
            chain.step(vv.tensor_scalar(dist[:, 1, :], delta[:], -1.0, 0.0, ALU.mult, ALU.max))
            chain.step(vv.tensor_scalar(side[:, 0, :], delta[:], 0.0, DK ** -0.5, ALU.is_ge, ALU.mult))
            chain.step(vv.tensor_scalar(side[:, 1, :], delta[:], 0.0, DK ** -0.5, ALU.is_le, ALU.mult))
            dve.wait_ge(tables_loaded, 16)
            dve.wait_ge(decay_loaded, 16)
            setup = chain.taken
            PER_HEAD = 47
            with dve.Fori(0, HEADS, 1) as i:
                start = Chain(dve, dve_chain, setup, PER_HEAD, i)
                start.step(vv.tensor_copy(raw_dec[:], raw_all[:, :, bass.ds(i, 1)].rearrange("p d o -> p (d o)")))
                x, e, u, ln_u, um1, t5 = raw_dec[:], small[1][:], small[2][:], small[3][:], small[4][:], small[5][:]
                start.step(vv.tensor_scalar(small[4][:], x, -1.0, None, ALU.mult))
                start.step(vv.tensor_tensor(small[4][:], x, small[4][:], ALU.max))
                vv.tensor_scalar(small[0][:], small[4][:], -1.0, None, ALU.mult).then_inc(lg_asked, 1)
                dve.wait_ge(lg_exp, 2 * i + 1)
                start.step(vv.tensor_scalar(um1, e, 1.0, None, ALU.add))
                vv.tensor_copy(u, um1).then_inc(lg_asked, 1)
                dve.wait_ge(lg_exp, 2 * i + 2)
                start.step(vv.tensor_scalar(um1, um1, 1.0, None, ALU.subtract))
                start.step(vv.tensor_scalar(t5, um1, 0.0, None, ALU.is_equal))
                start.step(vv.tensor_tensor(um1, um1, t5, ALU.add))
                start.step(vv.tensor_tensor(ln_u, ln_u, t5, ALU.add))
                start.step(vv.reciprocal(um1, um1))
                start.step(vv.tensor_tensor(ln_u, ln_u, e, ALU.mult))
                start.step(vv.tensor_tensor(ln_u, ln_u, um1, ALU.mult))
                start.step(vv.tensor_scalar(t5, x, 0.0, None, ALU.max))
                start.step(vv.tensor_tensor(t5, ln_u, t5, ALU.add))
                vv.tensor_scalar(lg[:], t5, -1.0, None, ALU.mult).then_inc(lg_ready, 1)
                dve.wait_ge(decays, i + 1)
                start.step(vv.tensor_tensor(mask2[:], mask2[:], side[:], ALU.mult))
                start.step(vv.tensor_tensor(mask[:], mask2[:, 0, :], mask2[:, 1, :], ALU.add))
                for col in (1, 3, 4):
                    start.step(vv.tensor_scalar(dec[:, :, col:col + 1], dec[:, :, col:col + 1], DK ** -0.5, None, ALU.mult))
                dve.wait_ge(kc_loaded, 16 * i + 16)
                for d in range(2):
                    for c in range(CT):
                        last = vv.tensor_scalar(kcd[d][:, c, :], kc[:, c, :], dec[:, d, 3 + c:4 + c], None, ALU.mult)
                last.then_inc(kc_scaled, 1)
                dve.wait_ge(q_loaded, 16 * i + 16)
                rotate(vv, start, q, q_raw, cs, tmp_q, q_rotated)
                for n in range(4):
                    dve.wait_ge(kt_done, 4 * i + n + 1)
                    for d in range(2):
                        last = vv.tensor_scalar(kd[d][:, 2 * n:2 * n + 2, :].rearrange("p c d -> p (c d)"), work[n % 2][:],
                                                dec[:, d, 1:2], None, ALU.mult)
                    last.then_inc(kt_read, 1)
                for n in range(2):
                    dve.wait_ge(sc_done, 2 * i + 2 + n + 1)
                    vv.tensor_tensor(weights[:, 4 * n:4 * n + 4, :], work[n % 2][:].rearrange("p (c n) -> p c n", c=4),
                                     mask[:, None, :].to_broadcast([P, 4, CHUNK]), ALU.mult).then_inc(sc_read, 1)
                dve.wait_ge(state_set, i + 1)
                dve.wait_ge(in_read, 4 * i + 4)
                for st in range(NC_):
                    for d in range(2):
                        c = st if d == 0 else NC_ - 1 - st
                        dve.wait_ge(stepped, 16 * i + 16 + 2 * st + d + 1)
                        vv.scalar_tensor_tensor(out=state[d][:], in0=state[d][:], scalar=dec[:, d, 2:3], in1=upd[d][:],
                                                op0=ALU.mult, op1=ALU.add).then_inc(advanced, 1)
                        add = vv.scalar_tensor_tensor(out=y[:, c, :], in0=cross[d][st % 2][:], scalar=dec[:, d, 0:1],
                                                      in1=y[:, c, :], op0=ALU.mult, op1=ALU.add)
                        if (st, d) == (NC_ - 1, 1):
                            add.then_inc(y_summed, 1)
                        else:
                            start.step(add)
                dve.wait_ge(squared, NC_ * i + NC_)

                def act_sqrt(root, mean):
                    vv.tensor_copy(scratch[2][:], mean).then_inc(root_asked, 1)
                    dve.wait_ge(root_ready, i + 1)

                rsqrt_of_mean(nc, start, act_sqrt, rstd[:], sums[:], tuple(x[:] for x in scratch), DK)
                start.step(vv.tensor_tensor(y[:], y[:], rstd[:, :, None].to_broadcast([P, NC_, DK]), ALU.mult))
                dve.wait_ge(silu_ready, i + 1)
                vv.tensor_tensor(y[:], y[:], gate[:], ALU.mult).then_inc(gated, 1)
                for n in range(4):
                    dve.wait_ge(yt_done, 4 * i + n + 1)
                    vv.tensor_copy(value[:, n % 2, :], work[n % 2][:]).then_inc(yt_read, 1)
                    dve.wait_ge(high, 4 * i + n + 1)
                    cols = (bass.ds(2 * i + n // 2, 1), slice((n % 2) * HALF, (n % 2 + 1) * HALF))
                    start.step(vv.tensor_tensor(yg_lo[:, cols[0], cols[1]].rearrange("p o t -> p (o t)"), value[:, n % 2, :],
                                                f32(yg_hi[:, cols[0], cols[1]].rearrange("p o t -> p (o t)")), ALU.subtract))
                assert start.taken == PER_HEAD, start.taken

        @block.tensor
        def _(pe):
            mm_ = nc.tensor.matmul
            pe.sem_inc(ctx_done, 1)
            pe.sem_inc(sc_done, 2)
            pe.sem_inc(stepped, 16)
            pe.sem_inc(gated, 1)
            pe.sem_inc(yt_read, 4)
            with pe.Fori(0, HEADS, 1) as i:
                pe.wait_ge(kc_scaled, i + 1)
                pe.wait_ge(vc_loaded, 16 * i + 16)
                for d in range(2):
                    for j in range(2):
                        for c in range(CT):
                            mm = mm_(upd[d][:, j, :], kcd[d][:, c, j * P:(j + 1) * P], vc[:, c, :],
                                     start=(c == 0), stop=(c == CT - 1))
                mm.then_inc(ctx_done, 1)
                pe.wait_ge(k_rotated, i + 2)
                for n in range(4):
                    if n >= 2:
                        pe.wait_ge(kt_read, 4 * i + n - 1)
                    else:
                        pe.wait_ge(yt_read, 4 * i + 4)
                    for c in range(2):
                        for j in range(2):
                            tr = nc.tensor.transpose(work[n % 2][:, c * DK + j * P:c * DK + (j + 1) * P],
                                                     k[:, j, (2 * n + c) * CHUNK:(2 * n + c + 1) * CHUNK], ident)
                    tr.then_inc(kt_done, 1)
                pe.wait_ge(q_rotated, i + 2)
                for n in range(2):
                    pe.wait_ge(kt_read, 4 * i + n + 3)
                    for c in range(4):
                        cols = slice((4 * n + c) * CHUNK, (4 * n + c + 1) * CHUNK)
                        for j in range(2):
                            mm = mm_(work[n % 2][:, c * CHUNK:(c + 1) * CHUNK], k[:, j, cols], q[:, j, cols],
                                     start=(j == 0), stop=(j == 1))
                    mm.then_inc(sc_done, 1)
                pe.wait_ge(v_loaded, 16 * i + 16)
                for n in range(4):
                    if n < 2:
                        pe.wait_ge(sc_read, 2 * i + n + 1)
                    else:
                        pe.wait_ge(in_read, 4 * i + n - 1)
                    if n == 0:
                        pe.wait_ge(sc_read, 2 * i + 2)
                    for c in range(2):
                        mm = mm_(work[n % 2][:, c * DK:(c + 1) * DK], weights[:, 2 * n + c, :], v[:, 2 * n + c, :],
                                 start=True, stop=True)
                    mm.then_inc(in_done, 1)
                pe.wait_ge(state_set, i + 1)
                for st in range(NC_):
                    for d in range(2):
                        c = st if d == 0 else NC_ - 1 - st
                        if st:
                            pe.wait_ge(advanced, 16 * i + 2 * (st - 1) + d + 1)
                        for j in range(2):
                            mm_(cross[d][st % 2][:], q[:, j, c * CHUNK:(c + 1) * CHUNK], state[d][:, j, :],
                                start=(j == 0), stop=(j == 1))
                        for j in range(2):
                            mm = mm_(upd[d][:, j, :], kd[d][:, c, j * P:(j + 1) * P], v[:, c, :], start=True, stop=True)
                        mm.then_inc(stepped, 1)
                pe.wait_ge(gated, i + 2)
                for n in range(4):
                    if n >= 2:
                        pe.wait_ge(yt_read, 4 * i + 4 + n - 1)
                    for c in range(4):
                        tr = nc.tensor.transpose(work[n % 2][:, c * P:(c + 1) * P],
                                                 y[:, 4 * (n % 2) + c, (n // 2) * P:(n // 2 + 1) * P], ident)
                    tr.then_inc(yt_done, 1)


def project(nc, name, w_blocks, n_blocks, a_hi, a_lo, token_major, gate_rows, result, add):
    with ExitStack() as ctx:
        p = Pool(nc, ctx)
        RING = 4
        GROUPS = 8 * n_blocks
        raw = p.sb(name + "_raw", [P, KT * NB])
        w_hi = [p.sb(f"{name}_w_hi{b}", [P, KT * NB], F32R) for b in range(2)]
        w_lo = [p.sb(f"{name}_w_lo{b}", [P, KT * NB], F32R) for b in range(2)]
        gate = p.sb(name + "_gate", [P, RING, HALF]) if gate_rows is not None else None
        bank = [p.ps(f"{name}_bank{b}", [P, HALF]) for b in range(RING)]
        raw_loaded = p.sem(name + "_raw_loaded")
        hi_ready = p.sem(name + "_hi_ready")
        lo_ready = p.sem(name + "_lo_ready")
        gate_loaded = [p.sem(f"{name}_gate_loaded{r}") for r in range(RING)]
        gate_ready = p.sem(name + "_gate_ready")
        group_done = p.sem(name + "_group_done")
        multiplied = p.sem(name + "_multiplied")
        evacuated = p.sem(name + "_evacuated")
        block = ctx.enter_context(nc.Block())

        def place(g):
            blk, r = g // 8, g % 8
            if token_major:
                return result[:, r, blk * NB:(blk + 1) * NB]
            tile = blk * 4 + r // 2
            return result[:, tile, (r % 2) * HALF:(r % 2 + 1) * HALF]

        @block.sync
        def _(sp):
            sp.dma_start(raw[:], w_blocks[0]).then_inc(raw_loaded, 16)
            for g in range(GROUPS):
                if g % 8 == 4 and g // 8 + 1 < n_blocks:
                    sp.wait_ge(lo_ready, g // 8 + 1)
                    sp.dma_start(raw[:], w_blocks[g // 8 + 1]).then_inc(raw_loaded, 16)
                if gate_rows is not None:
                    if g >= RING:
                        sp.wait_ge(evacuated, g - RING + 1)
                    tile, half = (g // 8) * 4 + g % 8 // 2, g % 2
                    sp.dma_start(gate[:, g % RING, :],
                                 gate_rows[tile * P:(tile + 1) * P, half * HALF:(half + 1) * HALF]).then_inc(gate_loaded[g % RING], 16)

        @block.scalar
        def _(act):
            def high_part(blk):
                act.wait_ge(raw_loaded, 16 * (blk + 1))
                nc.scalar.activation(w_hi[blk % 2][:], raw[:], ACT.Copy).then_inc(hi_ready, 1)

            high_part(0)
            for g in range(GROUPS):
                if g % 8 == 6 and g // 8 + 1 < n_blocks:
                    high_part(g // 8 + 1)
                if gate_rows is not None:
                    act.wait_ge(gate_loaded[g % RING], 16 * (g // RING + 1))
                    nc.scalar.activation(gate[:, g % RING, :], gate[:, g % RING, :], ACT.Sigmoid).then_inc(gate_ready, 1)
                else:
                    act.wait_ge(group_done, g + 1)
                    nc.scalar.activation(place(g), bank[g % RING][:], ACT.Copy).then_inc(evacuated, 1)

        @block.gpsimd
        def _(pool):
            for blk in range(n_blocks):
                pool.wait_ge(hi_ready, blk + 1)
                nc.gpsimd.tensor_tensor(w_lo[blk % 2][:], raw[:], f32(w_hi[blk % 2][:]), ALU.subtract).then_inc(lo_ready, 1)

        @block.vector
        def _(dve):
            if gate_rows is None:
                return
            for g in range(GROUPS):
                dve.wait_ge(group_done, g + 1)
                dve.wait_ge(gate_ready, g + 1)
                if add:
                    nc.vector.tensor_tensor(gate[:, g % RING, :], bank[g % RING][:], gate[:, g % RING, :], ALU.mult).then_inc(multiplied, 1)
                    dve.wait_ge(multiplied, g + 1)
                    nc.vector.tensor_tensor(place(g), place(g), gate[:, g % RING, :], ALU.add).then_inc(evacuated, 1)
                else:
                    nc.vector.tensor_tensor(place(g), bank[g % RING][:], gate[:, g % RING, :], ALU.mult).then_inc(evacuated, 1)

        @block.tensor
        def _(pe):
            for g in range(GROUPS):
                blk, r = g // 8, g % 8
                if r == 0:
                    pe.wait_ge(lo_ready, blk + 1)
                wh = w_hi[blk % 2][:].rearrange("p (k n) -> p k n", k=KT)
                wl = w_lo[blk % 2][:].rearrange("p (k n) -> p k n", k=KT)
                if g >= RING:
                    pe.wait_ge(evacuated, g - RING + 1)
                if token_major:
                    c = slice(r * P, (r + 1) * P)
                    pairs = [((a_hi[:, k, c], a_lo[:, k, c]), (wh[:, k, :], wl[:, k, :])) for k in range(KT)]
                else:
                    n = slice((r // 2) * P, (r // 2 + 1) * P)
                    c = slice((r % 2) * HALF, (r % 2 + 1) * HALF)
                    pairs = [((wh[:, k, n], wl[:, k, n]), (a_hi[:, k, c], a_lo[:, k, c])) for k in range(KT)]
                split_matmuls(nc, bank[g % RING][:], pairs).then_inc(group_done, 1)


def split_tile(nc, name, x, hi, lo):
    with ExitStack() as ctx:
        p = Pool(nc, ctx)
        high = p.sem(name + "_high")
        low = p.sem(name + "_low")
        block = ctx.enter_context(nc.Block())

        @block.scalar
        def _(act):
            for k in range(KT):
                nc.scalar.activation(hi[:, k, :], x[:, k, :], ACT.Copy).then_inc(high, 1)

        @block.vector
        def _(dve):
            for k in range(KT):
                dve.wait_ge(high, k + 1)
                nc.vector.tensor_tensor(lo[:, k, :], x[:, k, :], f32(hi[:, k, :]), ALU.subtract)


def conv_norm(nc, conv, gain_cols, bias_cols, u_hi, u_lo, ones):
    with ExitStack() as ctx:
        p = Pool(nc, ctx)
        x = p.sb("cn_x", [P, KT, SEQ])
        square = p.sb("cn_square", [P, 2, SEQ])
        var = p.sb("cn_var", [P, SEQ])
        root = p.sb("cn_root", [P, SEQ])
        rstd = p.sb("cn_rstd", [P, SEQ])
        gain = p.sb("cn_gain", [P, KT])
        bias = p.sb("cn_bias", [P, KT])
        mean_bank = [p.ps(f"cn_mean{h}", [P, HALF]) for h in range(2)]
        var_bank = [p.ps(f"cn_var_bank{h}", [P, HALF]) for h in range(2)]
        loaded = [p.sem(f"cn_loaded{k}") for k in range(KT)]
        cols_loaded = p.sem("cn_cols_loaded")
        mean_done = p.sem("cn_mean_done")
        centred = p.sem("cn_centred")
        squared = p.sem("cn_squared")
        var_done = p.sem("cn_var_done")
        square_read = p.sem("cn_square_read")
        root_asked = p.sem("cn_root_asked")
        root_ready = p.sem("cn_root_ready")
        chained = p.sem("cn_chained")
        scaled = p.sem("cn_scaled")
        silued = p.sem("cn_silued")
        high = p.sem("cn_high")
        block = ctx.enter_context(nc.Block())

        @block.sync
        def _(sp):
            for k in range(KT):
                sp.dma_start(x[:, k, :], conv[k * P:(k + 1) * P, :]).then_inc(loaded[k], 16)
            sp.dma_start(gain[:], gain_cols).then_inc(cols_loaded, 16)
            sp.dma_start(bias[:], bias_cols).then_inc(cols_loaded, 16)

        @block.tensor
        def _(pe):
            for k in range(KT):
                pe.wait_ge(loaded[k], 16)
                for h in range(2):
                    mm = nc.tensor.matmul(mean_bank[h][:], ones, x[:, k, h * HALF:(h + 1) * HALF],
                                          start=(k == 0), stop=(k == KT - 1))
            mm.then_inc(mean_done, 1)
            for k in range(KT):
                pe.wait_ge(squared, k + 1)
                for h in range(2):
                    mm = nc.tensor.matmul(var_bank[h][:], ones, square[:, k % 2, h * HALF:(h + 1) * HALF],
                                          start=(k == 0), stop=(k == KT - 1))
                mm.then_inc(square_read, 1)

        @block.vector
        def _(dve):
            v = nc.vector
            dve.wait_ge(mean_done, 1)
            for k in range(KT):
                for h in range(2):
                    cols = slice(h * HALF, (h + 1) * HALF)
                    v.scalar_tensor_tensor(out=x[:, k, cols], in0=mean_bank[h][:], scalar=-1.0 / D, in1=x[:, k, cols],
                                           op0=ALU.mult, op1=ALU.add).then_inc(centred, 1)
            dve.wait_ge(square_read, KT)
            chain = Chain(dve, chained)
            for h in range(2):
                chain.step(v.tensor_scalar(var[:, h * HALF:(h + 1) * HALF], var_bank[h][:], 1.0 / D, EPS, ALU.mult, ALU.add))
            v.tensor_copy(rstd[:, 0:1], var[:, 0:1]).then_inc(root_asked, 1)
            dve.wait_ge(root_ready, 1)
            chain.step(v.reciprocal(rstd[:], root[:]))
            chain.step(v.tensor_tensor(root[:], rstd[:], rstd[:], ALU.mult))
            chain.step(v.tensor_tensor(root[:], root[:], var[:], ALU.mult))
            chain.step(v.tensor_scalar(root[:], root[:], -0.5, 1.5, ALU.mult, ALU.add))
            chain.step(v.tensor_tensor(rstd[:], rstd[:], root[:], ALU.mult))
            for k in range(KT):
                v.tensor_tensor(x[:, k, :], x[:, k, :], rstd[:], ALU.mult).then_inc(scaled, 1)

        @block.gpsimd
        def _(pool):
            for k in range(KT):
                pool.wait_ge(high, k + 1)
                nc.gpsimd.tensor_tensor(u_lo[:, k, :], x[:, k, :], f32(u_hi[:, k, :]), ALU.subtract)

        @block.scalar
        def _(act):
            s = nc.scalar
            for k in range(KT):
                act.wait_ge(centred, 2 * (k + 1))
                if k >= 2:
                    act.wait_ge(square_read, k - 1)
                s.activation(square[:, k % 2, :], x[:, k, :], ACT.Square).then_inc(squared, 1)
            act.wait_ge(root_asked, 1)
            s.activation(root[:], var[:], ACT.Sqrt).then_inc(root_ready, 1)
            act.wait_ge(cols_loaded, 32)
            for k in range(KT):
                act.wait_ge(scaled, k + 1)
                s.activation(x[:, k, :], x[:, k, :], ACT.Silu, bias=bias[:, k:k + 1], scale=gain[:, k:k + 1]).then_inc(silued, 1)
                act.wait_ge(silued, k + 1)
                s.activation(u_hi[:, k, :], x[:, k, :], ACT.Copy).then_inc(high, 1)


def residual(nc, name, y, base_dram, row, out_dram):
    with ExitStack() as ctx:
        p = Pool(nc, ctx)
        base = p.sb(name + "_base", [P, TT, D])
        square = p.sb(name + "_square", [P, D])
        sums = p.sb(name + "_sums", [P, TT])
        rstd = p.sb(name + "_rstd", [P, TT])
        scratch = [p.sb(f"{name}_scratch{n}", [P, TT]) for n in range(3)]
        loaded = p.sem(name + "_loaded")
        summed = p.sem(name + "_summed")
        root_asked = p.sem(name + "_root_asked")
        root_ready = p.sem(name + "_root_ready")
        chained = p.sem(name + "_chained")
        weighted = p.sem(name + "_weighted")
        added = p.sem(name + "_added")
        stored = p.sem(name + "_stored")
        block = ctx.enter_context(nc.Block())
        view = lambda dram: dram.rearrange("(t p) d -> p t d", p=P)

        @block.sync
        def _(sp):
            sp.dma_start(base[:], view(base_dram)).then_inc(loaded, 16)
            for t in range(TT):
                sp.wait_ge(added, t + 1)
                sp.dma_start(view(out_dram)[:, t, :], y[:, t, :]).then_inc(stored, 16)
            sp.wait_ge(stored, 16 * TT)

        @block.scalar
        def _(act):
            for t in range(TT):
                if t:
                    act.wait_ge(summed, t)
                nc.scalar.activation(square[:], y[:, t, :], ACT.Square, accum_out=sums[:, t:t + 1]).then_inc(summed, 1)
            act.wait_ge(root_asked, 1)
            nc.scalar.activation(scratch[1][:], scratch[2][:], ACT.Sqrt).then_inc(root_ready, 1)

        @block.vector
        def _(dve):
            v = nc.vector
            dve.wait_ge(summed, TT)
            chain = Chain(dve, chained)

            def act_sqrt(root, mean):
                v.tensor_copy(scratch[2][:], mean).then_inc(root_asked, 1)
                dve.wait_ge(root_ready, 1)

            rsqrt_of_mean(nc, chain, act_sqrt, rstd[:], sums[:], tuple(x[:] for x in scratch), D)
            dve.wait_ge(loaded, 16)
            for t in range(TT):
                v.scalar_tensor_tensor(out=y[:, t, :], in0=y[:, t, :], scalar=rstd[:, t:t + 1], in1=row,
                                       op0=ALU.mult, op1=ALU.mult).then_inc(weighted, 1)
                dve.wait_ge(weighted, t + 1)
                v.tensor_tensor(y[:, t, :], y[:, t, :], base[:, t, :], ALU.add).then_inc(added, 1)

PEER_HEADS = 8
N_KEYS = 128
TOPK = 16
SIDES = 2 * PEER_HEADS
CAND = TOPK * TOPK
NEG = -3.0e38


def query_scores(nc, wq_blocks, keys, h_hi, h_lo, scores):
    with ExitStack() as ctx:
        p = Pool(nc, ctx)
        RING = 4
        BLKS = 4
        raw = p.sb("qs_raw", [P, KT * NB])
        w_hi = [p.sb(f"qs_w_hi{b}", [P, KT * NB], F32R) for b in range(2)]
        w_lo = [p.sb(f"qs_w_lo{b}", [P, KT * NB], F32R) for b in range(2)]
        key = p.sb("qs_key", [P, SIDES, N_KEYS])
        q = p.sb("qs_q", [P, RING, HALF])
        stage = p.sb("qs_stage", [P, RING, 4, N_KEYS])
        q_bank = [p.ps(f"qs_q_bank{b}", [P, HALF]) for b in range(RING)]
        s_bank = [p.ps(f"qs_s_bank{b}", [P, 4, N_KEYS]) for b in range(RING)]
        keys_loaded = p.sem("qs_keys_loaded")
        raw_loaded = p.sem("qs_raw_loaded")
        hi_ready = p.sem("qs_hi_ready")
        lo_ready = p.sem("qs_lo_ready")
        q_done, q_read = p.sem("qs_q_done"), p.sem("qs_q_read")
        s_done, s_read = p.sem("qs_s_done"), p.sem("qs_s_read")
        stored = [p.sem(f"qs_stored{r}") for r in range(RING)]
        block = ctx.enter_context(nc.Block())

        @block.sync
        def _(sp):
            sp.dma_start(raw[:], wq_blocks[0]).then_inc(raw_loaded, 16)
            sp.dma_start(key[:], keys).then_inc(keys_loaded, 16)
            for g in range(8 * BLKS):
                if g % 8 == 0 and g // 8 + 1 < BLKS:
                    sp.wait_ge(lo_ready, g // 8 + 1)
                    sp.dma_start(raw[:], wq_blocks[g // 8 + 1]).then_inc(raw_loaded, 16)
                side, half = g // 2, g % 2
                sp.wait_ge(s_read, g + 1)
                dst = scores.rearrange("(t p) (s n) -> s p t n", p=P, n=N_KEYS)[side, :, half * 4:half * 4 + 4, :]
                sp.dma_start(dst, stage[:, g % RING, :, :]).then_inc(stored[g % RING], 16)
            for r in range(RING):
                sp.wait_ge(stored[r], 16 * (8 * BLKS // RING))

        @block.scalar
        def _(act):
            def high_part(blk):
                act.wait_ge(raw_loaded, 16 * (blk + 1))
                nc.scalar.activation(w_hi[blk % 2][:], raw[:], ACT.Copy).then_inc(hi_ready, 1)

            high_part(0)
            for g in range(8 * BLKS):
                if g % 8 == 2 and g // 8 + 1 < BLKS:
                    high_part(g // 8 + 1)
                act.wait_ge(q_done, g + 1)
                if g >= RING:
                    act.wait_ge(s_done, g - RING + 1)
                nc.scalar.activation(q[:, g % RING, :], q_bank[g % RING][:], ACT.Copy).then_inc(q_read, 1)

        @block.gpsimd
        def _(pool):
            for blk in range(BLKS):
                pool.wait_ge(hi_ready, blk + 1)
                nc.gpsimd.tensor_tensor(w_lo[blk % 2][:], raw[:], f32(w_hi[blk % 2][:]), ALU.subtract).then_inc(lo_ready, 1)

        @block.vector
        def _(dve):
            for g in range(8 * BLKS):
                dve.wait_ge(s_done, g + 1)
                if g >= RING:
                    dve.wait_ge(stored[g % RING], 16 * (g // RING))
                nc.vector.tensor_copy(stage[:, g % RING, :, :], s_bank[g % RING][:]).then_inc(s_read, 1)

        @block.tensor
        def _(pe):
            def score(g):
                side = g // 2
                pe.wait_ge(q_read, g + 1)
                if g >= RING:
                    pe.wait_ge(s_read, g - RING + 1)
                for t in range(4):
                    mm = nc.tensor.matmul(s_bank[g % RING][:, t, :], q[:, g % RING, t * P:(t + 1) * P], key[:, side, :],
                                          start=True, stop=True)
                mm.then_inc(s_done, 1)

            pe.wait_ge(keys_loaded, 16)
            for g in range(8 * BLKS):
                blk, r = g // 8, g % 8
                if r == 0:
                    pe.wait_ge(lo_ready, blk + 1)
                wh = w_hi[blk % 2][:].rearrange("p (k n) -> p k n", k=KT)
                wl = w_lo[blk % 2][:].rearrange("p (k n) -> p k n", k=KT)
                if g >= RING:
                    pe.wait_ge(q_read, g - RING + 1)
                n = slice((r // 2) * P, (r // 2 + 1) * P)
                c = slice((r % 2) * HALF, (r % 2 + 1) * HALF)
                split_matmuls(nc, q_bank[g % RING][:], [((wh[:, k, n], wl[:, k, n]), (h_hi[:, k, c], h_lo[:, k, c]))
                                                        for k in range(KT)]).then_inc(q_done, 1)
                if g:
                    score(g - 1)
            score(8 * BLKS - 1)


def top_experts(nc, scores, first_T, second_T, gate_T, ident):
    with ExitStack() as ctx:
        p = Pool(nc, ctx)
        s = p.sb("te_s", [P, SIDES, N_KEYS])
        s2 = p.sb("te_s2", [P, SIDES, N_KEYS])
        top = p.sb("te_top", [P, SIDES, TOPK])
        top_i = p.sb("te_top_i", [P, SIDES, TOPK], U32)
        top_f = p.sb("te_top_f", [P, SIDES, TOPK])
        cand = p.sb("te_cand", [P, PEER_HEADS, CAND])
        cand2 = p.sb("te_cand2", [P, PEER_HEADS, CAND])
        best = p.sb("te_best", [P, PEER_HEADS, TOPK])
        sel = p.sb("te_sel", [P, PEER_HEADS * TOPK], U32)
        part_i = p.sb("te_part_i", [P, 2, PEER_HEADS * TOPK], U32)
        part = p.sb("te_part", [P, 2, PEER_HEADS * TOPK])
        hit = [p.sb(f"te_hit{d}", [P, PEER_HEADS * TOPK, TOPK]) for d in range(2)]
        found = p.sb("te_found", [P, 3, PEER_HEADS * TOPK])
        shifted = p.sb("te_shifted", [P, PEER_HEADS, TOPK])
        sums = p.sb("te_sums", [P, PEER_HEADS])
        ranks_i = p.sb("te_ranks_i", [P, TOPK], I32)
        ranks = p.sb("te_ranks", [P, TOPK])
        pad = p.sb("te_pad", [P, 1])
        bank = p.ps("te_bank", [P, 3, P])
        loaded = p.sem("te_loaded")
        made = p.sem("te_made")
        chain_sem = p.sem("te_chain")
        keys_taken = p.sem("te_keys_taken")
        exp_asked = p.sem("te_exp_asked")
        exp_ready = p.sem("te_exp_ready")
        parted = p.sem("te_parted")
        compared = p.sem("te_compared")
        second_hit = p.sem("te_second_hit")
        found_ready = p.sem("te_found_ready")
        turned = p.sem("te_turned")
        kept = p.sem("te_kept")
        block = ctx.enter_context(nc.Block())

        @block.sync
        def _(sp):
            sp.sem_inc(keys_taken, 1)
            with sp.Fori(0, TT, 1) as i:
                row = sp.snap(i * P)
                sp.wait_ge(keys_taken, i + 1)
                sp.dma_start(s[:].rearrange("p s n -> p (s n)"), scores[bass.ds(row, P), :]).then_inc(loaded, 16)

        def compare(side):
            pt = part[:, side, :]
            return nc.vector.tensor_tensor(hit[side][:], pt[:, :, None].to_broadcast([P, PEER_HEADS * TOPK, TOPK]),
                                           ranks[:, None, :].to_broadcast([P, PEER_HEADS * TOPK, TOPK]), ALU.is_equal)

        def weigh(engine, side):
            idx = top_f[:].rearrange("p (h e) k -> p h e k", e=2)[:, :, side, :]
            view = hit[side][:].rearrange("p (h k) a -> p h k a", h=PEER_HEADS)
            return engine.tensor_tensor(view, view, idx[:, :, None, :].to_broadcast([P, PEER_HEADS, TOPK, TOPK]), ALU.mult)

        @block.gpsimd
        def _(pool):
            nc.gpsimd.iota(ranks_i[:], pattern=[[1, TOPK]], base=0, channel_multiplier=0).then_inc(made, 1)
            pool.wait_ge(made, 1)
            nc.gpsimd.tensor_copy(ranks[:], ranks_i[:]).then_inc(made, 1)
            pool.wait_ge(made, 2)
            with pool.Fori(0, TT, 1) as i:
                pool.wait_ge(compared, i + 1)
                weigh(nc.gpsimd, 1).then_inc(second_hit, 1)

        @block.scalar
        def _(act):
            act.sem_inc(kept, 1)
            with act.Fori(0, TT, 1) as i:
                act.wait_ge(exp_asked, i + 1)
                nc.scalar.activation(shifted[:], shifted[:], ACT.Exp).then_inc(exp_ready, 1)
                act.wait_ge(turned, i + 1)
                for n, dst in enumerate((first_T, second_T, gate_T)):
                    last = nc.scalar.activation(dst[:, bass.ds(i * P, P)], bank[:, n, :], ACT.Copy)
                last.then_inc(kept, 1)

        @block.tensor
        def _(pe):
            with pe.Fori(0, TT, 1) as i:
                pe.wait_ge(found_ready, i + 1)
                pe.wait_ge(kept, i + 1)
                for n in range(3):
                    tr = nc.tensor.transpose(bank[:, n, :], found[:, n, :], ident)
                tr.then_inc(turned, 1)

        @block.vector
        def _(dve):
            v = nc.vector
            STEPS = 13
            dve.wait_ge(made, 2)

            def take_wait():
                v.memset(pad[:], 0.0)

            with dve.Fori(0, TT, 1) as i:
                chain = Chain(dve, chain_sem, 0, STEPS, i)
                dve.wait_ge(loaded, 16 * i + 16)
                take_wait()
                for c in range(SIDES):
                    last = v.max(top[:, c, 0:8], s[:, c, :])
                chain.step(last)
                take_wait()
                for c in range(SIDES):
                    last = v.match_replace(s2[:, c, :], top[:, c, 0:8], s[:, c, :], NEG)
                chain.step(last)
                take_wait()
                for c in range(SIDES):
                    last = v.max(top[:, c, 8:16], s2[:, c, :])
                chain.step(last)
                take_wait()
                for c in range(SIDES):
                    v.max_index(top_i[:, c, 8:16], top[:, c, 8:16], s2[:, c, :])
                    last = v.max_index(top_i[:, c, 0:8], top[:, c, 0:8], s[:, c, :])
                last.then_inc(keys_taken, 1)
                dve.wait_ge(keys_taken, i + 2)
                v.tensor_copy(top_f[:], top_i[:])
                pairs = top[:].rearrange("p (h e) k -> p h e k", e=2)
                chain.step(v.tensor_tensor(cand[:].rearrange("p h (a b) -> p h a b", a=TOPK),
                                           pairs[:, :, 0, :, None].to_broadcast([P, PEER_HEADS, TOPK, TOPK]),
                                           pairs[:, :, 1, None, :].to_broadcast([P, PEER_HEADS, TOPK, TOPK]), ALU.add))
                take_wait()
                for h in range(PEER_HEADS):
                    last = v.max(best[:, h, 0:8], cand[:, h, :])
                chain.step(last)
                take_wait()
                for h in range(PEER_HEADS):
                    last = v.match_replace(cand2[:, h, :], best[:, h, 0:8], cand[:, h, :], NEG)
                chain.step(last)
                take_wait()
                for h in range(PEER_HEADS):
                    last = v.max(best[:, h, 8:16], cand2[:, h, :])
                chain.step(last)
                v.tensor_tensor(shifted[:], best[:], best[:, :, 0:1].to_broadcast([P, PEER_HEADS, TOPK]),
                                ALU.subtract).then_inc(exp_asked, 1)
                for h in range(PEER_HEADS):
                    v.max_index(sel[:, h * TOPK + 8:h * TOPK + 16], best[:, h, 8:16], cand2[:, h, :])
                    last = v.max_index(sel[:, h * TOPK:h * TOPK + 8], best[:, h, 0:8], cand[:, h, :])
                chain.step(last)
                v.tensor_scalar(part_i[:, 0, :], sel[:], 4, None, ALU.logical_shift_right)
                chain.step(v.tensor_scalar(part_i[:, 1, :], sel[:], TOPK - 1, None, ALU.bitwise_and))
                v.tensor_copy(part[:], part_i[:]).then_inc(parted, 1)
                dve.wait_ge(parted, i + 1)
                compare(1).then_inc(compared, 1)
                chain.step(compare(0))
                chain.step(weigh(v, 0))
                dve.wait_ge(kept, i + 1)
                v.tensor_reduce(found[:, 0, :], hit[0][:], AX.X, ALU.add)
                dve.wait_ge(second_hit, i + 1)
                v.tensor_reduce(found[:, 1, :], hit[1][:], AX.X, ALU.add)
                dve.wait_ge(exp_ready, i + 1)
                chain.step(v.tensor_reduce(sums[:], shifted[:], AX.X, ALU.add))
                chain.step(v.reciprocal(sums[:], sums[:]))
                v.tensor_tensor(found[:, 2, :].rearrange("p (h k) -> p h k", h=PEER_HEADS), shifted[:],
                                sums[:, :, None].to_broadcast([P, PEER_HEADS, TOPK]), ALU.mult).then_inc(found_ready, 1)
                assert chain.taken == STEPS, chain.taken


def gate_matrix(nc, first_T, second_T, gate_T, g_dram):
    SPAN = 128
    TURN = 8
    QUAD = 4
    QUADS = TURN // QUAD
    with ExitStack() as ctx:
        p = Pool(nc, ctx)
        iota_i = p.sb("gm_iota_i", [P, P], I32)
        iota = p.sb("gm_iota", [P, P])
        weight_hi = p.sb("gm_weight_hi", [P, SEQ], F32R)
        weight_lo = p.sb("gm_weight_lo", [P, SEQ])
        hot_i = [p.sb(f"gm_hot_i{b}", [P, TURN, P], BF16) for b in range(2)]
        hot_j = [p.sb(f"gm_hot_j{b}", [P, TURN, P], F32R) for b in range(2)]
        hot_hi = [p.sb(f"gm_hot_hi{b}", [P, TURN, P], F32R) for b in range(2)]
        hot_lo = [p.sb(f"gm_hot_lo{b}", [P, TURN, P], F32R) for b in range(2)]
        slab = [p.sb(f"gm_slab{b}", [P, P, SPAN]) for b in range(2)]
        bank = [p.ps(f"gm_bank{b}", [P, QUAD, P]) for b in range(8)]
        made = p.sem("gm_made")
        weights_ready = p.sem("gm_weights_ready")
        i_ready = p.sem("gm_i_ready")
        hi_ready = p.sem("gm_hi_ready")
        lo_ready = p.sem("gm_lo_ready")
        quad_done = p.sem("gm_quad_done")
        quad_read = p.sem("gm_quad_read")
        stored = [p.sem(f"gm_stored{b}") for b in range(2)]
        PAIRS = SEQ // (2 * SPAN)
        PER_SLAB = SPAN // QUAD
        TURNS = SEQ // TURN
        block = ctx.enter_context(nc.Block())

        def rows_of(x, t0):
            return x[:, bass.ds(t0, TURN)][:, :, None].to_broadcast([P, TURN, P])

        iota_rows = iota[:, None, :].to_broadcast([P, TURN, P])

        @block.sync
        def _(sp):
            with sp.Fori(0, PAIRS, 1) as i:
                col = sp.snap(i * 2 * SPAN)
                for b in range(2):
                    sp.wait_ge(quad_read, (2 * i + b + 1) * PER_SLAB + 8)
                    for part in range(2):
                        rows = slice(part * (P // 2), (part + 1) * (P // 2))
                        sp.dma_start(g_dram[rows, :, bass.ds(col + b * SPAN, SPAN)].rearrange("i j t -> j i t"),
                                     slab[b][:, rows, :]).then_inc(stored[b], 16)
            for b in range(2):
                sp.wait_ge(stored[b], 32 * (PAIRS + 1))

        @block.gpsimd
        def _(pool):
            pool.sem_inc(lo_ready, 2)
            nc.gpsimd.iota(iota_i[:], pattern=[[1, P]], base=0, channel_multiplier=0).then_inc(made, 1)
            pool.wait_ge(made, 1)
            nc.gpsimd.tensor_copy(iota[:], iota_i[:]).then_inc(made, 1)
            pool.wait_ge(weights_ready, 2)
            with pool.Fori(0, TURNS // 2, 1) as i:
                for b in range(2):
                    pool.wait_ge(i_ready, 2 * i + b + 1)
                    pool.wait_ge(quad_done, QUADS * 2 * i + QUADS * (b + 1))
                    nc.gpsimd.tensor_tensor(hot_lo[b][:], hot_i[b][:], rows_of(weight_lo, i * 2 * TURN + b * TURN),
                                            ALU.mult).then_inc(lo_ready, 1)

        @block.vector
        def _(dve):
            v = nc.vector
            dve.wait_ge(made, 2)
            dve.wait_ge(weights_ready, 1)
            v.tensor_tensor(weight_lo[:], gate_T[:], f32(weight_hi[:]), ALU.subtract).then_inc(weights_ready, 1)
            dve.wait_ge(weights_ready, 2)
            with dve.Fori(0, TURNS // 2, 1) as i:
                for b in range(2):
                    t0 = i * 2 * TURN + b * TURN
                    dve.wait_ge(lo_ready, 2 * i + b + 1)
                    v.tensor_tensor(hot_i[b][:], rows_of(first_T, t0), iota_rows, ALU.is_equal).then_inc(i_ready, 1)
                    dve.wait_ge(quad_done, QUADS * 2 * i + QUADS * (b + 1))
                    v.tensor_tensor(hot_j[b][:], rows_of(second_T, t0), iota_rows, ALU.is_equal)
                    dve.wait_ge(i_ready, 2 * i + b + 1)
                    v.tensor_tensor(hot_hi[b][:], hot_i[b][:], rows_of(f32(weight_hi[:]), t0), ALU.mult).then_inc(hi_ready, 1)

        @block.scalar
        def _(act):
            for b in range(2):
                act.sem_inc(stored[b], 32)
            act.sem_inc(quad_read, 8)
            nc.scalar.activation(weight_hi[:], gate_T[:], ACT.Copy).then_inc(weights_ready, 1)
            with act.Fori(0, PAIRS, 1) as i:
                for b in range(2):
                    act.wait_ge(stored[b], 32 * i + 32)
                    for n in range(PER_SLAB):
                        q = b * PER_SLAB + n
                        act.wait_ge(quad_done, i * 2 * PER_SLAB + q + 1 + 2 * QUADS)
                        nc.scalar.activation(slab[b][:, :, n * QUAD:(n + 1) * QUAD].rearrange("p i t -> p t i"),
                                             bank[q % 8][:], ACT.Copy).then_inc(quad_read, 1)

        @block.tensor
        def _(pe):
            pe.sem_inc(quad_done, 2 * QUADS)
            with pe.Fori(0, TURNS // 4, 1) as i:
                for turn in range(4):
                    b = turn % 2
                    pe.wait_ge(hi_ready, 4 * i + turn + 1)
                    pe.wait_ge(lo_ready, 4 * i + turn + 1 + 2)
                    for n in range(QUADS):
                        q = turn * QUADS + n
                        pe.wait_ge(quad_read, i * 4 * QUADS + q + 1)
                        for c in range(QUAD):
                            t = n * QUAD + c
                            nc.tensor.matmul(bank[q][:, c, :], hot_j[b][:, t, :], hot_hi[b][:, t, :], start=True, stop=False)
                            mm = nc.tensor.matmul(bank[q][:, c, :], hot_j[b][:, t, :], hot_lo[b][:, t, :], start=False, stop=True)
                        mm.then_inc(quad_done, 1)


def experts(nc, u_tiles, v_dram, g_dram, h_hi, h_lo, acc):
    PAIRS = N_KEYS // 2
    with ExitStack() as ctx:
        p = Pool(nc, ctx)
        u_raw = p.sb("ex_u_raw", [P, KT, P])
        v_raw = p.sb("ex_v_raw", [P, D])
        u_hi = [p.sb(f"ex_u_hi{b}", [P, KT, P], F32R) for b in range(2)]
        u_lo = [p.sb(f"ex_u_lo{b}", [P, KT, P], F32R) for b in range(2)]
        v_hi = [p.sb(f"ex_v_hi{b}", [P, D], F32R) for b in range(4)]
        v_lo = [p.sb(f"ex_v_lo{b}", [P, D], F32R) for b in range(4)]
        gates = p.sb("ex_gates", [P, 2, SEQ])
        w_hi = [p.sb(f"ex_w_hi{b}", [P, SEQ], F32R) for b in range(4)]
        w_lo = [p.sb(f"ex_w_lo{b}", [P, SEQ], F32R) for b in range(4)]
        value = p.sb("ex_value", [P, 2, HALF])
        u_bank = [p.ps(f"ex_u_bank{b}", [P, HALF]) for b in range(4)]
        v_bank = [p.ps(f"ex_v_bank{b}", [P, HALF]) for b in range(4)]
        u_loaded, v_loaded = p.sem("ex_u_loaded"), p.sem("ex_v_loaded")
        g_loaded = [p.sem(f"ex_g_loaded{b}") for b in range(2)]
        u_hi_ready, v_hi_ready = p.sem("ex_u_hi_ready"), p.sem("ex_v_hi_ready")
        u_lo_ready, v_lo_ready = p.sem("ex_u_lo_ready"), p.sem("ex_v_lo_ready")
        u_done = p.sem("ex_u_done")
        gelu_done = p.sem("ex_gelu_done")
        gated = p.sem("ex_gated")
        w_hi_ready = p.sem("ex_w_hi_ready")
        w_lo_ready = p.sem("ex_w_lo_ready")
        v_done = p.sem("ex_v_done")
        added = p.sem("ex_added")
        block = ctx.enter_context(nc.Block())

        def walk(eng, visit):
            visit(0, 0, 0)
            with eng.Fori(0, (PAIRS - 2) // 2, 1) as i:
                visit(1, i, 1)
                visit(2, i, 1)
            visit(PAIRS - 1, 0, 0)

        @block.sync
        def _(sp):
            sp.sem_inc(u_lo_ready, 1)
            sp.sem_inc(v_lo_ready, 1)

            def load_u(e, i, step):
                sp.wait_ge(u_lo_ready, 4 * i + e + 1)
                src = u_tiles[bass.ds(i * 4 + e, 1)] if step else u_tiles[e:e + 1]
                sp.dma_start(u_raw[:], src.rearrange("o p (k n) -> (o p) k n", k=KT)).then_inc(u_loaded, 16)

            def load_v(e, i, step):
                sp.wait_ge(v_lo_ready, 4 * i + e + 1)
                src = v_dram[bass.ds(i * (4 * P) + e * P, P), :] if step else v_dram[e * P:(e + 1) * P, :]
                sp.dma_start(v_raw[:], src).then_inc(v_loaded, 16)

            def load_g(e, i, step):
                sp.wait_ge(gated, 8 * i + 2 * e + 2)
                src = g_dram[bass.ds(i * 4 + e, 1)] if step else g_dram[e:e + 1]
                sp.dma_start(gates[:, e % 2, :], src.rearrange("o j t -> (o j) t")).then_inc(g_loaded[e % 2], 16)

            load_u(0, 0, 0)
            load_u(1, 0, 0)
            load_g(0, 0, 0)
            load_g(1, 0, 0)

            def visit(r, i, step):
                for e in (2 * r, 2 * r + 1):
                    if r < PAIRS - 1:
                        load_u(e + 2, i, step)
                    load_v(e, i, step)
                    if r < PAIRS - 1:
                        load_g(e + 2, i, step)

            walk(sp, visit)

        @block.scalar
        def _(act):
            s = nc.scalar
            act.sem_inc(gelu_done, 4)

            def high_u(e, i):
                act.wait_ge(u_loaded, 64 * i + 16 * (e + 1))
                act.wait_ge(u_done, 8 * i + 2 * e + 2)
                s.activation(u_hi[e % 2][:], u_raw[:], ACT.Copy).then_inc(u_hi_ready, 1)

            high_u(0, 0)
            high_u(1, 0)

            def visit(r, i, step):
                for e in (2 * r, 2 * r + 1):
                    for half in range(2):
                        g = 2 * e + half
                        act.wait_ge(u_done, 8 * i + g + 1 + 4)
                        act.wait_ge(w_lo_ready, 8 * i + g + 1)
                        s.activation(value[:, g % 2, :], u_bank[g % 4][:], ACT.Gelu_apprx_tanh).then_inc(gelu_done, 1)
                        act.wait_ge(gated, 8 * i + g + 1 + 4)
                        act.wait_ge(v_done, 32 * i + 16 * (r + 1))
                        s.activation(w_hi[e % 4][:, half * HALF:(half + 1) * HALF], value[:, g % 2, :], ACT.Copy).then_inc(w_hi_ready, 1)
                    if r < PAIRS - 1:
                        high_u(e + 2, i)
                    act.wait_ge(v_loaded, 64 * i + 16 * (e + 1))
                    s.activation(v_hi[e % 4][:], v_raw[:], ACT.Copy).then_inc(v_hi_ready, 1)

            walk(act, visit)

        @block.gpsimd
        def _(pool):
            g_ = nc.gpsimd
            pool.sem_inc(w_lo_ready, 2)

            def low_u(e, i):
                pool.wait_ge(u_hi_ready, 4 * i + e + 1)
                g_.tensor_tensor(u_lo[e % 2][:], u_raw[:], f32(u_hi[e % 2][:]), ALU.subtract).then_inc(u_lo_ready, 1)

            low_u(0, 0)
            low_u(1, 0)

            def visit(r, i, step):
                for e in (2 * r, 2 * r + 1):
                    for half in range(2):
                        g = 2 * e + half
                        cols = slice(half * HALF, (half + 1) * HALF)
                        pool.wait_ge(w_hi_ready, 8 * i + g + 1)
                        g_.tensor_tensor(w_lo[e % 4][:, cols], value[:, g % 2, :], f32(w_hi[e % 4][:, cols]),
                                         ALU.subtract).then_inc(w_lo_ready, 1)
                    if r < PAIRS - 1:
                        low_u(e + 2, i)
                    pool.wait_ge(v_hi_ready, 4 * i + e + 1)
                    g_.tensor_tensor(v_lo[e % 4][:], v_raw[:], f32(v_hi[e % 4][:]), ALU.subtract).then_inc(v_lo_ready, 1)

            walk(pool, visit)

        @block.vector
        def _(dve):
            v = nc.vector
            dve.sem_inc(gated, 4)
            v.memset(acc[:], 0.0).then_inc(added, 16)

            def gate(g, i):
                e, half = g // 2, g % 2
                dve.wait_ge(gelu_done, 8 * i + g + 1 + 4)
                if half == 0:
                    dve.wait_ge(g_loaded[e % 2], 32 * i + 16 * (e // 2 + 1))
                v.tensor_tensor(value[:, g % 2, :], value[:, g % 2, :], gates[:, e % 2, half * HALF:(half + 1) * HALF],
                                ALU.mult).then_inc(gated, 1)

            def add(r, n, i):
                out = acc[:, n // 2, (n % 2) * HALF:(n % 2 + 1) * HALF]
                dve.wait_ge(v_done, 32 * i + 16 * r + n + 1 + 32)
                dve.wait_ge(added, 32 * i + 16 * r + n + 1)
                v.tensor_tensor(out, v_bank[n % 4][:], out, ALU.add).then_inc(added, 1)

            def visit(r, i, step):
                for n in range(16):
                    if r:
                        add(r - 1, n, i)
                    if n % 4 == 3:
                        gate(4 * r + n // 4, i)

            walk(dve, visit)
            for n in range(16):
                add(PAIRS - 1, n, 0)

        @block.tensor
        def _(pe):
            pe.sem_inc(u_done, 4)
            pe.sem_inc(v_done, 32)
            mm_ = nc.tensor.matmul

            def first(r, n, i):
                e, half = 2 * r + n // 8, (n // 4) % 2
                g = 2 * e + half
                if n % 8 == 0:
                    pe.wait_ge(u_lo_ready, 4 * i + e + 2)
                if n % 4 == 0:
                    pe.wait_ge(gelu_done, 8 * i + g + 1)
                cols = slice(half * HALF, (half + 1) * HALF)
                uh, ul = u_hi[e % 2], u_lo[e % 2]
                for k in (2 * (n % 4), 2 * (n % 4) + 1):
                    mm_(u_bank[g % 4][:], uh[:, k, :], h_hi[:, k, cols], start=(k == 0), stop=False)
                    mm_(u_bank[g % 4][:], uh[:, k, :], h_lo[:, k, cols], start=False, stop=False)
                    mm = mm_(u_bank[g % 4][:], ul[:, k, :], h_hi[:, k, cols], start=False, stop=(k == KT - 1))
                if n % 4 == 3:
                    mm.then_inc(u_done, 1)

            def second(r, n, i):
                if n == 0:
                    pe.wait_ge(w_lo_ready, 8 * i + 4 * r + 4 + 2)
                    pe.wait_ge(v_lo_ready, 4 * i + 2 * r + 3)
                pe.wait_ge(added, 32 * i + 16 * r + n + 13)
                rows = slice((n // 2) * P, (n // 2 + 1) * P)
                cols = slice((n % 2) * HALF, (n % 2 + 1) * HALF)
                for c in range(2):
                    b = (2 * r + c) % 4
                    mm_(v_bank[n % 4][:], w_hi[b][:, rows], v_hi[b][:, cols], start=(c == 0), stop=False)
                    mm_(v_bank[n % 4][:], w_hi[b][:, rows], v_lo[b][:, cols], start=False, stop=False)
                    mm = mm_(v_bank[n % 4][:], w_lo[b][:, rows], v_hi[b][:, cols], start=False, stop=(c == 1))
                mm.then_inc(v_done, 1)

            def visit(r, i, step):
                for n in range(16):
                    first(r, n, i)
                    if r:
                        second(r - 1, n, i)

            walk(pe, visit)
            for n in range(16):
                second(PAIRS - 1, n, 0)


def cols(v):
    v = v.reshape(-1, KT, P)
    return np.ascontiguousarray(v.transpose(2, 0, 1))


def column_blocks(w, width=NB):
    n = w.shape[1] // width
    return np.ascontiguousarray(w.reshape(KT, P, n, width).transpose(2, 1, 0, 3)).reshape(n, P, KT * width)


def rotary_tables():
    rows = np.repeat(np.arange(SEQ // GRID_W, dtype=np.float32), GRID_W)
    columns = np.tile(np.arange(GRID_W, dtype=np.float32), SEQ // GRID_W)
    quarter = DK // 4
    inv = (np.float32(10000.0) ** (-np.arange(quarter, dtype=np.float32) / np.float32(quarter))).astype(np.float32)
    ang = np.concatenate([rows[:, None] * inv, columns[:, None] * inv], axis=-1)
    return np.ascontiguousarray(np.stack([np.cos(ang).T, np.sin(ang).T], axis=1).astype(np.float32))


def layout(x, c, ctx, c_ctx, w_mod, b_mod, norm_gain, w_in, ret_decay_raw, w_ret_o, conv_w, conv_b,
           conv_norm_g, conv_norm_b, w_conv_o, w_out, peer_wq, peer_keys, peer_u, peer_v):
    return {
        "x": x[0], "ctx": ctx[0],
        "c_cols": np.ascontiguousarray(np.stack([c[0], c_ctx], -1).reshape(KT, P, 2).transpose(1, 0, 2)),
        "w_mod": column_blocks(w_mod[0]), "b_mod": cols(b_mod[0]), "gain": cols(norm_gain[0]),
        "w_in": np.ascontiguousarray(column_blocks(w_in[0])[W_IN_ORDER]),
        "decay": ret_decay_raw[0], "rotary": rotary_tables(),
        "w_ret_o": column_blocks(w_ret_o[0]), "w_conv_o": column_blocks(w_conv_o[0]), "w_out": column_blocks(w_out[0]),
        "conv_w": np.ascontiguousarray(conv_w[0].T.reshape(KT, P, CONV_W).transpose(1, 0, 2)),
        "w_query": column_blocks(peer_wq[0]),
        "keys": np.ascontiguousarray(peer_keys[0].reshape(SIDES, N_KEYS, P).transpose(2, 0, 1)),
        "u_tiles": np.ascontiguousarray(peer_u[0].reshape(N_KEYS, N_KEYS, KT, P).transpose(0, 3, 2, 1)).reshape(N_KEYS, P, D),
        "v": peer_v[0],
        "conv_b": cols(conv_b[0])[:, 0], "conv_norm_g": cols(conv_norm_g[0])[:, 0], "conv_norm_b": cols(conv_norm_b[0])[:, 0],
    }


def scratch(nc, name, shape):
    return nc.dram_tensor(name, shape, F32, kind="Internal").ap()


def mixer_program(nc, a, lat1, keep, ones, ident, mod, rows):
    fm = scratch(nc, "proj_fm", [FM_ROWS, SEQ])
    tm = scratch(nc, "proj_tm", [2 * HEADS, SEQ, DK])
    ctx_kv = scratch(nc, "ctx_kv", [2 * HEADS, CTX, DK])
    conv = scratch(nc, "conv_out", [D, SEQ])
    tokens = lambda dram: dram.rearrange("(t p) d -> p t d", p=P)

    with ExitStack() as s:
        p = Pool(nc, s)
        h_hi, h_lo = p.sb("h_hi", [P, KT, SEQ], F32R), p.sb("h_lo", [P, KT, SEQ], F32R)
        hc_hi, hc_lo = p.sb("hc_hi", [P, KT, CTX], F32R), p.sb("hc_lo", [P, KT, CTX], F32R)
        with ExitStack() as s2:
            q = Pool(nc, s2)
            x, cx = q.sb("x", [P, TT, D]), q.sb("cx", [P, CT, D])
            groups = [(1, 0, CT, k, mod["ac"][:, k:k + 1], mod["bc"][:, k:k + 1], hc_hi[:, k, :], hc_lo[:, k, :])
                      for k in range(KT)]
            groups += latent_groups(mod["a1"], mod["b1"], h_hi, h_lo)
            normalise(nc, "n1", [(x[:], tokens(a["x"])), (cx[:], tokens(a["ctx"]))], groups, ident)
        input_projection(nc, a["w_in"], h_hi, h_lo, hc_hi, hc_lo, fm, tm, ctx_kv, a["conv_w"], a["conv_b"], conv)

    with ExitStack() as s:
        p = Pool(nc, s)
        with ExitStack() as s2:
            q = Pool(nc, s2, "right")
            yg_hi, yg_lo = q.sb("yg_hi", [P, KT, SEQ], F32R), q.sb("yg_lo", [P, KT, SEQ], F32R)
            retention(nc, fm, tm, ctx_kv, a["decay"], a["rotary"], yg_hi, yg_lo, ident)
            merged = p.sb("merged", [P, KT, SEQ])
            project(nc, "pa", a["w_ret_o"], 2, yg_hi, yg_lo, False, fm[8 * NB:10 * NB, :], merged, False)
        with ExitStack() as s2:
            q = Pool(nc, s2, "right")
            u_hi, u_lo = q.sb("u_hi", [P, KT, SEQ], F32R), q.sb("u_lo", [P, KT, SEQ], F32R)
            conv_norm(nc, conv, a["conv_norm_g"], a["conv_norm_b"], u_hi, u_lo, ones)
            project(nc, "pb", a["w_conv_o"], 2, u_hi, u_lo, False, fm[10 * NB:12 * NB, :], merged, True)
        with ExitStack() as s2:
            q = Pool(nc, s2, "right")
            m_hi, m_lo = q.sb("m_hi", [P, KT, SEQ], F32R), q.sb("m_lo", [P, KT, SEQ], F32R)
            split_tile(nc, "ms", merged, m_hi, m_lo)
            project(nc, "po", a["w_out"], 2, m_hi, m_lo, True, None, merged, False)
        residual(nc, "r1", merged, a["x"], rows["g1"][:], lat1)
        h2 = Pool(nc, keep, "right")
        hi, lo = h2.sb("h2_hi", [P, KT, SEQ], F32R), h2.sb("h2_lo", [P, KT, SEQ], F32R)
        normalise(nc, "n2", [(merged[:], None)], latent_groups(mod["a2"], mod["b2"], hi, lo), ident)
    return hi, lo


def latent_groups(a, b, hi, lo):
    return [(0, 4 * half, 4, k, a[:, k:k + 1], b[:, k:k + 1], hi[:, k, half * HALF:(half + 1) * HALF],
             lo[:, k, half * HALF:(half + 1) * HALF]) for k in range(KT) for half in range(2)]


def spill(nc, name, pairs):
    with ExitStack() as ctx:
        p = Pool(nc, ctx)
        copied = p.sem(name + "_copied")
        block = ctx.enter_context(nc.Block())

        @block.gpsimd
        def _(pool):
            for dst, src in pairs:
                pool.dma_start(dst, src).then_inc(copied, 16)
            pool.wait_ge(copied, 16 * len(pairs))


def layer_program(nc, a, out):
    lat1 = scratch(nc, "lat1", [SEQ, D])
    scores = scratch(nc, "scores", [SEQ, SIDES * N_KEYS])
    gates = scratch(nc, "gates", [N_KEYS, N_KEYS, SEQ])
    kept_h2 = [nc.dram_tensor(f"kept_h2_{n}", [P, KT, SEQ], F32R, kind="Internal").ap() for n in ("hi", "lo")]
    with ExitStack() as keep:
        p = Pool(nc, keep)
        ones, ident = p.sb("ones", [P, P]), p.sb("ident", [P, P])
        mod = {k: p.sb("mod_" + k, [P, KT]) for k in ("a1", "b1", "a2", "b2", "ac", "bc")}
        g2_row = p.sb("row_g2", [P, D])
        constants(nc, ones, ident)
        with ExitStack() as s:
            rows = {"g1": Pool(nc, s).sb("row_g1", [P, D]), "g2": g2_row}
            conditioning(nc, a["c_cols"], a["w_mod"], a["b_mod"], a["gain"], mod, rows, ones[:], ident[:])
            h2 = mixer_program(nc, a, lat1, s, ones[:], ident[:], mod, rows)
            query_scores(nc, a["w_query"], a["keys"], *h2, scores)
            spill(nc, "keep_h2", [(dst, src[:]) for dst, src in zip(kept_h2, h2)])
        with ExitStack() as s:
            q = Pool(nc, s)
            first_T, second_T, gate_T = (q.sb(n, [P, SEQ]) for n in ("first_T", "second_T", "gate_T"))
            top_experts(nc, scores, first_T, second_T, gate_T, ident[:])
            gate_matrix(nc, first_T, second_T, gate_T, gates)
        acc = p.sb("retrieved", [P, TT, D])
        with ExitStack() as s:
            q = Pool(nc, s)
            h2 = [q.sb(f"again_h2_{n}", [P, KT, SEQ], F32R) for n in ("hi", "lo")]
            spill(nc, "again_h2", [(dst[:], src) for dst, src in zip(h2, kept_h2)])
            experts(nc, a["u_tiles"], a["v"], gates, *h2, acc)
        residual(nc, "r2", acc, lat1, g2_row[:], out)


def kernel(**inputs):
    from concourse import bacc
    from concourse.bass_utils import run_bass_kernel_spmd

    arrays = layout(**inputs)
    nc = bacc.Bacc("TRN2", target_bir_lowering=False, num_devices=1)
    a = {name: nc.dram_tensor("in_" + name, array.shape, mybir.dt.from_np(array.dtype),
                               kind="ExternalInput").ap()
         for name, array in arrays.items()}
    out = nc.dram_tensor("out", (SEQ, D), F32, kind="ExternalOutput").ap()
    layer_program(nc, a, out)
    nc.finalize()
    result = run_bass_kernel_spmd(nc, [{"in_" + name: array for name, array in arrays.items()}], core_ids=[0])
    return result.results[0]["out"][None]
```

```python
import numpy as np
from contextlib import ExitStack

import concourse.bass as bass
from concourse import mybir
from concourse.alu_op_type import AluOpType as ALU

ACT = mybir.ActivationFunctionType
AX = mybir.AxisListType
F32 = mybir.dt.float32
F32R = mybir.dt.float32r
BF16 = mybir.dt.bfloat16
I32 = mybir.dt.int32
U32 = mybir.dt.uint32

P = 128
SEQ = 1024
CTX = 256
D = 1024
KT = D // P
TT = SEQ // P
CT = CTX // P
HALF = 512
NB = 512
EPS = 1e-6
HEADS = 4
DK = 256
GRID_W = 64
CONV_W = 31


class Pool:

    def __init__(self, nc, ctx, side="left"):
        self.nc, self.ctx, self.side, self.sems = nc, ctx, side, []
        ctx.callback(self.give_back)

    def give_back(self):
        if self.sems:
            self.nc.clear_and_free_semaphores(self.sems)
            self.nc.all_engine_barrier()

    def sem(self, name):
        self.sems.append(self.nc.alloc_semaphore(name))
        return self.sems[-1]

    def sb(self, name, shape, dt=F32):
        return self.ctx.enter_context(self.nc.sbuf_tensor(name, shape, dt, side=self.side))

    def ps(self, name, shape, dt=F32):
        return self.ctx.enter_context(self.nc.psum_tensor(name, shape, dt))


class Chain:

    def __init__(self, eng, sem, base=0, per_turn=0, i=0):
        self.eng, self.sem, self.base, self.per_turn, self.i, self.taken = eng, sem, base, per_turn, i, 0

    def step(self, instruction):
        self.taken += 1
        instruction.then_inc(self.sem, 1)
        count = self.base + self.taken
        self.eng.wait_ge(self.sem, self.i * self.per_turn + count if self.per_turn else count)


def f32(ap):
    return ap.bitcast(F32)


def split_matmuls(nc, out, pairs):
    last = None
    for n, ((s_hi, s_lo), (m_hi, m_lo)) in enumerate(pairs):
        nc.tensor.matmul(out, s_hi, m_hi, start=(n == 0), stop=False)
        nc.tensor.matmul(out, s_hi, m_lo, start=False, stop=False)
        last = nc.tensor.matmul(out, s_lo, m_hi, start=False, stop=(n == len(pairs) - 1))
    return last

BLOCKS = ["glu_a", "glu_b", "glu_a", "glu_b", "q", "q", "k", "k",
          "gate_a", "gate_a", "gate_b", "gate_b", "v", "v", "g_ret", "g_ret"]
W_IN_ORDER = [8, 10, 9, 11, 0, 1, 2, 3, 12, 13, 14, 15, 4, 5, 6, 7]
FM_ROWS = 12 * NB


def input_projection(nc, w_blocks, h_hi, h_lo, hc_hi, hc_lo, fm, tm, ctx_kv, conv_w, conv_b, conv):
    with ExitStack() as ctx:
        p = Pool(nc, ctx)
        RING = 4
        raw = p.sb("ip_raw", [P, KT * NB])
        w_hi = [p.sb(f"ip_w_hi{b}", [P, KT * NB], F32R) for b in range(2)]
        w_lo = [p.sb(f"ip_w_lo{b}", [P, KT * NB], F32R) for b in range(2)]
        stage = p.sb("ip_stage", [P, RING, HALF])
        bank = [p.ps(f"ip_bank{b}", [P, HALF]) for b in range(RING)]

        glu = p.sb("ip_glu", [P, 2, SEQ])
        PAD = CONV_W // 2
        padded = [p.sb(f"ip_padded{b}", [P, SEQ + 2 * PAD]) for b in range(2)]
        convolved = p.sb("ip_convolved", [P, 2, SEQ])
        taps = p.sb("ip_taps", [P, KT, CONV_W])
        conv_bias = p.sb("ip_conv_bias", [P, KT])

        taps_loaded = p.sem("ip_taps_loaded")
        glu_loaded = p.sem("ip_glu_loaded")
        sigmoid_ready = p.sem("ip_sigmoid_ready")
        glu_ready = p.sem("ip_glu_ready")
        conv_chain = p.sem("ip_conv_chain")
        conv_ready = p.sem("ip_conv_ready")
        conv_stored = [p.sem(f"ip_conv_stored{b}") for b in range(2)]
        raw_loaded = p.sem("ip_raw_loaded")
        hi_ready = p.sem("ip_hi_ready")
        lo_ready = p.sem("ip_lo_ready")
        group_done = p.sem("ip_group_done")
        evacuated = p.sem("ip_evacuated")
        stored = [p.sem(f"ip_stored{r}") for r in range(RING)]

        SEGMENTS = [(0, 2, False, False, True), (4, 1, False, False, False), (6, 1, False, True, False),
                    (8, 2, False, False, True), (12, 1, True, True, False), (14, 1, True, False, False)]
        N_BLOCKS = 16
        CONV_FIRST = 4

        def walk(eng, visit):
            group = 0
            for first, pairs, token_major, context, rolled in SEGMENTS:
                per_block = 8 + (CT if context else 0)
                if rolled:
                    with eng.Fori(0, pairs, 1) as i:
                        for b in range(2):
                            visit(first + b, i, b, group + b * per_block, 2 * per_block,
                                  token_major, context, True, True)
                else:
                    for b in range(2):
                        blk = first + b
                        visit(blk, 0, b, group + b * per_block, 0, token_major, context,
                              blk + 1 < N_BLOCKS, blk + 2 < N_BLOCKS)
                group += 2 * pairs * per_block

        block = ctx.enter_context(nc.Block())

        @block.sync
        def _(sp):
            for r in range(RING):
                sp.sem_inc(stored[r], 16)
            sp.dma_start(raw[:], w_blocks[0]).then_inc(raw_loaded, 16)
            sp.dma_start(taps[:], conv_w).then_inc(taps_loaded, 16)
            sp.dma_start(conv_bias[:], conv_b).then_inc(taps_loaded, 16)
            for b in range(2):
                sp.sem_inc(conv_stored[b], 16)
            sp.sem_inc(conv_ready, 2)
            sp.wait_ge(lo_ready, 1)
            sp.dma_start(raw[:], w_blocks[1]).then_inc(raw_loaded, 16)

            def visit(blk, i, b, group, step, token_major, context, ahead, load):
                if load:
                    sp.wait_ge(lo_ready, blk + 2 + 2 * i)
                    src = w_blocks[bass.ds(blk + 2 + 2 * i, 1)] if step else w_blocks[blk + 2:blk + 3]
                    sp.dma_start(raw[:], src.rearrange("o p n -> (o p) n")).then_inc(raw_loaded, 16)
                tile = blk - CONV_FIRST
                if 0 <= tile < KT:
                    if tile == 0:
                        for r in range(RING):
                            sp.wait_ge(stored[r], 16 * (CONV_FIRST * 8 // RING + 1))
                    else:
                        sp.wait_ge(glu_ready, tile + 2 * i)
                    row = tile * P + (tile // 4) * NB
                    rows = fm[bass.ds(row + 2 * P * i, P + NB), :] if step else fm[row:row + P + NB, :]
                    for j in range(2):
                        sp.dma_start(glu[:, j, :], rows[j * NB:j * NB + P, :]).then_inc(glu_loaded, 16)
                if 0 < tile <= KT:
                    store_tile(tile - 1, i if step else 0, step)
                for g in range(8 + (CT if context else 0)):
                    sp.wait_ge(evacuated, group + g + 1 + RING + step * i)
                    slot = (group + g) % RING
                    if g >= 8:
                        j = (blk - 6) if blk < 8 else (blk - 12 + 2)
                        dst = ctx_kv[2 * j:2 * j + 2, (g - 8) * P:(g - 7) * P, :].rearrange("e t d -> t e d")
                    elif token_major:
                        h = 2 * (blk - 12)
                        dst = tm[h:h + 2, g * P:(g + 1) * P, :].rearrange("e t d -> t e d")
                    else:
                        row = blk * NB + (g // 2) * P
                        cols = slice((g % 2) * HALF, (g % 2 + 1) * HALF)
                        dst = fm[bass.ds(row + 2 * NB * i, P), cols] if step else fm[row:row + P, cols]
                    src = stage[:, slot, :]
                    if g >= 8 or token_major:
                        src = src.rearrange("p (e d) -> p e d", e=2)
                    sp.dma_start(dst, src).then_inc(stored[slot], 16)

            def store_tile(tile, i, step):
                sp.wait_ge(conv_ready, tile + 3 + 2 * i)
                dst = conv[bass.ds(tile * P + 2 * P * i, P), :] if step else conv[tile * P:(tile + 1) * P, :]
                sp.dma_start(dst, convolved[:, tile % 2, :]).then_inc(conv_stored[tile % 2], 16)

            walk(sp, visit)
            for b in range(2):
                sp.wait_ge(conv_stored[b], 16 * (KT // 2 + 1))
            total = 16 * 8 + 4 * CT
            for r in range(RING):
                sp.wait_ge(stored[r], 16 * (total // RING + 1))

        @block.scalar
        def _(act):
            def split(blk, i, b):
                act.wait_ge(raw_loaded, 16 * (blk + 1) + 32 * i)
                nc.scalar.activation(w_hi[b][:], raw[:], ACT.Copy).then_inc(hi_ready, 1)

            split(0, 0, 0)

            def visit(blk, i, b, group, step, token_major, context, ahead, load):
                if ahead:
                    split(blk + 1, i, 1 - b)
                tile = blk - CONV_FIRST
                for g in range(8 + (CT if context else 0)):
                    if g == 1 and 0 <= tile < KT:
                        act.wait_ge(glu_loaded, 32 * (tile + 1) + 64 * i)
                        nc.scalar.activation(glu[:, 1, :], glu[:, 1, :], ACT.Sigmoid).then_inc(sigmoid_ready, 1)
                    slot = (group + g) % RING
                    act.wait_ge(group_done, group + g + 1 + step * i)
                    act.wait_ge(stored[slot], 16 * ((group + g) // RING + 1) + 16 * (step // RING) * i)
                    nc.scalar.activation(stage[:, slot, :], bank[slot][:], ACT.Copy).then_inc(evacuated, 1)

            walk(act, visit)

        @block.vector
        def _(dve):
            def visit(blk, i, b, group, step, token_major, context, ahead, load):
                tile = blk - CONV_FIRST
                if 0 <= tile < KT:
                    chain = Chain(dve, conv_chain, (CONV_W - 1) * tile, 2 * (CONV_W - 1) if step else 0, i)
                    out = convolved[:, tile % 2, :]
                    tap = taps[:, bass.ds(tile + 2 * i, 1), :] if step else taps[:, tile:tile + 1, :]
                    tap = tap.rearrange("p o w -> p (o w)")
                    bias = conv_bias[:, bass.ds(tile + 2 * i, 1)] if step else conv_bias[:, tile:tile + 1]
                    dve.wait_ge(glu_ready, tile + 1 + 2 * i)
                    dve.wait_ge(conv_stored[tile % 2], 16 * (tile // 2 + 1) + 16 * i)
                    chain.step(nc.vector.tensor_scalar(out, padded[tile % 2][:, 0:SEQ], tap[:, 0:1], bias, ALU.mult, ALU.add))
                    for w in range(1, CONV_W):
                        add = nc.vector.scalar_tensor_tensor(out=out, in0=padded[tile % 2][:, w:w + SEQ], scalar=tap[:, w:w + 1],
                                                             in1=out, op0=ALU.mult, op1=ALU.add)
                        if w < CONV_W - 1:
                            chain.step(add)
                        else:
                            add.then_inc(conv_ready, 1)

            dve.wait_ge(taps_loaded, 32)
            walk(dve, visit)

        @block.gpsimd
        def _(pool):
            def low_part(blk, i, b):
                pool.wait_ge(hi_ready, blk + 1 + 2 * i)
                nc.gpsimd.tensor_tensor(w_lo[b][:], raw[:], f32(w_hi[b][:]), ALU.subtract).then_inc(lo_ready, 1)

            for b in range(2):
                nc.gpsimd.memset(padded[b][:, 0:PAD], 0.0)
                nc.gpsimd.memset(padded[b][:, SEQ + PAD:], 0.0)
            low_part(0, 0, 0)

            def visit(blk, i, b, group, step, token_major, context, ahead, load):
                if ahead:
                    low_part(blk + 1, i, 1 - b)
                tile = blk - CONV_FIRST
                if 0 <= tile < KT:
                    pool.wait_ge(sigmoid_ready, tile + 1 + 2 * i)
                    pool.wait_ge(conv_ready, tile + 1 + 2 * i)
                    nc.gpsimd.tensor_tensor(padded[tile % 2][:, PAD:PAD + SEQ], glu[:, 0, :], glu[:, 1, :],
                                            ALU.mult).then_inc(glu_ready, 1)

            walk(pool, visit)

        @block.tensor
        def _(pe):
            pe.sem_inc(evacuated, RING)

            def visit(blk, i, b, group, step, token_major, context, ahead, load):
                pe.wait_ge(lo_ready, blk + 1 + 2 * i)
                wh = w_hi[b][:].rearrange("p (k n) -> p k n", k=KT)
                wl = w_lo[b][:].rearrange("p (k n) -> p k n", k=KT)
                for g in range(8 + (CT if context else 0)):
                    slot = (group + g) % RING
                    pe.wait_ge(evacuated, group + g + 1 + step * i)
                    if g >= 8:
                        c = slice((g - 8) * P, (g - 7) * P)
                        pairs = [((hc_hi[:, k, c], hc_lo[:, k, c]), (wh[:, k, :], wl[:, k, :])) for k in range(KT)]
                    elif token_major:
                        c = slice(g * P, (g + 1) * P)
                        pairs = [((h_hi[:, k, c], h_lo[:, k, c]), (wh[:, k, :], wl[:, k, :])) for k in range(KT)]
                    else:
                        n = slice((g // 2) * P, (g // 2 + 1) * P)
                        c = slice((g % 2) * HALF, (g % 2 + 1) * HALF)
                        pairs = [((wh[:, k, n], wl[:, k, n]), (h_hi[:, k, c], h_lo[:, k, c])) for k in range(KT)]
                    split_matmuls(nc, bank[slot][:], pairs).then_inc(group_done, 1)

            walk(pe, visit)


def rsqrt_of_mean(nc, chain, act_sqrt, out, sums, scratch, n):
    v = nc.vector
    mean, root, y2 = scratch
    chain.step(v.tensor_scalar(mean, sums, 1.0 / n, EPS, ALU.mult, ALU.add))
    act_sqrt(root, mean)
    chain.step(v.reciprocal(out, root))
    chain.step(v.tensor_tensor(y2, out, out, ALU.mult))
    chain.step(v.tensor_tensor(y2, y2, mean, ALU.mult))
    chain.step(v.tensor_scalar(y2, y2, -0.5, 1.5, ALU.mult, ALU.add))
    chain.step(v.tensor_tensor(out, out, y2, ALU.mult))

SH1, SC1, G1, SH2, SC2, G2 = range(6)


def conditioning(nc, c_cols, w_mod_blocks, b_mod_cols, gain_cols, mod, rows, ones, ident):
    NBLK = 12
    with ExitStack() as ctx:
        p = Pool(nc, ctx)
        w = [p.sb(f"cd_w{b}", [P, KT, NB]) for b in range(3)]
        c2 = p.sb("cd_c", [P, KT, 2])
        c2s = p.sb("cd_cs", [P, KT, 2])
        bias = p.sb("cd_bias", [P, 6, KT])
        gain = p.sb("cd_gain", [P, 4, KT])
        lat = p.sb("cd_lat", [P, 6, KT])
        cmod = p.sb("cd_cmod", [P, 2, KT])
        g12 = p.sb("cd_g12", [P, 2, KT])
        diag = p.sb("cd_diag", [P, 2, D])
        row2 = p.sb("cd_row2", [2, 6 * D])
        row_bank = [p.ps(f"cd_row_bank{b}", [2, NB]) for b in range(2)]
        acc = p.ps("cd_acc", [P, 6 * KT, 2])
        spread = [p.ps(f"cd_spread{n}", [P, HALF]) for n in range(4)]
        small_loaded = p.sem("cd_small_loaded")
        w_loaded = [p.sem(f"cd_w_loaded{b}") for b in range(3)]
        w_used = p.sem("cd_w_used")
        silu_ready = p.sem("cd_silu_ready")
        row_copied = p.sem("cd_row_copied")
        turned = p.sem("cd_turned")
        chained = p.sem("cd_chained")
        diag_ready = p.sem("cd_diag_ready")
        spread_done = p.sem("cd_spread_done")
        block = ctx.enter_context(nc.Block())

        @block.sync
        def _(sp):
            sp.dma_start(c2[:], c_cols).then_inc(small_loaded, 16)
            sp.dma_start(bias[:], b_mod_cols).then_inc(small_loaded, 16)
            sp.dma_start(gain[:], gain_cols).then_inc(small_loaded, 16)
            for n in range(NBLK):
                if n >= 3:
                    sp.wait_ge(w_used, n - 2)
                sp.dma_start(w[n % 3][:].rearrange("p k n -> p (k n)"), w_mod_blocks[n]).then_inc(w_loaded[n % 3], 16)

        @block.scalar
        def _(act):
            act.wait_ge(small_loaded, 48)
            nc.scalar.activation(c2s[:], c2[:], ACT.Silu).then_inc(silu_ready, 1)
            for n in range(NBLK):
                act.wait_ge(w_used, n + 1)
                nc.scalar.activation(row2[:, n * NB:(n + 1) * NB], row_bank[n % 2][:], ACT.Copy).then_inc(row_copied, 1)

        @block.tensor
        def _(pe):
            pe.wait_ge(silu_ready, 1)
            for n in range(NBLK):
                pe.wait_ge(w_loaded[n % 3], 16 * (n // 3 + 1))
                if n >= 2:
                    pe.wait_ge(row_copied, n - 1)
                for k in range(KT):
                    mm = nc.tensor.matmul(row_bank[n % 2][:], c2s[:, k, :], w[n % 3][:, k, :],
                                          start=(k == 0), stop=(k == KT - 1))
                mm.then_inc(w_used, 1)
            pe.wait_ge(row_copied, NBLK)
            for m in range(6 * KT):
                tr = nc.tensor.transpose(acc[:, m, :], row2[:, m * P:(m + 1) * P], ident[0:2, 0:2])
            tr.then_inc(turned, 1)
            pe.wait_ge(diag_ready, 1)
            for n in range(4):
                mm = nc.tensor.matmul(spread[n][:], ones, diag[:, n // 2, (n % 2) * HALF:(n % 2 + 1) * HALF],
                                      start=True, stop=True)
            mm.then_inc(spread_done, 1)

        @block.vector
        def _(dve):
            v = nc.vector
            chain = Chain(dve, chained)
            dve.wait_ge(small_loaded, 48)
            dve.wait_ge(turned, 1)
            sums = acc[:].rearrange("p (m k) c -> p m k c", m=6)
            chain.step(v.tensor_tensor(lat[:], sums[:, :, :, 0], bias[:], ALU.add))
            chain.step(v.tensor_tensor(cmod[:], sums[:, 0:2, :, 1], bias[:, 0:2, :], ALU.add))
            for a, b, source, sh, sc, g in (("a1", "b1", lat, SH1, SC1, 0), ("a2", "b2", lat, SH2, SC2, 2),
                                            ("ac", "bc", cmod, SH1, SC1, 0)):
                chain.step(v.scalar_tensor_tensor(out=mod[a][:], in0=source[:, sc, :], scalar=1.0, in1=gain[:, g, :],
                                                  op0=ALU.add, op1=ALU.mult))
                chain.step(v.tensor_copy(mod[b][:], source[:, sh, :]))
            chain.step(v.tensor_tensor(g12[:, 0, :], lat[:, G1, :], gain[:, 1, :], ALU.mult))
            chain.step(v.tensor_tensor(g12[:, 1, :], lat[:, G2, :], gain[:, 3, :], ALU.mult))
            for m in range(2):
                for k in range(KT):
                    last = v.tensor_scalar(diag[:, m, k * P:(k + 1) * P], ident, g12[:, m, k:k + 1], None, ALU.mult)
            last.then_inc(diag_ready, 1)
            dve.wait_ge(spread_done, 1)
            for m, row in enumerate((rows["g1"], rows["g2"])):
                for half in range(2):
                    v.tensor_copy(row[:, half * HALF:(half + 1) * HALF], spread[2 * m + half][:])


def normalise(nc, name, sources, groups, ident):
    with ExitStack() as ctx:
        p = Pool(nc, ctx)
        RING = 4
        tiles = sum(x.shape[1] for x, _ in sources)
        at = [sum(x.shape[1] for x, _ in sources[:n]) for n in range(len(sources))]
        squares = p.sb(name + "_squares", [P, D])
        sums = p.sb(name + "_sums", [P, tiles])
        rstd = p.sb(name + "_rstd", [P, tiles])
        scratch = [p.sb(f"{name}_scratch{n}", [P, tiles]) for n in range(3)]
        value = p.sb(name + "_value", [P, RING, HALF])
        bank = [p.ps(f"{name}_bank{b}", [P, HALF]) for b in range(RING)]
        loaded = [p.sem(f"{name}_loaded{n}") for n in range(len(sources))]
        summed = p.sem(name + "_summed")
        mean_ready = p.sem(name + "_mean_ready")
        root_ready = p.sem(name + "_root_ready")
        chained = p.sem(name + "_chained")
        scaled = p.sem(name + "_scaled")
        turned = p.sem(name + "_turned")
        valued = p.sem(name + "_valued")
        high = p.sem(name + "_high")
        low = p.sem(name + "_low")
        block = ctx.enter_context(nc.Block())

        @block.sync
        def _(sp):
            for n, (x, dram) in enumerate(sources):
                if dram is not None:
                    sp.dma_start(x, dram).then_inc(loaded[n], 16)

        @block.scalar
        def _(act):
            for n, (x, dram) in enumerate(sources):
                if dram is not None:
                    act.wait_ge(loaded[n], 16)
                for t in range(x.shape[1]):
                    c = at[n] + t
                    if c:
                        act.wait_ge(summed, c)
                    nc.scalar.activation(squares[:], x[:, t, :], ACT.Square, accum_out=sums[:, c:c + 1]).then_inc(summed, 1)
            act.wait_ge(mean_ready, 1)
            nc.scalar.activation(scratch[1][:], scratch[0][:], ACT.Sqrt).then_inc(root_ready, 1)
            for g, (_, _, m, _, _, _, hi, _) in enumerate(groups):
                act.wait_ge(valued, g + 1)
                nc.scalar.activation(hi, value[:, g % RING, 0:m * P], ACT.Copy).then_inc(high, 1)

        @block.vector
        def _(dve):
            v = nc.vector
            chain = Chain(dve, chained)
            dve.wait_ge(summed, tiles)

            def act_sqrt(root, mean):
                v.tensor_copy(scratch[2][:], mean).then_inc(mean_ready, 1)
                dve.wait_ge(root_ready, 1)

            rsqrt_of_mean(nc, chain, act_sqrt, rstd[:], sums[:], (scratch[0][:], scratch[1][:], scratch[2][:]), D)
            for n, (x, _) in enumerate(sources):
                for t in range(x.shape[1]):
                    v.tensor_scalar(x[:, t, :], x[:, t, :], rstd[:, at[n] + t:at[n] + t + 1], None, ALU.mult).then_inc(scaled, 1)

            def low_part(g):
                m, lo, hi = groups[g][2], groups[g][7], groups[g][6]
                dve.wait_ge(high, g + 1)
                v.tensor_tensor(lo, value[:, g % RING, 0:m * P], f32(hi), ALU.subtract).then_inc(low, 1)

            for g, (_, _, m, _, a, b, _, _) in enumerate(groups):
                dve.wait_ge(turned, g + 1)
                if g >= RING:
                    dve.wait_ge(low, g - RING + 1)
                v.tensor_scalar(value[:, g % RING, 0:m * P], bank[g % RING][:, 0:m * P], a, b,
                                ALU.mult, ALU.add).then_inc(valued, 1)
                if g >= 1:
                    low_part(g - 1)
            low_part(len(groups) - 1)

        @block.tensor
        def _(pe):
            pe.wait_ge(scaled, tiles)
            for g, (n, first, m, k, _, _, _, _) in enumerate(groups):
                if g >= RING:
                    pe.wait_ge(valued, g - RING + 1)
                for t in range(m):
                    tr = nc.tensor.transpose(bank[g % RING][:, t * P:(t + 1) * P],
                                             sources[n][0][:, first + t, k * P:(k + 1) * P], ident)
                tr.then_inc(turned, 1)


def constants(nc, ones, ident):
    with ExitStack() as ctx:
        p = Pool(nc, ctx)
        zeroed = p.sem("cs_zeroed")
        block = ctx.enter_context(nc.Block())

        @block.gpsimd
        def _(pool):
            nc.gpsimd.memset(ones[:], 1.0)
            nc.gpsimd.memset(ident[:], 0.0).then_inc(zeroed, 1)
            pool.wait_ge(zeroed, 1)
            nc.gpsimd.affine_select(out=ident[:], in_=ident[:], compare_op=ALU.not_equal, fill=1.0, base=0,
                                    pattern=[[-1, P]], channel_multiplier=1)

CHUNK = 128
NC_ = SEQ // CHUNK
Q_ROW, K_ROW = 4 * NB, 6 * NB

ROTATE_STEPS = 3


def rotate(engine, chain, out, raw, cos_sin, tmp, done):
    cos, sin = cos_sin[:, 0, :], cos_sin[:, 1, :]
    engine.tensor_tensor(out[:, 0, :], raw[:, 0, :], cos, ALU.mult)
    engine.tensor_tensor(out[:, 1, :], raw[:, 0, :], sin, ALU.mult)
    chain.step(engine.tensor_tensor(tmp[:], raw[:, 1, :], sin, ALU.mult))
    chain.step(engine.tensor_tensor(out[:, 0, :], out[:, 0, :], tmp[:], ALU.subtract))
    chain.step(engine.tensor_tensor(tmp[:], raw[:, 1, :], cos, ALU.mult))
    engine.tensor_tensor(out[:, 1, :], out[:, 1, :], tmp[:], ALU.add).then_inc(done, 1)


def retention(nc, fm, tm, ctx_kv, decay_raw, cos_sin, yg_hi, yg_lo, ident):
    with ExitStack() as ctx:
        p = Pool(nc, ctx)
        q_raw = p.sb("rt_q_raw", [P, 2, SEQ])
        k_raw = p.sb("rt_k_raw", [P, 2, SEQ])
        q = p.sb("rt_q", [P, 2, SEQ])
        k = p.sb("rt_k", [P, 2, SEQ])
        v = p.sb("rt_v", [P, NC_, DK])
        gate = p.sb("rt_gate", [P, NC_, DK])
        kc = p.sb("rt_kc", [P, CT, DK])
        vc = p.sb("rt_vc", [P, CT, DK])
        kcd = [p.sb(f"rt_kcd{d}", [P, CT, DK]) for d in range(2)]
        kd = [p.sb(f"rt_kd{d}", [P, NC_, DK]) for d in range(2)]
        state = [p.sb(f"rt_state{d}", [P, 2, DK]) for d in range(2)]
        y = p.sb("rt_y", [P, NC_, DK])
        weights = p.sb("rt_weights", [P, NC_, CHUNK])
        cs = p.sb("rt_cos_sin", [P, 2, SEQ])
        tmp_q = p.sb("rt_tmp_q", [P, SEQ])
        tmp_k = p.sb("rt_tmp_k", [P, SEQ])
        value = p.sb("rt_value", [P, 2, HALF])
        dist = p.sb("rt_dist", [P, 2, CHUNK])
        side = p.sb("rt_side", [P, 2, CHUNK])
        delta = p.sb("rt_delta", [P, CHUNK])
        powers = p.sb("rt_powers", [P, 2, 5])
        power_i = p.sb("rt_power_i", [P, 2, 5], I32)
        delta_i = p.sb("rt_delta_i", [P, CHUNK], I32)
        dec = p.sb("rt_dec", [P, 2, 5])
        mask2 = p.sb("rt_mask2", [P, 2, CHUNK])
        mask = p.sb("rt_mask", [P, CHUNK])
        raw_all = p.sb("rt_raw_all", [P, 2, HEADS])
        raw_dec = p.sb("rt_raw_dec", [P, 2])
        lg = p.sb("rt_lg", [P, 2])
        small = [p.sb(f"rt_small{n}", [P, 2]) for n in range(6)]
        square = p.sb("rt_square", [P, DK])
        sums = p.sb("rt_sums", [P, NC_])
        rstd = p.sb("rt_rstd", [P, NC_])
        scratch = [p.sb(f"rt_scratch{n}", [P, NC_]) for n in range(3)]

        work = [p.ps(f"rt_work{b}", [P, HALF]) for b in range(2)]
        upd = [p.ps(f"rt_upd{d}", [P, 2, DK]) for d in range(2)]
        cross = [[p.ps(f"rt_cross{d}{b}", [P, DK]) for b in range(2)] for d in range(2)]

        tables_loaded = p.sem("rt_tables_loaded")
        made = p.sem("rt_made")
        decay_loaded = p.sem("rt_decay_loaded")
        q_loaded, k_loaded, kc_loaded, vc_loaded, v_loaded, g_loaded = (
            p.sem(f"rt_{x}_loaded") for x in ("q", "k", "kc", "vc", "v", "g"))
        q_rotated = p.sem("rt_q_rotated")
        k_rotated = p.sem("rt_k_rotated")
        pool_chain = p.sem("rt_pool_chain")
        dve_chain = p.sem("rt_dve_chain")
        lg_exp = p.sem("rt_lg_exp")
        lg_asked = p.sem("rt_lg_asked")
        lg_ready = p.sem("rt_lg_ready")
        decays = p.sem("rt_decays")
        kc_scaled = p.sem("rt_kc_scaled")
        ctx_done = p.sem("rt_ctx_done")
        state_set = p.sem("rt_state_set")
        kt_done, kt_read = p.sem("rt_kt_done"), p.sem("rt_kt_read")
        sc_done, sc_read = p.sem("rt_sc_done"), p.sem("rt_sc_read")
        in_done, in_read = p.sem("rt_in_done"), p.sem("rt_in_read")
        yt_done, yt_read = p.sem("rt_yt_done"), p.sem("rt_yt_read")
        stepped = p.sem("rt_stepped")
        advanced = p.sem("rt_advanced")
        y_summed = p.sem("rt_y_summed")
        squared = p.sem("rt_squared")
        root_asked = p.sem("rt_root_asked")
        root_ready = p.sem("rt_root_ready")
        silu_ready = p.sem("rt_silu_ready")
        gated = p.sem("rt_gated")
        high = p.sem("rt_high")
        low = p.sem("rt_low")

        block = ctx.enter_context(nc.Block())

        @block.sync
        def _(sp):
            sp.sem_inc(q_rotated, 1)
            sp.dma_start(raw_all[:].rearrange("p d h -> p (d h)"),
                         decay_raw.rearrange("(o d) h -> o (d h)", o=1).to_broadcast([P, 2 * HEADS])).then_inc(decay_loaded, 16)
            sp.dma_start(cs[:], cos_sin).then_inc(tables_loaded, 16)
            with sp.Fori(0, HEADS, 1) as i:
                q_row, k_row = sp.snap(i * DK + Q_ROW), sp.snap(i * DK + K_ROW)
                v_head, g_head = sp.snap(i * 1), sp.snap(i + HEADS)
                sp.wait_ge(q_rotated, i + 1)
                sp.dma_start(q_raw[:], fm[bass.ds(q_row, DK), :].rearrange("(j p) t -> p j t", p=P)).then_inc(q_loaded, 16)
                sp.wait_ge(k_rotated, i + 1)
                sp.dma_start(k_raw[:], fm[bass.ds(k_row, DK), :].rearrange("(j p) t -> p j t", p=P)).then_inc(k_loaded, 16)
                sp.wait_ge(ctx_done, i + 1)
                sp.dma_start(kc[:], ctx_kv[bass.ds(i, 1)].rearrange("o (c p) d -> p (o c) d", p=P)).then_inc(kc_loaded, 16)
                sp.dma_start(vc[:], ctx_kv[bass.ds(g_head, 1)].rearrange("o (c p) d -> p (o c) d", p=P)).then_inc(vc_loaded, 16)
                sp.wait_ge(stepped, i * 16 + 16)
                sp.dma_start(v[:], tm[bass.ds(i, 1)].rearrange("o (c p) d -> p (o c) d", p=P)).then_inc(v_loaded, 16)
                sp.wait_ge(gated, i + 1)
                sp.dma_start(gate[:], tm[bass.ds(g_head, 1)].rearrange("o (c p) d -> p (o c) d", p=P)).then_inc(g_loaded, 16)

        @block.gpsimd
        def _(pool):
            g = nc.gpsimd
            pool.sem_inc(k_rotated, 1)
            for d, cols in enumerate((((1, 1), (-1, CHUNK - 1), (0, CHUNK), (-1, CTX - 1), (-1, CTX - 1 - P)),
                                      ((-1, CHUNK), (1, 0), (0, CHUNK), (1, 0), (1, P)))):
                for c, (mult, base) in enumerate(cols):
                    g.iota(power_i[:, d, c:c + 1], pattern=[[0, 1]], base=base, channel_multiplier=mult)
            g.iota(delta_i[:], pattern=[[1, CHUNK]], base=0, channel_multiplier=-1).then_inc(made, 1)
            pool.wait_ge(tables_loaded, 16)
            with pool.Fori(0, HEADS, 1) as i:
                pool.wait_ge(k_loaded, 16 * i + 16)
                chain = Chain(pool, pool_chain, 0, ROTATE_STEPS, i)
                pool.wait_ge(sc_done, i * 2 + 2)
                rotate(g, chain, k, k_raw, cs, tmp_k, k_rotated)

        @block.scalar
        def _(act):
            s = nc.scalar
            with act.Fori(0, HEADS, 1) as i:
                act.wait_ge(lg_asked, 2 * i + 1)
                s.activation(small[1][:], small[0][:], ACT.Exp).then_inc(lg_exp, 1)
                act.wait_ge(lg_asked, 2 * i + 2)
                s.activation(small[3][:], small[2][:], ACT.Ln).then_inc(lg_exp, 1)
                act.wait_ge(lg_ready, i + 1)
                for d in range(2):
                    s.activation(dec[:, d, :], powers[:, d, :], ACT.Exp, scale=lg[:, d:d + 1])
                    last = s.activation(mask2[:, d, :], dist[:, d, :], ACT.Exp, scale=lg[:, d:d + 1])
                last.then_inc(decays, 1)
                act.wait_ge(ctx_done, i + 2)
                for d in range(2):
                    last = s.activation(state[d][:], upd[d][:], ACT.Copy)
                last.then_inc(state_set, 1)
                for n in range(4):
                    act.wait_ge(in_done, 4 * i + n + 1)
                    s.activation(y[:, 2 * n:2 * n + 2, :].rearrange("p c d -> p (c d)"), work[n % 2][:], ACT.Copy).then_inc(in_read, 1)
                act.wait_ge(g_loaded, 16 * i + 16)
                s.activation(gate[:], gate[:], ACT.Silu).then_inc(silu_ready, 1)
                act.wait_ge(y_summed, i + 1)
                for c in range(NC_):
                    if c:
                        act.wait_ge(squared, NC_ * i + c)
                    s.activation(square[:], y[:, c, :], ACT.Square, accum_out=sums[:, c:c + 1]).then_inc(squared, 1)
                act.wait_ge(root_asked, i + 1)
                s.activation(scratch[1][:], scratch[2][:], ACT.Sqrt).then_inc(root_ready, 1)
                for n in range(4):
                    act.wait_ge(yt_read, 4 * i + 4 + n + 1)
                    s.activation(yg_hi[:, bass.ds(2 * i + n // 2, 1), (n % 2) * HALF:(n % 2 + 1) * HALF].rearrange("p o t -> p (o t)"),
                                 value[:, n % 2, :], ACT.Copy).then_inc(high, 1)

        @block.vector
        def _(dve):
            vv = nc.vector
            chain = Chain(dve, dve_chain)
            dve.wait_ge(made, 1)
            chain.step(vv.tensor_copy(powers[:], power_i[:]))
            chain.step(vv.tensor_copy(delta[:], delta_i[:]))
            chain.step(vv.tensor_scalar(dist[:, 0, :], delta[:], 0.0, None, ALU.max))
            chain.step(vv.tensor_scalar(dist[:, 1, :], delta[:], -1.0, 0.0, ALU.mult, ALU.max))
            chain.step(vv.tensor_scalar(side[:, 0, :], delta[:], 0.0, DK ** -0.5, ALU.is_ge, ALU.mult))
            chain.step(vv.tensor_scalar(side[:, 1, :], delta[:], 0.0, DK ** -0.5, ALU.is_le, ALU.mult))
            dve.wait_ge(tables_loaded, 16)
            dve.wait_ge(decay_loaded, 16)
            setup = chain.taken
            PER_HEAD = 47
            with dve.Fori(0, HEADS, 1) as i:
                start = Chain(dve, dve_chain, setup, PER_HEAD, i)
                start.step(vv.tensor_copy(raw_dec[:], raw_all[:, :, bass.ds(i, 1)].rearrange("p d o -> p (d o)")))
                x, e, u, ln_u, um1, t5 = raw_dec[:], small[1][:], small[2][:], small[3][:], small[4][:], small[5][:]
                start.step(vv.tensor_scalar(small[4][:], x, -1.0, None, ALU.mult))
                start.step(vv.tensor_tensor(small[4][:], x, small[4][:], ALU.max))
                vv.tensor_scalar(small[0][:], small[4][:], -1.0, None, ALU.mult).then_inc(lg_asked, 1)
                dve.wait_ge(lg_exp, 2 * i + 1)
                start.step(vv.tensor_scalar(um1, e, 1.0, None, ALU.add))
                vv.tensor_copy(u, um1).then_inc(lg_asked, 1)
                dve.wait_ge(lg_exp, 2 * i + 2)
                start.step(vv.tensor_scalar(um1, um1, 1.0, None, ALU.subtract))
                start.step(vv.tensor_scalar(t5, um1, 0.0, None, ALU.is_equal))
                start.step(vv.tensor_tensor(um1, um1, t5, ALU.add))
                start.step(vv.tensor_tensor(ln_u, ln_u, t5, ALU.add))
                start.step(vv.reciprocal(um1, um1))
                start.step(vv.tensor_tensor(ln_u, ln_u, e, ALU.mult))
                start.step(vv.tensor_tensor(ln_u, ln_u, um1, ALU.mult))
                start.step(vv.tensor_scalar(t5, x, 0.0, None, ALU.max))
                start.step(vv.tensor_tensor(t5, ln_u, t5, ALU.add))
                vv.tensor_scalar(lg[:], t5, -1.0, None, ALU.mult).then_inc(lg_ready, 1)
                dve.wait_ge(decays, i + 1)
                start.step(vv.tensor_tensor(mask2[:], mask2[:], side[:], ALU.mult))
                start.step(vv.tensor_tensor(mask[:], mask2[:, 0, :], mask2[:, 1, :], ALU.add))
                for col in (1, 3, 4):
                    start.step(vv.tensor_scalar(dec[:, :, col:col + 1], dec[:, :, col:col + 1], DK ** -0.5, None, ALU.mult))
                dve.wait_ge(kc_loaded, 16 * i + 16)
                for d in range(2):
                    for c in range(CT):
                        last = vv.tensor_scalar(kcd[d][:, c, :], kc[:, c, :], dec[:, d, 3 + c:4 + c], None, ALU.mult)
                last.then_inc(kc_scaled, 1)
                dve.wait_ge(q_loaded, 16 * i + 16)
                rotate(vv, start, q, q_raw, cs, tmp_q, q_rotated)
                for n in range(4):
                    dve.wait_ge(kt_done, 4 * i + n + 1)
                    for d in range(2):
                        last = vv.tensor_scalar(kd[d][:, 2 * n:2 * n + 2, :].rearrange("p c d -> p (c d)"), work[n % 2][:],
                                                dec[:, d, 1:2], None, ALU.mult)
                    last.then_inc(kt_read, 1)
                for n in range(2):
                    dve.wait_ge(sc_done, 2 * i + 2 + n + 1)
                    vv.tensor_tensor(weights[:, 4 * n:4 * n + 4, :], work[n % 2][:].rearrange("p (c n) -> p c n", c=4),
                                     mask[:, None, :].to_broadcast([P, 4, CHUNK]), ALU.mult).then_inc(sc_read, 1)
                dve.wait_ge(state_set, i + 1)
                dve.wait_ge(in_read, 4 * i + 4)
                for st in range(NC_):
                    for d in range(2):
                        c = st if d == 0 else NC_ - 1 - st
                        dve.wait_ge(stepped, 16 * i + 16 + 2 * st + d + 1)
                        vv.scalar_tensor_tensor(out=state[d][:], in0=state[d][:], scalar=dec[:, d, 2:3], in1=upd[d][:],
                                                op0=ALU.mult, op1=ALU.add).then_inc(advanced, 1)
                        add = vv.scalar_tensor_tensor(out=y[:, c, :], in0=cross[d][st % 2][:], scalar=dec[:, d, 0:1],
                                                      in1=y[:, c, :], op0=ALU.mult, op1=ALU.add)
                        if (st, d) == (NC_ - 1, 1):
                            add.then_inc(y_summed, 1)
                        else:
                            start.step(add)
                dve.wait_ge(squared, NC_ * i + NC_)

                def act_sqrt(root, mean):
                    vv.tensor_copy(scratch[2][:], mean).then_inc(root_asked, 1)
                    dve.wait_ge(root_ready, i + 1)

                rsqrt_of_mean(nc, start, act_sqrt, rstd[:], sums[:], tuple(x[:] for x in scratch), DK)
                start.step(vv.tensor_tensor(y[:], y[:], rstd[:, :, None].to_broadcast([P, NC_, DK]), ALU.mult))
                dve.wait_ge(silu_ready, i + 1)
                vv.tensor_tensor(y[:], y[:], gate[:], ALU.mult).then_inc(gated, 1)
                for n in range(4):
                    dve.wait_ge(yt_done, 4 * i + n + 1)
                    vv.tensor_copy(value[:, n % 2, :], work[n % 2][:]).then_inc(yt_read, 1)
                    dve.wait_ge(high, 4 * i + n + 1)
                    cols = (bass.ds(2 * i + n // 2, 1), slice((n % 2) * HALF, (n % 2 + 1) * HALF))
                    start.step(vv.tensor_tensor(yg_lo[:, cols[0], cols[1]].rearrange("p o t -> p (o t)"), value[:, n % 2, :],
                                                f32(yg_hi[:, cols[0], cols[1]].rearrange("p o t -> p (o t)")), ALU.subtract))
                assert start.taken == PER_HEAD, start.taken

        @block.tensor
        def _(pe):
            mm_ = nc.tensor.matmul
            pe.sem_inc(ctx_done, 1)
            pe.sem_inc(sc_done, 2)
            pe.sem_inc(stepped, 16)
            pe.sem_inc(gated, 1)
            pe.sem_inc(yt_read, 4)
            with pe.Fori(0, HEADS, 1) as i:
                pe.wait_ge(kc_scaled, i + 1)
                pe.wait_ge(vc_loaded, 16 * i + 16)
                for d in range(2):
                    for j in range(2):
                        for c in range(CT):
                            mm = mm_(upd[d][:, j, :], kcd[d][:, c, j * P:(j + 1) * P], vc[:, c, :],
                                     start=(c == 0), stop=(c == CT - 1))
                mm.then_inc(ctx_done, 1)
                pe.wait_ge(k_rotated, i + 2)
                for n in range(4):
                    if n >= 2:
                        pe.wait_ge(kt_read, 4 * i + n - 1)
                    else:
                        pe.wait_ge(yt_read, 4 * i + 4)
                    for c in range(2):
                        for j in range(2):
                            tr = nc.tensor.transpose(work[n % 2][:, c * DK + j * P:c * DK + (j + 1) * P],
                                                     k[:, j, (2 * n + c) * CHUNK:(2 * n + c + 1) * CHUNK], ident)
                    tr.then_inc(kt_done, 1)
                pe.wait_ge(q_rotated, i + 2)
                for n in range(2):
                    pe.wait_ge(kt_read, 4 * i + n + 3)
                    for c in range(4):
                        cols = slice((4 * n + c) * CHUNK, (4 * n + c + 1) * CHUNK)
                        for j in range(2):
                            mm = mm_(work[n % 2][:, c * CHUNK:(c + 1) * CHUNK], k[:, j, cols], q[:, j, cols],
                                     start=(j == 0), stop=(j == 1))
                    mm.then_inc(sc_done, 1)
                pe.wait_ge(v_loaded, 16 * i + 16)
                for n in range(4):
                    if n < 2:
                        pe.wait_ge(sc_read, 2 * i + n + 1)
                    else:
                        pe.wait_ge(in_read, 4 * i + n - 1)
                    if n == 0:
                        pe.wait_ge(sc_read, 2 * i + 2)
                    for c in range(2):
                        mm = mm_(work[n % 2][:, c * DK:(c + 1) * DK], weights[:, 2 * n + c, :], v[:, 2 * n + c, :],
                                 start=True, stop=True)
                    mm.then_inc(in_done, 1)
                pe.wait_ge(state_set, i + 1)
                for st in range(NC_):
                    for d in range(2):
                        c = st if d == 0 else NC_ - 1 - st
                        if st:
                            pe.wait_ge(advanced, 16 * i + 2 * (st - 1) + d + 1)
                        for j in range(2):
                            mm_(cross[d][st % 2][:], q[:, j, c * CHUNK:(c + 1) * CHUNK], state[d][:, j, :],
                                start=(j == 0), stop=(j == 1))
                        for j in range(2):
                            mm = mm_(upd[d][:, j, :], kd[d][:, c, j * P:(j + 1) * P], v[:, c, :], start=True, stop=True)
                        mm.then_inc(stepped, 1)
                pe.wait_ge(gated, i + 2)
                for n in range(4):
                    if n >= 2:
                        pe.wait_ge(yt_read, 4 * i + 4 + n - 1)
                    for c in range(4):
                        tr = nc.tensor.transpose(work[n % 2][:, c * P:(c + 1) * P],
                                                 y[:, 4 * (n % 2) + c, (n // 2) * P:(n // 2 + 1) * P], ident)
                    tr.then_inc(yt_done, 1)


def project(nc, name, w_blocks, n_blocks, a_hi, a_lo, token_major, gate_rows, result, add):
    with ExitStack() as ctx:
        p = Pool(nc, ctx)
        RING = 4
        GROUPS = 8 * n_blocks
        raw = p.sb(name + "_raw", [P, KT * NB])
        w_hi = [p.sb(f"{name}_w_hi{b}", [P, KT * NB], F32R) for b in range(2)]
        w_lo = [p.sb(f"{name}_w_lo{b}", [P, KT * NB], F32R) for b in range(2)]
        gate = p.sb(name + "_gate", [P, RING, HALF]) if gate_rows is not None else None
        bank = [p.ps(f"{name}_bank{b}", [P, HALF]) for b in range(RING)]
        raw_loaded = p.sem(name + "_raw_loaded")
        hi_ready = p.sem(name + "_hi_ready")
        lo_ready = p.sem(name + "_lo_ready")
        gate_loaded = [p.sem(f"{name}_gate_loaded{r}") for r in range(RING)]
        gate_ready = p.sem(name + "_gate_ready")
        group_done = p.sem(name + "_group_done")
        multiplied = p.sem(name + "_multiplied")
        evacuated = p.sem(name + "_evacuated")
        block = ctx.enter_context(nc.Block())

        def place(g):
            blk, r = g // 8, g % 8
            if token_major:
                return result[:, r, blk * NB:(blk + 1) * NB]
            tile = blk * 4 + r // 2
            return result[:, tile, (r % 2) * HALF:(r % 2 + 1) * HALF]

        @block.sync
        def _(sp):
            sp.dma_start(raw[:], w_blocks[0]).then_inc(raw_loaded, 16)
            for g in range(GROUPS):
                if g % 8 == 4 and g // 8 + 1 < n_blocks:
                    sp.wait_ge(lo_ready, g // 8 + 1)
                    sp.dma_start(raw[:], w_blocks[g // 8 + 1]).then_inc(raw_loaded, 16)
                if gate_rows is not None:
                    if g >= RING:
                        sp.wait_ge(evacuated, g - RING + 1)
                    tile, half = (g // 8) * 4 + g % 8 // 2, g % 2
                    sp.dma_start(gate[:, g % RING, :],
                                 gate_rows[tile * P:(tile + 1) * P, half * HALF:(half + 1) * HALF]).then_inc(gate_loaded[g % RING], 16)

        @block.scalar
        def _(act):
            def high_part(blk):
                act.wait_ge(raw_loaded, 16 * (blk + 1))
                nc.scalar.activation(w_hi[blk % 2][:], raw[:], ACT.Copy).then_inc(hi_ready, 1)

            high_part(0)
            for g in range(GROUPS):
                if g % 8 == 6 and g // 8 + 1 < n_blocks:
                    high_part(g // 8 + 1)
                if gate_rows is not None:
                    act.wait_ge(gate_loaded[g % RING], 16 * (g // RING + 1))
                    nc.scalar.activation(gate[:, g % RING, :], gate[:, g % RING, :], ACT.Sigmoid).then_inc(gate_ready, 1)
                else:
                    act.wait_ge(group_done, g + 1)
                    nc.scalar.activation(place(g), bank[g % RING][:], ACT.Copy).then_inc(evacuated, 1)

        @block.gpsimd
        def _(pool):
            for blk in range(n_blocks):
                pool.wait_ge(hi_ready, blk + 1)
                nc.gpsimd.tensor_tensor(w_lo[blk % 2][:], raw[:], f32(w_hi[blk % 2][:]), ALU.subtract).then_inc(lo_ready, 1)

        @block.vector
        def _(dve):
            if gate_rows is None:
                return
            for g in range(GROUPS):
                dve.wait_ge(group_done, g + 1)
                dve.wait_ge(gate_ready, g + 1)
                if add:
                    nc.vector.tensor_tensor(gate[:, g % RING, :], bank[g % RING][:], gate[:, g % RING, :], ALU.mult).then_inc(multiplied, 1)
                    dve.wait_ge(multiplied, g + 1)
                    nc.vector.tensor_tensor(place(g), place(g), gate[:, g % RING, :], ALU.add).then_inc(evacuated, 1)
                else:
                    nc.vector.tensor_tensor(place(g), bank[g % RING][:], gate[:, g % RING, :], ALU.mult).then_inc(evacuated, 1)

        @block.tensor
        def _(pe):
            for g in range(GROUPS):
                blk, r = g // 8, g % 8
                if r == 0:
                    pe.wait_ge(lo_ready, blk + 1)
                wh = w_hi[blk % 2][:].rearrange("p (k n) -> p k n", k=KT)
                wl = w_lo[blk % 2][:].rearrange("p (k n) -> p k n", k=KT)
                if g >= RING:
                    pe.wait_ge(evacuated, g - RING + 1)
                if token_major:
                    c = slice(r * P, (r + 1) * P)
                    pairs = [((a_hi[:, k, c], a_lo[:, k, c]), (wh[:, k, :], wl[:, k, :])) for k in range(KT)]
                else:
                    n = slice((r // 2) * P, (r // 2 + 1) * P)
                    c = slice((r % 2) * HALF, (r % 2 + 1) * HALF)
                    pairs = [((wh[:, k, n], wl[:, k, n]), (a_hi[:, k, c], a_lo[:, k, c])) for k in range(KT)]
                split_matmuls(nc, bank[g % RING][:], pairs).then_inc(group_done, 1)


def split_tile(nc, name, x, hi, lo):
    with ExitStack() as ctx:
        p = Pool(nc, ctx)
        high = p.sem(name + "_high")
        low = p.sem(name + "_low")
        block = ctx.enter_context(nc.Block())

        @block.scalar
        def _(act):
            for k in range(KT):
                nc.scalar.activation(hi[:, k, :], x[:, k, :], ACT.Copy).then_inc(high, 1)

        @block.vector
        def _(dve):
            for k in range(KT):
                dve.wait_ge(high, k + 1)
                nc.vector.tensor_tensor(lo[:, k, :], x[:, k, :], f32(hi[:, k, :]), ALU.subtract)


def conv_norm(nc, conv, gain_cols, bias_cols, u_hi, u_lo, ones):
    with ExitStack() as ctx:
        p = Pool(nc, ctx)
        x = p.sb("cn_x", [P, KT, SEQ])
        square = p.sb("cn_square", [P, 2, SEQ])
        var = p.sb("cn_var", [P, SEQ])
        root = p.sb("cn_root", [P, SEQ])
        rstd = p.sb("cn_rstd", [P, SEQ])
        gain = p.sb("cn_gain", [P, KT])
        bias = p.sb("cn_bias", [P, KT])
        mean_bank = [p.ps(f"cn_mean{h}", [P, HALF]) for h in range(2)]
        var_bank = [p.ps(f"cn_var_bank{h}", [P, HALF]) for h in range(2)]
        loaded = [p.sem(f"cn_loaded{k}") for k in range(KT)]
        cols_loaded = p.sem("cn_cols_loaded")
        mean_done = p.sem("cn_mean_done")
        centred = p.sem("cn_centred")
        squared = p.sem("cn_squared")
        var_done = p.sem("cn_var_done")
        square_read = p.sem("cn_square_read")
        root_asked = p.sem("cn_root_asked")
        root_ready = p.sem("cn_root_ready")
        chained = p.sem("cn_chained")
        scaled = p.sem("cn_scaled")
        silued = p.sem("cn_silued")
        high = p.sem("cn_high")
        block = ctx.enter_context(nc.Block())

        @block.sync
        def _(sp):
            for k in range(KT):
                sp.dma_start(x[:, k, :], conv[k * P:(k + 1) * P, :]).then_inc(loaded[k], 16)
            sp.dma_start(gain[:], gain_cols).then_inc(cols_loaded, 16)
            sp.dma_start(bias[:], bias_cols).then_inc(cols_loaded, 16)

        @block.tensor
        def _(pe):
            for k in range(KT):
                pe.wait_ge(loaded[k], 16)
                for h in range(2):
                    mm = nc.tensor.matmul(mean_bank[h][:], ones, x[:, k, h * HALF:(h + 1) * HALF],
                                          start=(k == 0), stop=(k == KT - 1))
            mm.then_inc(mean_done, 1)
            for k in range(KT):
                pe.wait_ge(squared, k + 1)
                for h in range(2):
                    mm = nc.tensor.matmul(var_bank[h][:], ones, square[:, k % 2, h * HALF:(h + 1) * HALF],
                                          start=(k == 0), stop=(k == KT - 1))
                mm.then_inc(square_read, 1)

        @block.vector
        def _(dve):
            v = nc.vector
            dve.wait_ge(mean_done, 1)
            for k in range(KT):
                for h in range(2):
                    cols = slice(h * HALF, (h + 1) * HALF)
                    v.scalar_tensor_tensor(out=x[:, k, cols], in0=mean_bank[h][:], scalar=-1.0 / D, in1=x[:, k, cols],
                                           op0=ALU.mult, op1=ALU.add).then_inc(centred, 1)
            dve.wait_ge(square_read, KT)
            chain = Chain(dve, chained)
            for h in range(2):
                chain.step(v.tensor_scalar(var[:, h * HALF:(h + 1) * HALF], var_bank[h][:], 1.0 / D, EPS, ALU.mult, ALU.add))
            v.tensor_copy(rstd[:, 0:1], var[:, 0:1]).then_inc(root_asked, 1)
            dve.wait_ge(root_ready, 1)
            chain.step(v.reciprocal(rstd[:], root[:]))
            chain.step(v.tensor_tensor(root[:], rstd[:], rstd[:], ALU.mult))
            chain.step(v.tensor_tensor(root[:], root[:], var[:], ALU.mult))
            chain.step(v.tensor_scalar(root[:], root[:], -0.5, 1.5, ALU.mult, ALU.add))
            chain.step(v.tensor_tensor(rstd[:], rstd[:], root[:], ALU.mult))
            for k in range(KT):
                v.tensor_tensor(x[:, k, :], x[:, k, :], rstd[:], ALU.mult).then_inc(scaled, 1)

        @block.gpsimd
        def _(pool):
            for k in range(KT):
                pool.wait_ge(high, k + 1)
                nc.gpsimd.tensor_tensor(u_lo[:, k, :], x[:, k, :], f32(u_hi[:, k, :]), ALU.subtract)

        @block.scalar
        def _(act):
            s = nc.scalar
            for k in range(KT):
                act.wait_ge(centred, 2 * (k + 1))
                if k >= 2:
                    act.wait_ge(square_read, k - 1)
                s.activation(square[:, k % 2, :], x[:, k, :], ACT.Square).then_inc(squared, 1)
            act.wait_ge(root_asked, 1)
            s.activation(root[:], var[:], ACT.Sqrt).then_inc(root_ready, 1)
            act.wait_ge(cols_loaded, 32)
            for k in range(KT):
                act.wait_ge(scaled, k + 1)
                s.activation(x[:, k, :], x[:, k, :], ACT.Silu, bias=bias[:, k:k + 1], scale=gain[:, k:k + 1]).then_inc(silued, 1)
                act.wait_ge(silued, k + 1)
                s.activation(u_hi[:, k, :], x[:, k, :], ACT.Copy).then_inc(high, 1)


def residual(nc, name, y, base_dram, row, out_dram):
    with ExitStack() as ctx:
        p = Pool(nc, ctx)
        base = p.sb(name + "_base", [P, TT, D])
        square = p.sb(name + "_square", [P, D])
        sums = p.sb(name + "_sums", [P, TT])
        rstd = p.sb(name + "_rstd", [P, TT])
        scratch = [p.sb(f"{name}_scratch{n}", [P, TT]) for n in range(3)]
        loaded = p.sem(name + "_loaded")
        summed = p.sem(name + "_summed")
        root_asked = p.sem(name + "_root_asked")
        root_ready = p.sem(name + "_root_ready")
        chained = p.sem(name + "_chained")
        weighted = p.sem(name + "_weighted")
        added = p.sem(name + "_added")
        stored = p.sem(name + "_stored")
        block = ctx.enter_context(nc.Block())
        view = lambda dram: dram.rearrange("(t p) d -> p t d", p=P)

        @block.sync
        def _(sp):
            sp.dma_start(base[:], view(base_dram)).then_inc(loaded, 16)
            for t in range(TT):
                sp.wait_ge(added, t + 1)
                sp.dma_start(view(out_dram)[:, t, :], y[:, t, :]).then_inc(stored, 16)
            sp.wait_ge(stored, 16 * TT)

        @block.scalar
        def _(act):
            for t in range(TT):
                if t:
                    act.wait_ge(summed, t)
                nc.scalar.activation(square[:], y[:, t, :], ACT.Square, accum_out=sums[:, t:t + 1]).then_inc(summed, 1)
            act.wait_ge(root_asked, 1)
            nc.scalar.activation(scratch[1][:], scratch[2][:], ACT.Sqrt).then_inc(root_ready, 1)

        @block.vector
        def _(dve):
            v = nc.vector
            dve.wait_ge(summed, TT)
            chain = Chain(dve, chained)

            def act_sqrt(root, mean):
                v.tensor_copy(scratch[2][:], mean).then_inc(root_asked, 1)
                dve.wait_ge(root_ready, 1)

            rsqrt_of_mean(nc, chain, act_sqrt, rstd[:], sums[:], tuple(x[:] for x in scratch), D)
            dve.wait_ge(loaded, 16)
            for t in range(TT):
                v.scalar_tensor_tensor(out=y[:, t, :], in0=y[:, t, :], scalar=rstd[:, t:t + 1], in1=row,
                                       op0=ALU.mult, op1=ALU.mult).then_inc(weighted, 1)
                dve.wait_ge(weighted, t + 1)
                v.tensor_tensor(y[:, t, :], y[:, t, :], base[:, t, :], ALU.add).then_inc(added, 1)

PEER_HEADS = 8
N_KEYS = 128
TOPK = 16
SIDES = 2 * PEER_HEADS
CAND = TOPK * TOPK
NEG = -3.0e38


def query_scores(nc, wq_blocks, keys, h_hi, h_lo, scores):
    with ExitStack() as ctx:
        p = Pool(nc, ctx)
        RING = 4
        BLKS = 4
        raw = p.sb("qs_raw", [P, KT * NB])
        w_hi = [p.sb(f"qs_w_hi{b}", [P, KT * NB], F32R) for b in range(2)]
        w_lo = [p.sb(f"qs_w_lo{b}", [P, KT * NB], F32R) for b in range(2)]
        key = p.sb("qs_key", [P, SIDES, N_KEYS])
        q = p.sb("qs_q", [P, RING, HALF])
        stage = p.sb("qs_stage", [P, RING, 4, N_KEYS])
        q_bank = [p.ps(f"qs_q_bank{b}", [P, HALF]) for b in range(RING)]
        s_bank = [p.ps(f"qs_s_bank{b}", [P, 4, N_KEYS]) for b in range(RING)]
        keys_loaded = p.sem("qs_keys_loaded")
        raw_loaded = p.sem("qs_raw_loaded")
        hi_ready = p.sem("qs_hi_ready")
        lo_ready = p.sem("qs_lo_ready")
        q_done, q_read = p.sem("qs_q_done"), p.sem("qs_q_read")
        s_done, s_read = p.sem("qs_s_done"), p.sem("qs_s_read")
        stored = [p.sem(f"qs_stored{r}") for r in range(RING)]
        block = ctx.enter_context(nc.Block())

        @block.sync
        def _(sp):
            sp.dma_start(raw[:], wq_blocks[0]).then_inc(raw_loaded, 16)
            sp.dma_start(key[:], keys).then_inc(keys_loaded, 16)
            for g in range(8 * BLKS):
                if g % 8 == 0 and g // 8 + 1 < BLKS:
                    sp.wait_ge(lo_ready, g // 8 + 1)
                    sp.dma_start(raw[:], wq_blocks[g // 8 + 1]).then_inc(raw_loaded, 16)
                side, half = g // 2, g % 2
                sp.wait_ge(s_read, g + 1)
                dst = scores.rearrange("(t p) (s n) -> s p t n", p=P, n=N_KEYS)[side, :, half * 4:half * 4 + 4, :]
                sp.dma_start(dst, stage[:, g % RING, :, :]).then_inc(stored[g % RING], 16)
            for r in range(RING):
                sp.wait_ge(stored[r], 16 * (8 * BLKS // RING))

        @block.scalar
        def _(act):
            def high_part(blk):
                act.wait_ge(raw_loaded, 16 * (blk + 1))
                nc.scalar.activation(w_hi[blk % 2][:], raw[:], ACT.Copy).then_inc(hi_ready, 1)

            high_part(0)
            for g in range(8 * BLKS):
                if g % 8 == 2 and g // 8 + 1 < BLKS:
                    high_part(g // 8 + 1)
                act.wait_ge(q_done, g + 1)
                if g >= RING:
                    act.wait_ge(s_done, g - RING + 1)
                nc.scalar.activation(q[:, g % RING, :], q_bank[g % RING][:], ACT.Copy).then_inc(q_read, 1)

        @block.gpsimd
        def _(pool):
            for blk in range(BLKS):
                pool.wait_ge(hi_ready, blk + 1)
                nc.gpsimd.tensor_tensor(w_lo[blk % 2][:], raw[:], f32(w_hi[blk % 2][:]), ALU.subtract).then_inc(lo_ready, 1)

        @block.vector
        def _(dve):
            for g in range(8 * BLKS):
                dve.wait_ge(s_done, g + 1)
                if g >= RING:
                    dve.wait_ge(stored[g % RING], 16 * (g // RING))
                nc.vector.tensor_copy(stage[:, g % RING, :, :], s_bank[g % RING][:]).then_inc(s_read, 1)

        @block.tensor
        def _(pe):
            def score(g):
                side = g // 2
                pe.wait_ge(q_read, g + 1)
                if g >= RING:
                    pe.wait_ge(s_read, g - RING + 1)
                for t in range(4):
                    mm = nc.tensor.matmul(s_bank[g % RING][:, t, :], q[:, g % RING, t * P:(t + 1) * P], key[:, side, :],
                                          start=True, stop=True)
                mm.then_inc(s_done, 1)

            pe.wait_ge(keys_loaded, 16)
            for g in range(8 * BLKS):
                blk, r = g // 8, g % 8
                if r == 0:
                    pe.wait_ge(lo_ready, blk + 1)
                wh = w_hi[blk % 2][:].rearrange("p (k n) -> p k n", k=KT)
                wl = w_lo[blk % 2][:].rearrange("p (k n) -> p k n", k=KT)
                if g >= RING:
                    pe.wait_ge(q_read, g - RING + 1)
                n = slice((r // 2) * P, (r // 2 + 1) * P)
                c = slice((r % 2) * HALF, (r % 2 + 1) * HALF)
                split_matmuls(nc, q_bank[g % RING][:], [((wh[:, k, n], wl[:, k, n]), (h_hi[:, k, c], h_lo[:, k, c]))
                                                        for k in range(KT)]).then_inc(q_done, 1)
                if g:
                    score(g - 1)
            score(8 * BLKS - 1)

SPAN = 64
SLABS = SEQ // SPAN
EARLY_BESIDE_TOP = 40
EARLY_BESIDE_GATES = 32
EARLY = EARLY_BESIDE_TOP + EARLY_BESIDE_GATES
GELU = ACT.Gelu_apprx_tanh


class EarlyProducts:

    def __init__(self, nc, p, name, u_tiles, h, acts, first_tile, tiles, per_turn):
        self.nc, self.u_tiles, self.h, self.acts = nc, u_tiles, h, acts
        self.first_tile, self.tiles, self.per_turn = first_tile, tiles, per_turn
        self.u_raw = p.sb(name + "_u_raw", [P, KT, P])
        self.u_hi = [p.sb(f"{name}_u_hi{b}", [P, KT, P], F32R) for b in range(2)]
        self.u_lo = [p.sb(f"{name}_u_lo{b}", [P, KT, P], F32R) for b in range(2)]
        self.value = [p.sb(f"{name}_value{b}", [P, SEQ]) for b in range(2)]
        self.bank = [p.ps(f"{name}_bank{b}", [P, HALF]) for b in range(4)]
        self.u_loaded = p.sem(name + "_u_loaded")
        self.u_hi_ready = p.sem(name + "_u_hi_ready")
        self.u_lo_ready = p.sem(name + "_u_lo_ready")
        self.u_done = p.sem(name + "_u_done")
        self.gelu_done = p.sem(name + "_gelu_done")
        self.stored = [p.sem(f"{name}_stored{b}") for b in range(2)]

    def credit(self, sp):
        sp.sem_inc(self.u_lo_ready, 1)
        sp.sem_inc(self.u_done, 4)
        sp.sem_inc(self.gelu_done, 4)
        for b in range(2):
            sp.sem_inc(self.stored[b], 16)

    def tile(self, dram, n, i):
        at = i * self.per_turn + (self.first_tile + n)
        return dram[at:at + 1] if isinstance(i, int) else dram[bass.ds(at, 1)]

    def load_u(self, sp, n, i=0):
        sp.wait_ge(self.u_lo_ready, self.per_turn * i + n + 1)
        src = self.tile(self.u_tiles, n, i).rearrange("o p (k n) -> (o p) k n", k=KT)
        sp.dma_start(self.u_raw[:], src).then_inc(self.u_loaded, 16)

    def store(self, sp, n, i=0):
        sp.wait_ge(self.gelu_done, 2 * self.per_turn * i + 2 * n + 2 + 4)
        dst = self.tile(self.acts, n, i).rearrange("o p t -> (o p) t")
        sp.dma_start(dst, self.value[n % 2][:]).then_inc(self.stored[n % 2], 16)

    def last_stores(self, sp):
        for b in range(2):
            sp.wait_ge(self.stored[b], 16 * (self.tiles // 2 + 1))

    def high_u(self, act, n, i=0):
        act.wait_ge(self.u_loaded, 16 * self.per_turn * i + 16 * (n + 1))
        act.wait_ge(self.u_done, 2 * self.per_turn * i + 2 * n + 2)
        self.nc.scalar.activation(self.u_hi[n % 2][:], self.u_raw[:], ACT.Copy).then_inc(self.u_hi_ready, 1)

    def low_u(self, pool, n, i=0):
        pool.wait_ge(self.u_hi_ready, self.per_turn * i + n + 1)
        self.nc.gpsimd.tensor_tensor(self.u_lo[n % 2][:], self.u_raw[:], f32(self.u_hi[n % 2][:]),
                                     ALU.subtract).then_inc(self.u_lo_ready, 1)

    def product(self, pe, g, k, i=0):
        n, half, cols = g // 2, g % 2, slice((g % 2) * HALF, (g % 2 + 1) * HALF)
        if k == 0:
            pe.wait_ge(self.u_lo_ready, self.per_turn * i + n + 2)
            pe.wait_ge(self.gelu_done, 2 * self.per_turn * i + g + 1)
        mm, bank, (h_hi, h_lo) = self.nc.tensor.matmul, self.bank[g % 4], self.h
        mm(bank[:], self.u_hi[n % 2][:, k, :], h_hi[:, k, cols], start=(k == 0), stop=False)
        mm(bank[:], self.u_hi[n % 2][:, k, :], h_lo[:, k, cols], start=False, stop=False)
        last = mm(bank[:], self.u_lo[n % 2][:, k, :], h_hi[:, k, cols], start=False, stop=(k == KT - 1))
        if k == KT - 1:
            last.then_inc(self.u_done, 1)

    def gelu(self, act, g, i=0):
        n, half = g // 2, g % 2
        act.wait_ge(self.u_done, 2 * self.per_turn * i + g + 1 + 4)
        if half == 0:
            act.wait_ge(self.stored[n % 2], 8 * self.per_turn * i + 16 * (n // 2 + 1))
        self.nc.scalar.activation(self.value[n % 2][:, half * HALF:(half + 1) * HALF], self.bank[g % 4][:],
                                  GELU).then_inc(self.gelu_done, 1)


def top_experts(nc, scores, first_T, second_T, gate_T, ident, u_tiles, h, acts):
    PER_TOKENS = EARLY_BESIDE_TOP // TT
    BODY = 2 * PER_TOKENS
    BODIES = TT // 2
    with ExitStack() as ctx:
        p = Pool(nc, ctx)
        s = p.sb("te_s", [P, SIDES, N_KEYS])
        s2 = p.sb("te_s2", [P, SIDES, N_KEYS])
        top = p.sb("te_top", [P, SIDES, TOPK])
        top_i = p.sb("te_top_i", [P, SIDES, TOPK], U32)
        top_f = p.sb("te_top_f", [P, SIDES, TOPK])
        cand = p.sb("te_cand", [P, PEER_HEADS, CAND])
        cand2 = p.sb("te_cand2", [P, PEER_HEADS, CAND])
        best = p.sb("te_best", [P, PEER_HEADS, TOPK])
        sel = p.sb("te_sel", [P, PEER_HEADS * TOPK], U32)
        part_i = p.sb("te_part_i", [P, 2, PEER_HEADS * TOPK], U32)
        part = p.sb("te_part", [P, 2, PEER_HEADS * TOPK])
        hit = [p.sb(f"te_hit{d}", [P, PEER_HEADS * TOPK, TOPK]) for d in range(2)]
        found = p.sb("te_found", [P, 3, PEER_HEADS * TOPK])
        shifted = p.sb("te_shifted", [P, PEER_HEADS, TOPK])
        sums = p.sb("te_sums", [P, PEER_HEADS])
        ranks_i = p.sb("te_ranks_i", [P, TOPK], I32)
        ranks = p.sb("te_ranks", [P, TOPK])
        pad = p.sb("te_pad", [P, 1])
        bank = p.ps("te_bank", [P, 3, P])
        loaded = p.sem("te_loaded")
        made = p.sem("te_made")
        chain_sem = p.sem("te_chain")
        keys_taken = p.sem("te_keys_taken")
        exp_asked = p.sem("te_exp_asked")
        exp_ready = p.sem("te_exp_ready")
        parted = p.sem("te_parted")
        compared = p.sem("te_compared")
        second_hit = p.sem("te_second_hit")
        found_ready = p.sem("te_found_ready")
        turned = p.sem("te_turned")
        kept = p.sem("te_kept")
        early = EarlyProducts(nc, p, "te_early", u_tiles, h, acts, 0, EARLY_BESIDE_TOP, BODY)
        block = ctx.enter_context(nc.Block())

        def walk(eng, body):
            with eng.Fori(0, BODIES - 1, 1) as i:
                body(i, True)
            body(BODIES - 1, False)

        @block.sync
        def _(sp):
            early.credit(sp)
            s_rows = s[:].rearrange("p s n -> p (s n)")
            sp.dma_start(s_rows, scores[0:P, :]).then_inc(loaded, 16)
            early.load_u(sp, 0)
            early.load_u(sp, 1)

            def body(i, more):
                rows = []
                for t in range(2):
                    at = i * (2 * P) + (t + 1) * P
                    rows.append(slice(at, at + P) if isinstance(i, int) else bass.ds(sp.snap(at), P))
                for n in range(BODY):
                    if more or n + 2 < BODY:
                        early.load_u(sp, n + 2, i)
                    early.store(sp, n, i)
                    t = n // PER_TOKENS
                    if n % PER_TOKENS == 2 and (more or t == 0):
                        sp.wait_ge(keys_taken, 2 * i + t + 1)
                        sp.dma_start(s_rows, scores[rows[t], :]).then_inc(loaded, 16)

            walk(sp, body)
            early.last_stores(sp)

        def compare(side):
            pt = part[:, side, :]
            return nc.vector.tensor_tensor(hit[side][:], pt[:, :, None].to_broadcast([P, PEER_HEADS * TOPK, TOPK]),
                                           ranks[:, None, :].to_broadcast([P, PEER_HEADS * TOPK, TOPK]), ALU.is_equal)

        def weigh(engine, side):
            idx = top_f[:].rearrange("p (h e) k -> p h e k", e=2)[:, :, side, :]
            view = hit[side][:].rearrange("p (h k) a -> p h k a", h=PEER_HEADS)
            return engine.tensor_tensor(view, view, idx[:, :, None, :].to_broadcast([P, PEER_HEADS, TOPK, TOPK]), ALU.mult)

        @block.gpsimd
        def _(pool):
            nc.gpsimd.iota(ranks_i[:], pattern=[[1, TOPK]], base=0, channel_multiplier=0).then_inc(made, 1)
            pool.wait_ge(made, 1)
            nc.gpsimd.tensor_copy(ranks[:], ranks_i[:]).then_inc(made, 1)
            pool.wait_ge(made, 2)
            early.low_u(pool, 0)
            early.low_u(pool, 1)

            def body(i, more):
                for n in range(BODY):
                    if more or n + 2 < BODY:
                        early.low_u(pool, n + 2, i)
                    if n % PER_TOKENS == 3:
                        pool.wait_ge(compared, 2 * i + n // PER_TOKENS + 1)
                        weigh(nc.gpsimd, 1).then_inc(second_hit, 1)

            walk(pool, body)

        @block.scalar
        def _(act):
            act.sem_inc(kept, 1)
            early.high_u(act, 0)
            early.high_u(act, 1)

            def body(i, more):
                for n in range(BODY):
                    t = n // PER_TOKENS
                    early.gelu(act, 2 * n, i)
                    early.gelu(act, 2 * n + 1, i)
                    if more or n + 2 < BODY:
                        early.high_u(act, n + 2, i)
                    if n % PER_TOKENS == 3:
                        act.wait_ge(exp_asked, 2 * i + t + 1)
                        nc.scalar.activation(shifted[:], shifted[:], ACT.Exp).then_inc(exp_ready, 1)
                    if n % PER_TOKENS == 4:
                        act.wait_ge(turned, 2 * i + t + 1)
                        for m, dst in enumerate((first_T, second_T, gate_T)):
                            at = i * (2 * P) + t * P
                            cols = slice(at, at + P) if isinstance(i, int) else bass.ds(at, P)
                            copied = nc.scalar.activation(dst[:, cols], bank[:, m, :], ACT.Copy)
                        copied.then_inc(kept, 1)

            walk(act, body)

        @block.tensor
        def _(pe):
            with pe.Fori(0, BODIES, 1) as i:
                for n in range(BODY):
                    for half in range(2):
                        for k in range(KT):
                            early.product(pe, 2 * n + half, k, i)
                    if n % PER_TOKENS == PER_TOKENS - 1:
                        t = n // PER_TOKENS
                        pe.wait_ge(found_ready, 2 * i + t + 1)
                        pe.wait_ge(kept, 2 * i + t + 1)
                        for m in range(3):
                            tr = nc.tensor.transpose(bank[:, m, :], found[:, m, :], ident)
                        tr.then_inc(turned, 1)

        @block.vector
        def _(dve):
            v = nc.vector
            STEPS = 13
            dve.wait_ge(made, 2)

            def take_wait():
                v.memset(pad[:], 0.0)

            with dve.Fori(0, TT, 1) as i:
                chain = Chain(dve, chain_sem, 0, STEPS, i)
                dve.wait_ge(loaded, 16 * i + 16)
                take_wait()
                for c in range(SIDES):
                    last = v.max(top[:, c, 0:8], s[:, c, :])
                chain.step(last)
                take_wait()
                for c in range(SIDES):
                    last = v.match_replace(s2[:, c, :], top[:, c, 0:8], s[:, c, :], NEG)
                chain.step(last)
                take_wait()
                for c in range(SIDES):
                    last = v.max(top[:, c, 8:16], s2[:, c, :])
                chain.step(last)
                take_wait()
                for c in range(SIDES):
                    v.max_index(top_i[:, c, 8:16], top[:, c, 8:16], s2[:, c, :])
                    last = v.max_index(top_i[:, c, 0:8], top[:, c, 0:8], s[:, c, :])
                last.then_inc(keys_taken, 1)
                dve.wait_ge(keys_taken, i + 1)
                v.tensor_copy(top_f[:], top_i[:])
                pairs = top[:].rearrange("p (h e) k -> p h e k", e=2)
                chain.step(v.tensor_tensor(cand[:].rearrange("p h (a b) -> p h a b", a=TOPK),
                                           pairs[:, :, 0, :, None].to_broadcast([P, PEER_HEADS, TOPK, TOPK]),
                                           pairs[:, :, 1, None, :].to_broadcast([P, PEER_HEADS, TOPK, TOPK]), ALU.add))
                take_wait()
                for h in range(PEER_HEADS):
                    last = v.max(best[:, h, 0:8], cand[:, h, :])
                chain.step(last)
                take_wait()
                for h in range(PEER_HEADS):
                    last = v.match_replace(cand2[:, h, :], best[:, h, 0:8], cand[:, h, :], NEG)
                chain.step(last)
                take_wait()
                for h in range(PEER_HEADS):
                    last = v.max(best[:, h, 8:16], cand2[:, h, :])
                chain.step(last)
                v.tensor_tensor(shifted[:], best[:], best[:, :, 0:1].to_broadcast([P, PEER_HEADS, TOPK]),
                                ALU.subtract).then_inc(exp_asked, 1)
                for h in range(PEER_HEADS):
                    v.max_index(sel[:, h * TOPK + 8:h * TOPK + 16], best[:, h, 8:16], cand2[:, h, :])
                    last = v.max_index(sel[:, h * TOPK:h * TOPK + 8], best[:, h, 0:8], cand[:, h, :])
                chain.step(last)
                v.tensor_scalar(part_i[:, 0, :], sel[:], 4, None, ALU.logical_shift_right)
                chain.step(v.tensor_scalar(part_i[:, 1, :], sel[:], TOPK - 1, None, ALU.bitwise_and))
                v.tensor_copy(part[:], part_i[:]).then_inc(parted, 1)
                dve.wait_ge(parted, i + 1)
                compare(1).then_inc(compared, 1)
                chain.step(compare(0))
                chain.step(weigh(v, 0))
                dve.wait_ge(kept, i + 1)
                v.tensor_reduce(found[:, 0, :], hit[0][:], AX.X, ALU.add)
                dve.wait_ge(second_hit, i + 1)
                v.tensor_reduce(found[:, 1, :], hit[1][:], AX.X, ALU.add)
                dve.wait_ge(exp_ready, i + 1)
                chain.step(v.tensor_reduce(sums[:], shifted[:], AX.X, ALU.add))
                chain.step(v.reciprocal(sums[:], sums[:]))
                v.tensor_tensor(found[:, 2, :].rearrange("p (h k) -> p h k", h=PEER_HEADS), shifted[:],
                                sums[:, :, None].to_broadcast([P, PEER_HEADS, TOPK]), ALU.mult).then_inc(found_ready, 1)
                assert chain.taken == STEPS, chain.taken


def gate_matrix(nc, first_T, second_T, gate_T, g_dram, u_tiles, h, acts):
    TURN = 8
    QUAD = 4
    QUADS = TURN // QUAD
    PER_SLAB = SPAN // QUAD
    BODY = 2 * SPAN // TURN
    BODIES = SLABS // 2
    TILES = EARLY_BESIDE_GATES // BODIES
    UNITS = 2 * KT * TILES

    def turn_of(unit):
        return unit * (BODY - 2) // UNITS
    with ExitStack() as ctx:
        p = Pool(nc, ctx)
        iota_i = p.sb("gm_iota_i", [P, P], I32)
        iota = p.sb("gm_iota", [P, P])
        weight_hi = p.sb("gm_weight_hi", [P, SEQ], F32R)
        weight_lo = gate_T
        hot_i = [p.sb(f"gm_hot_i{b}", [P, TURN, P], BF16) for b in range(2)]
        hot_j = [p.sb(f"gm_hot_j{b}", [P, TURN, P], F32R) for b in range(2)]
        hot_hi = [p.sb(f"gm_hot_hi{b}", [P, TURN, P], F32R) for b in range(2)]
        hot_lo = [p.sb(f"gm_hot_lo{b}", [P, TURN, P], F32R) for b in range(2)]
        slab = [p.sb(f"gm_slab{b}", [P, P, SPAN]) for b in range(2)]
        bank = [p.ps(f"gm_bank{b}", [P, QUAD, P]) for b in range(4)]
        made = p.sem("gm_made")
        weights_ready = p.sem("gm_weights_ready")
        i_ready = p.sem("gm_i_ready")
        hi_ready = p.sem("gm_hi_ready")
        lo_ready = p.sem("gm_lo_ready")
        quad_done = p.sem("gm_quad_done")
        quad_read = p.sem("gm_quad_read")
        stored = [p.sem(f"gm_stored{b}") for b in range(2)]
        early = EarlyProducts(nc, p, "gm_early", u_tiles, h, acts, EARLY_BESIDE_TOP, EARLY_BESIDE_GATES, TILES)
        block = ctx.enter_context(nc.Block())

        def walk(eng, body):
            with eng.Fori(0, BODIES - 1, 1) as i:
                body(i, True)
            body(BODIES - 1, False)

        def rows_of(x, t0):
            return x[:, bass.ds(t0, TURN)][:, :, None].to_broadcast([P, TURN, P])

        iota_rows = iota[:, None, :].to_broadcast([P, TURN, P])

        @block.sync
        def _(sp):
            early.credit(sp)
            early.load_u(sp, 0)
            early.load_u(sp, 1)

            def body(i, more):
                for b in range(2):
                    for n in range(b * TILES // 2, (b + 1) * TILES // 2):
                        if more or n + 2 < TILES:
                            early.load_u(sp, n + 2, i)
                        early.store(sp, n, i)
                    sp.wait_ge(quad_read, 2 * PER_SLAB * i + (b + 1) * PER_SLAB + 4)
                    at = i * 2 + b
                    dst = g_dram[at:at + 1] if isinstance(i, int) else g_dram[bass.ds(at, 1)]
                    sp.dma_start(dst.rearrange("s j i t -> (s j) i t"), slab[b][:]).then_inc(stored[b], 16)

            walk(sp, body)
            early.last_stores(sp)
            for b in range(2):
                sp.wait_ge(stored[b], 16 * (BODIES + 1))

        @block.gpsimd
        def _(pool):
            pool.sem_inc(lo_ready, 2)
            nc.gpsimd.iota(iota_i[:], pattern=[[1, P]], base=0, channel_multiplier=0).then_inc(made, 1)
            pool.wait_ge(made, 1)
            nc.gpsimd.tensor_copy(iota[:], iota_i[:]).then_inc(made, 1)
            early.low_u(pool, 0)
            early.low_u(pool, 1)
            pool.wait_ge(weights_ready, 2)
            ends = [turn_of(2 * KT * (n + 1) - 1) for n in range(TILES)]

            def body(i, more):
                for turn in range(BODY):
                    b = turn % 2
                    pool.wait_ge(i_ready, BODY * i + turn + 1)
                    pool.wait_ge(quad_done, QUADS * BODY * i + QUADS * (turn + 1))
                    nc.gpsimd.tensor_tensor(hot_lo[b][:], hot_i[b][:], rows_of(weight_lo, i * (BODY * TURN) + turn * TURN),
                                            ALU.mult).then_inc(lo_ready, 1)
                    if turn - 2 in ends and (more or ends.index(turn - 2) + 2 < TILES):
                        early.low_u(pool, ends.index(turn - 2) + 2, i)

            walk(pool, body)

        @block.vector
        def _(dve):
            v = nc.vector
            dve.wait_ge(made, 2)
            dve.wait_ge(weights_ready, 1)
            v.tensor_tensor(weight_lo[:], weight_lo[:], f32(weight_hi[:]), ALU.subtract).then_inc(weights_ready, 1)
            dve.wait_ge(weights_ready, 2)
            with dve.Fori(0, SEQ // (2 * TURN), 1) as i:
                for b in range(2):
                    t0 = i * 2 * TURN + b * TURN
                    dve.wait_ge(lo_ready, 2 * i + b + 1)
                    v.tensor_tensor(hot_i[b][:], rows_of(first_T, t0), iota_rows, ALU.is_equal).then_inc(i_ready, 1)
                    dve.wait_ge(quad_done, QUADS * 2 * i + QUADS * (b + 1))
                    v.tensor_tensor(hot_j[b][:], rows_of(second_T, t0), iota_rows, ALU.is_equal)
                    dve.wait_ge(i_ready, 2 * i + b + 1)
                    v.tensor_tensor(hot_hi[b][:], hot_i[b][:], rows_of(f32(weight_hi[:]), t0), ALU.mult).then_inc(hi_ready, 1)

        @block.scalar
        def _(act):
            for b in range(2):
                act.sem_inc(stored[b], 16)
            act.sem_inc(quad_read, 4)
            nc.scalar.activation(weight_hi[:], gate_T[:], ACT.Copy).then_inc(weights_ready, 1)
            early.high_u(act, 0)
            early.high_u(act, 1)

            def body(i, more):
                unit = 0
                for turn in range(BODY):
                    b = 2 * turn // BODY
                    if turn % (BODY // 2) == 0:
                        act.wait_ge(stored[b], 16 * i + 16)
                    for q in range(turn * QUADS, (turn + 1) * QUADS):
                        n = q % PER_SLAB
                        act.wait_ge(quad_done, 2 * PER_SLAB * i + q + 1 + 2 * QUADS)
                        nc.scalar.activation(slab[b][:, :, n * QUAD:(n + 1) * QUAD].rearrange("p i t -> p t i"),
                                             bank[q % 4][:], ACT.Copy).then_inc(quad_read, 1)
                    while unit < UNITS and turn_of(unit) == turn:
                        unit += 1
                        if unit % KT == 0:
                            early.gelu(act, unit // KT - 1, i)
                        if unit % (2 * KT) == 0 and (more or unit // (2 * KT) + 1 < TILES):
                            early.high_u(act, unit // (2 * KT) + 1, i)

            walk(act, body)

        @block.tensor
        def _(pe):
            pe.sem_inc(quad_done, 2 * QUADS)
            with pe.Fori(0, BODIES, 1) as i:
                unit = 0
                for turn in range(BODY):
                    b = turn % 2
                    pe.wait_ge(hi_ready, BODY * i + turn + 1)
                    pe.wait_ge(lo_ready, BODY * i + turn + 1 + 2)
                    for n in range(QUADS):
                        q = turn * QUADS + n
                        pe.wait_ge(quad_read, i * (BODY * QUADS) + q + 1)
                        for c in range(QUAD):
                            t = n * QUAD + c
                            nc.tensor.matmul(bank[q % 4][:, c, :], hot_j[b][:, t, :], hot_hi[b][:, t, :], start=True, stop=False)
                            mm = nc.tensor.matmul(bank[q % 4][:, c, :], hot_j[b][:, t, :], hot_lo[b][:, t, :], start=False, stop=True)
                        mm.then_inc(quad_done, 1)
                    while unit < UNITS and turn_of(unit) == turn:
                        early.product(pe, unit // KT, unit % KT, i)
                        unit += 1


class SecondProducts:

    def __init__(self, nc, p, name, acc):
        self.nc, self.acc = nc, acc
        self.v_hi = [p.sb(f"{name}_v_hi{b}", [P, D], F32R) for b in range(4)]
        self.v_lo = [p.sb(f"{name}_v_lo{b}", [P, D], F32R) for b in range(4)]
        self.w_hi = [p.sb(f"{name}_w_hi{b}", [P, SEQ], F32R) for b in range(4)]
        self.w_lo = [p.sb(f"{name}_w_lo{b}", [P, SEQ], F32R) for b in range(4)]
        self.bank = [p.ps(f"{name}_v_bank{b}", [P, HALF]) for b in range(4)]
        self.v_lo_ready = p.sem(name + "_v_lo_ready")
        self.w_lo_ready = p.sem(name + "_w_lo_ready")
        self.done = p.sem(name + "_v_done")
        self.added = p.sem(name + "_added")

    def product(self, pe, r, n, i):
        if n == 0:
            pe.wait_ge(self.w_lo_ready, 8 * i + 4 * r + 4 + 4)
            pe.wait_ge(self.v_lo_ready, 4 * i + 2 * r + 2 + 2)
        pe.wait_ge(self.added, 32 * i + 16 * r + n + 13)
        rows = slice((n // 2) * P, (n // 2 + 1) * P)
        cols = slice((n % 2) * HALF, (n % 2 + 1) * HALF)
        mm_, bank = self.nc.tensor.matmul, self.bank[n % 4][:]
        for c in range(2):
            b = (2 * r + c) % 4
            mm_(bank, self.w_hi[b][:, rows], self.v_hi[b][:, cols], start=(c == 0), stop=False)
            mm_(bank, self.w_hi[b][:, rows], self.v_lo[b][:, cols], start=False, stop=False)
            mm = mm_(bank, self.w_lo[b][:, rows], self.v_hi[b][:, cols], start=False, stop=(c == 1))
        mm.then_inc(self.done, 1)

    def add(self, dve, r, n, i):
        out = self.acc[:, n // 2, (n % 2) * HALF:(n % 2 + 1) * HALF]
        dve.wait_ge(self.done, 32 * i + 16 * r + n + 1 + 32)
        dve.wait_ge(self.added, 32 * i + 16 * r + n + 1)
        self.nc.vector.tensor_tensor(out, self.bank[n % 4][:], out, ALU.add).then_inc(self.added, 1)


def half_gates(g_dram, pair, half):
    slabs = slice(half * SLABS // 2, (half + 1) * SLABS // 2)
    at = slice(2 * pair, 2 * pair + 2) if isinstance(pair, int) else bass.ds(2 * pair, 2)
    return g_dram[slabs, :, at, :].rearrange("s j i t -> j s (i t)")


def early_experts(nc, acts, v_dram, g_dram, acc):
    PAIRS = EARLY // 2
    with ExitStack() as ctx:
        p = Pool(nc, ctx)
        sp_ = SecondProducts(nc, p, "ee", acc)
        v_raw = [p.sb(f"ee_v_raw{b}", [P, D]) for b in range(2)]
        value = [p.sb(f"ee_value{b}", [P, SEQ]) for b in range(2)]
        gates = p.sb("ee_gates", [P, SLABS, 2, SPAN])
        v_loaded, act_loaded = ([p.sem(f"ee_{x}_loaded{b}") for b in range(2)] for x in ("v", "act"))
        g_loaded = [p.sem(f"ee_g_loaded{half}") for half in range(2)]
        v_hi_ready, w_hi_ready = p.sem("ee_v_hi_ready"), p.sem("ee_w_hi_ready")
        gated = p.sem("ee_gated")
        block = ctx.enter_context(nc.Block())

        def walk(eng, visit):
            with eng.Fori(0, PAIRS // 2, 1) as i:
                visit(0, i)
                visit(1, i)

        @block.sync
        def _(sp):
            sp.sem_inc(sp_.v_lo_ready, 2)
            sp.sem_inc(sp_.w_lo_ready, 4)
            sp.sem_inc(gated, 4)

            def visit(r, i):
                pair = i * 2 + r
                for c in range(2):
                    e = 2 * r + c
                    sp.wait_ge(sp_.v_lo_ready, 4 * i + e + 1)
                    sp.dma_start(v_raw[c][:], v_dram[bass.ds(i * (4 * P) + e * P, P), :]).then_inc(v_loaded[c], 16)
                for c in range(2):
                    e = 2 * r + c
                    sp.wait_ge(gated, 8 * i + 4 * r + c + 3)
                    half = gates[:, c * SLABS // 2:(c + 1) * SLABS // 2].rearrange("p s i t -> p s (i t)")
                    sp.dma_start(half, half_gates(g_dram, pair, c)).then_inc(g_loaded[c], 16)
                    sp.wait_ge(sp_.w_lo_ready, 8 * i + 2 * e + 2)
                    sp.dma_start(value[c][:], acts[bass.ds(i * 4 + e, 1)].rearrange("o p t -> (o p) t")).then_inc(act_loaded[c], 16)

            walk(sp, visit)

        @block.scalar
        def _(act):
            s = nc.scalar

            def visit(r, i):
                for c in range(2):
                    e = 2 * r + c
                    act.wait_ge(sp_.done, 32 * i + 16 * (r + 1))
                    act.wait_ge(v_loaded[c], 32 * i + 16 * (r + 1))
                    s.activation(sp_.v_hi[e][:], v_raw[c][:], ACT.Copy).then_inc(v_hi_ready, 1)
                    for half in range(2):
                        cols = slice(half * HALF, (half + 1) * HALF)
                        act.wait_ge(gated, 8 * i + 2 * e + half + 1 + 4)
                        s.activation(sp_.w_hi[e][:, cols], value[c][:, cols], ACT.Copy).then_inc(w_hi_ready, 1)

            walk(act, visit)

        @block.gpsimd
        def _(pool):
            sub = nc.gpsimd.tensor_tensor

            def visit(r, i):
                for c in range(2):
                    e = 2 * r + c
                    pool.wait_ge(v_hi_ready, 4 * i + e + 1)
                    sub(sp_.v_lo[e][:], v_raw[c][:], f32(sp_.v_hi[e][:]), ALU.subtract).then_inc(sp_.v_lo_ready, 1)
                    for half in range(2):
                        cols = slice(half * HALF, (half + 1) * HALF)
                        pool.wait_ge(w_hi_ready, 8 * i + 2 * e + half + 1)
                        sub(sp_.w_lo[e][:, cols], value[c][:, cols], f32(sp_.w_hi[e][:, cols]),
                            ALU.subtract).then_inc(sp_.w_lo_ready, 1)

            walk(pool, visit)

        @block.vector
        def _(dve):
            dve.sem_inc(sp_.done, 32)
            nc.vector.memset(acc[:], 0.0).then_inc(sp_.added, 16)

            def gate(g, i):
                c, half = (g // 2) % 2, g % 2
                dve.wait_ge(act_loaded[c], 32 * i + 16 * (g // 4 + 1))
                dve.wait_ge(g_loaded[half], 32 * i + 16 * (g // 4 + 1))
                out = value[c][:, half * HALF:(half + 1) * HALF].rearrange("p (s t) -> p s t", t=SPAN)
                nc.vector.tensor_tensor(out, out, gates[:, half * SLABS // 2:(half + 1) * SLABS // 2, c, :],
                                        ALU.mult).then_inc(gated, 1)

            def visit(r, i, more=True):
                for n in range(16):
                    if n % 4 == 0 and more:
                        gate(4 * (r + 1) + n // 4, i)
                    sp_.add(dve, r, n, i)

            for g in range(4):
                gate(g, 0)
            with dve.Fori(0, PAIRS // 2 - 1, 1) as i:
                visit(0, i)
                visit(1, i)
            visit(0, PAIRS // 2 - 1)
            visit(1, PAIRS // 2 - 1, more=False)

        @block.tensor
        def _(pe):
            def visit(r, i):
                for n in range(16):
                    sp_.product(pe, r, n, i)

            walk(pe, visit)


def experts(nc, u_tiles, v_dram, g_dram, h_hi, h_lo, acc):
    PAIRS = (N_KEYS - EARLY) // 2
    LAG = 4
    with ExitStack() as ctx:
        p = Pool(nc, ctx)
        sp_ = SecondProducts(nc, p, "ex", acc)
        u_raw = p.sb("ex_u_raw", [P, KT, P])
        v_raw = p.sb("ex_v_raw", [P, D])
        u_hi = [p.sb(f"ex_u_hi{b}", [P, KT, P], F32R) for b in range(2)]
        u_lo = [p.sb(f"ex_u_lo{b}", [P, KT, P], F32R) for b in range(2)]
        gates = p.sb("ex_gates", [P, SLABS, 2, SPAN])
        value = p.sb("ex_value", [P, 2, HALF])
        u_bank = [p.ps(f"ex_u_bank{b}", [P, HALF]) for b in range(4)]
        u_loaded, v_loaded = p.sem("ex_u_loaded"), p.sem("ex_v_loaded")
        g_loaded = [p.sem(f"ex_g_loaded{half}") for half in range(2)]
        u_hi_ready, v_hi_ready = p.sem("ex_u_hi_ready"), p.sem("ex_v_hi_ready")
        u_lo_ready = p.sem("ex_u_lo_ready")
        u_done = p.sem("ex_u_done")
        gelu_done = p.sem("ex_gelu_done")
        gated = p.sem("ex_gated")
        w_hi_ready = p.sem("ex_w_hi_ready")
        block = ctx.enter_context(nc.Block())

        def walk(eng, visit):
            visit(0, 0)
            visit(1, 0)
            with eng.Fori(0, (PAIRS - 4) // 2, 1) as i:
                visit(2, i)
                visit(3, i)
            visit(PAIRS - 2, 0)
            visit(PAIRS - 1, 0)

        def lagged(step, r, n, i):
            if n >= LAG and r >= 1:
                step(r - 1, n - LAG, i)
            elif n < LAG and r >= 2:
                step(r - 2, n - LAG + 16, i)

        def lagged_rest(step):
            for n in range(16 - LAG, 16):
                step(PAIRS - 2, n, 0)
            for n in range(16):
                step(PAIRS - 1, n, 0)

        @block.sync
        def _(sp):
            sp.sem_inc(u_lo_ready, 1)
            sp.sem_inc(sp_.v_lo_ready, 2)
            sp.sem_inc(sp_.w_lo_ready, 4)

            def load_u(e, i):
                sp.wait_ge(u_lo_ready, 4 * i + e + 1)
                at = i * 4 + (EARLY + e)
                src = u_tiles[at:at + 1] if isinstance(i, int) else u_tiles[bass.ds(at, 1)]
                sp.dma_start(u_raw[:], src.rearrange("o p (k n) -> (o p) k n", k=KT)).then_inc(u_loaded, 16)

            def load_v(e, i):
                sp.wait_ge(sp_.v_lo_ready, 4 * i + e + 2)
                at = i * (4 * P) + (EARLY + e) * P
                src = v_dram[at:at + P, :] if isinstance(i, int) else v_dram[bass.ds(at, P), :]
                sp.dma_start(v_raw[:], src).then_inc(v_loaded, 16)

            def load_g(r, half, i):
                sp.wait_ge(gated, 8 * i + 4 * r + half + 3)
                place = gates[:, half * SLABS // 2:(half + 1) * SLABS // 2].rearrange("p s i t -> p s (i t)")
                sp.dma_start(place, half_gates(g_dram, i * 2 + (EARLY // 2 + r), half)).then_inc(g_loaded[half], 16)

            load_u(0, 0)
            load_u(1, 0)
            load_g(0, 0, 0)
            load_g(0, 1, 0)

            def visit(r, i):
                for e in (2 * r, 2 * r + 1):
                    load_v(e, i)
                    if r < PAIRS - 1:
                        load_u(e + 2, i)
                if r < PAIRS - 1:
                    load_g(r + 1, 0, i)
                    load_g(r + 1, 1, i)

            walk(sp, visit)

        @block.scalar
        def _(act):
            s = nc.scalar
            act.sem_inc(gelu_done, 4)

            def high_u(e, i):
                act.wait_ge(u_loaded, 64 * i + 16 * (e + 1))
                act.wait_ge(u_done, 8 * i + 2 * e + 2)
                s.activation(u_hi[e % 2][:], u_raw[:], ACT.Copy).then_inc(u_hi_ready, 1)

            high_u(0, 0)
            high_u(1, 0)

            def visit(r, i):
                for e in (2 * r, 2 * r + 1):
                    for half in range(2):
                        g = 2 * e + half
                        act.wait_ge(u_done, 8 * i + g + 1 + 4)
                        act.wait_ge(sp_.w_lo_ready, 8 * i + g + 1 + 2)
                        s.activation(value[:, g % 2, :], u_bank[g % 4][:], ACT.Gelu_apprx_tanh).then_inc(gelu_done, 1)
                        act.wait_ge(gated, 8 * i + g + 1 + 4)
                        act.wait_ge(sp_.done, 32 * i + 16 * (r + 1))
                        s.activation(sp_.w_hi[e % 4][:, half * HALF:(half + 1) * HALF], value[:, g % 2, :], ACT.Copy).then_inc(w_hi_ready, 1)
                    if r < PAIRS - 1:
                        high_u(e + 2, i)
                    act.wait_ge(v_loaded, 64 * i + 16 * (e + 1))
                    s.activation(sp_.v_hi[e % 4][:], v_raw[:], ACT.Copy).then_inc(v_hi_ready, 1)

            walk(act, visit)

        @block.gpsimd
        def _(pool):
            g_ = nc.gpsimd

            def low_u(e, i):
                pool.wait_ge(u_hi_ready, 4 * i + e + 1)
                g_.tensor_tensor(u_lo[e % 2][:], u_raw[:], f32(u_hi[e % 2][:]), ALU.subtract).then_inc(u_lo_ready, 1)

            low_u(0, 0)
            low_u(1, 0)

            def visit(r, i):
                for e in (2 * r, 2 * r + 1):
                    for half in range(2):
                        g = 2 * e + half
                        cols = slice(half * HALF, (half + 1) * HALF)
                        pool.wait_ge(w_hi_ready, 8 * i + g + 1)
                        g_.tensor_tensor(sp_.w_lo[e % 4][:, cols], value[:, g % 2, :], f32(sp_.w_hi[e % 4][:, cols]),
                                         ALU.subtract).then_inc(sp_.w_lo_ready, 1)
                    if r < PAIRS - 1:
                        low_u(e + 2, i)
                    pool.wait_ge(v_hi_ready, 4 * i + e + 1)
                    g_.tensor_tensor(sp_.v_lo[e % 4][:], v_raw[:], f32(sp_.v_hi[e % 4][:]), ALU.subtract).then_inc(sp_.v_lo_ready, 1)

            walk(pool, visit)

        @block.vector
        def _(dve):
            v = nc.vector
            dve.sem_inc(gated, 4)
            dve.sem_inc(sp_.added, 16)

            def gate(g, i):
                e, half = g // 2, g % 2
                dve.wait_ge(gelu_done, 8 * i + g + 1 + 4)
                dve.wait_ge(g_loaded[half], 32 * i + 16 * (e // 2 + 1))
                out = value[:, g % 2, :].rearrange("p (s t) -> p s t", t=SPAN)
                v.tensor_tensor(out, out, gates[:, half * SLABS // 2:(half + 1) * SLABS // 2, e % 2, :],
                                ALU.mult).then_inc(gated, 1)

            def add(r, n, i):
                sp_.add(dve, r, n, i)

            def visit(r, i):
                for n in range(16):
                    lagged(add, r, n, i)
                    if n % 4 == 3:
                        gate(4 * r + n // 4, i)

            walk(dve, visit)
            lagged_rest(add)

        @block.tensor
        def _(pe):
            pe.sem_inc(u_done, 4)
            pe.sem_inc(sp_.done, 32)
            mm_ = nc.tensor.matmul

            def first(r, n, i):
                e, half = 2 * r + n // 8, (n // 4) % 2
                g = 2 * e + half
                if n % 8 == 0:
                    pe.wait_ge(u_lo_ready, 4 * i + e + 2)
                if n % 4 == 0:
                    pe.wait_ge(gelu_done, 8 * i + g + 1)
                cols = slice(half * HALF, (half + 1) * HALF)
                uh, ul = u_hi[e % 2], u_lo[e % 2]
                for k in (2 * (n % 4), 2 * (n % 4) + 1):
                    mm_(u_bank[g % 4][:], uh[:, k, :], h_hi[:, k, cols], start=(k == 0), stop=False)
                    mm_(u_bank[g % 4][:], uh[:, k, :], h_lo[:, k, cols], start=False, stop=False)
                    mm = mm_(u_bank[g % 4][:], ul[:, k, :], h_hi[:, k, cols], start=False, stop=(k == KT - 1))
                if n % 4 == 3:
                    mm.then_inc(u_done, 1)

            def second(r, n, i):
                sp_.product(pe, r, n, i)

            def visit(r, i):
                for n in range(16):
                    first(r, n, i)
                    lagged(second, r, n, i)

            walk(pe, visit)
            lagged_rest(second)


def cols(v):
    v = v.reshape(-1, KT, P)
    return np.ascontiguousarray(v.transpose(2, 0, 1))


def column_blocks(w, width=NB):
    n = w.shape[1] // width
    return np.ascontiguousarray(w.reshape(KT, P, n, width).transpose(2, 1, 0, 3)).reshape(n, P, KT * width)


def rotary_tables():
    rows = np.repeat(np.arange(SEQ // GRID_W, dtype=np.float32), GRID_W)
    columns = np.tile(np.arange(GRID_W, dtype=np.float32), SEQ // GRID_W)
    quarter = DK // 4
    inv = (np.float32(10000.0) ** (-np.arange(quarter, dtype=np.float32) / np.float32(quarter))).astype(np.float32)
    ang = np.concatenate([rows[:, None] * inv, columns[:, None] * inv], axis=-1)
    return np.ascontiguousarray(np.stack([np.cos(ang).T, np.sin(ang).T], axis=1).astype(np.float32))


def layout(x, c, ctx, c_ctx, w_mod, b_mod, norm_gain, w_in, ret_decay_raw, w_ret_o, conv_w, conv_b,
           conv_norm_g, conv_norm_b, w_conv_o, w_out, peer_wq, peer_keys, peer_u, peer_v):
    return {
        "x": x[0], "ctx": ctx[0],
        "c_cols": np.ascontiguousarray(np.stack([c[0], c_ctx], -1).reshape(KT, P, 2).transpose(1, 0, 2)),
        "w_mod": column_blocks(w_mod[0]), "b_mod": cols(b_mod[0]), "gain": cols(norm_gain[0]),
        "w_in": np.ascontiguousarray(column_blocks(w_in[0])[W_IN_ORDER]),
        "decay": ret_decay_raw[0], "rotary": rotary_tables(),
        "w_ret_o": column_blocks(w_ret_o[0]), "w_conv_o": column_blocks(w_conv_o[0]), "w_out": column_blocks(w_out[0]),
        "conv_w": np.ascontiguousarray(conv_w[0].T.reshape(KT, P, CONV_W).transpose(1, 0, 2)),
        "w_query": column_blocks(peer_wq[0]),
        "keys": np.ascontiguousarray(peer_keys[0].reshape(SIDES, N_KEYS, P).transpose(2, 0, 1)),
        "u_tiles": np.ascontiguousarray(peer_u[0].reshape(N_KEYS, N_KEYS, KT, P).transpose(0, 3, 2, 1)).reshape(N_KEYS, P, D),
        "v": peer_v[0],
        "conv_b": cols(conv_b[0])[:, 0], "conv_norm_g": cols(conv_norm_g[0])[:, 0], "conv_norm_b": cols(conv_norm_b[0])[:, 0],
    }


def scratch(nc, name, shape):
    return nc.dram_tensor(name, shape, F32, kind="Internal").ap()


def mixer_program(nc, a, lat1, keep, ones, ident, mod, rows):
    fm = scratch(nc, "proj_fm", [FM_ROWS, SEQ])
    tm = scratch(nc, "proj_tm", [2 * HEADS, SEQ, DK])
    ctx_kv = scratch(nc, "ctx_kv", [2 * HEADS, CTX, DK])
    conv = scratch(nc, "conv_out", [D, SEQ])
    tokens = lambda dram: dram.rearrange("(t p) d -> p t d", p=P)

    with ExitStack() as s:
        p = Pool(nc, s)
        h_hi, h_lo = p.sb("h_hi", [P, KT, SEQ], F32R), p.sb("h_lo", [P, KT, SEQ], F32R)
        hc_hi, hc_lo = p.sb("hc_hi", [P, KT, CTX], F32R), p.sb("hc_lo", [P, KT, CTX], F32R)
        with ExitStack() as s2:
            q = Pool(nc, s2)
            x, cx = q.sb("x", [P, TT, D]), q.sb("cx", [P, CT, D])
            groups = [(1, 0, CT, k, mod["ac"][:, k:k + 1], mod["bc"][:, k:k + 1], hc_hi[:, k, :], hc_lo[:, k, :])
                      for k in range(KT)]
            groups += latent_groups(mod["a1"], mod["b1"], h_hi, h_lo)
            normalise(nc, "n1", [(x[:], tokens(a["x"])), (cx[:], tokens(a["ctx"]))], groups, ident)
        input_projection(nc, a["w_in"], h_hi, h_lo, hc_hi, hc_lo, fm, tm, ctx_kv, a["conv_w"], a["conv_b"], conv)

    with ExitStack() as s:
        p = Pool(nc, s)
        with ExitStack() as s2:
            q = Pool(nc, s2, "right")
            yg_hi, yg_lo = q.sb("yg_hi", [P, KT, SEQ], F32R), q.sb("yg_lo", [P, KT, SEQ], F32R)
            retention(nc, fm, tm, ctx_kv, a["decay"], a["rotary"], yg_hi, yg_lo, ident)
            merged = p.sb("merged", [P, KT, SEQ])
            project(nc, "pa", a["w_ret_o"], 2, yg_hi, yg_lo, False, fm[8 * NB:10 * NB, :], merged, False)
        with ExitStack() as s2:
            q = Pool(nc, s2, "right")
            u_hi, u_lo = q.sb("u_hi", [P, KT, SEQ], F32R), q.sb("u_lo", [P, KT, SEQ], F32R)
            conv_norm(nc, conv, a["conv_norm_g"], a["conv_norm_b"], u_hi, u_lo, ones)
            project(nc, "pb", a["w_conv_o"], 2, u_hi, u_lo, False, fm[10 * NB:12 * NB, :], merged, True)
        with ExitStack() as s2:
            q = Pool(nc, s2, "right")
            m_hi, m_lo = q.sb("m_hi", [P, KT, SEQ], F32R), q.sb("m_lo", [P, KT, SEQ], F32R)
            split_tile(nc, "ms", merged, m_hi, m_lo)
            project(nc, "po", a["w_out"], 2, m_hi, m_lo, True, None, merged, False)
        residual(nc, "r1", merged, a["x"], rows["g1"][:], lat1)
        h2 = Pool(nc, keep, "right")
        hi, lo = h2.sb("h2_hi", [P, KT, SEQ], F32R), h2.sb("h2_lo", [P, KT, SEQ], F32R)
        normalise(nc, "n2", [(merged[:], None)], latent_groups(mod["a2"], mod["b2"], hi, lo), ident)
    return hi, lo


def latent_groups(a, b, hi, lo):
    return [(0, 4 * half, 4, k, a[:, k:k + 1], b[:, k:k + 1], hi[:, k, half * HALF:(half + 1) * HALF],
             lo[:, k, half * HALF:(half + 1) * HALF]) for k in range(KT) for half in range(2)]


def layer_program(nc, a, out):
    lat1 = scratch(nc, "lat1", [SEQ, D])
    scores = scratch(nc, "scores", [SEQ, SIDES * N_KEYS])
    gates = scratch(nc, "gates", [SLABS, N_KEYS, N_KEYS, SPAN])
    acts = scratch(nc, "acts", [EARLY, P, SEQ])
    with ExitStack() as keep:
        p = Pool(nc, keep)
        ones, ident = p.sb("ones", [P, P]), p.sb("ident", [P, P])
        mod = {k: p.sb("mod_" + k, [P, KT]) for k in ("a1", "b1", "a2", "b2", "ac", "bc")}
        g2_row = p.sb("row_g2", [P, D])
        constants(nc, ones, ident)
        with ExitStack() as s:
            rows = {"g1": Pool(nc, s).sb("row_g1", [P, D]), "g2": g2_row}
            conditioning(nc, a["c_cols"], a["w_mod"], a["b_mod"], a["gain"], mod, rows, ones[:], ident[:])
            h2 = mixer_program(nc, a, lat1, keep, ones[:], ident[:], mod, rows)
        query_scores(nc, a["w_query"], a["keys"], *h2, scores)
        with ExitStack() as s:
            q = Pool(nc, s)
            first_T, second_T, gate_T = (q.sb(n, [P, SEQ]) for n in ("first_T", "second_T", "gate_T"))
            top_experts(nc, scores, first_T, second_T, gate_T, ident[:], a["u_tiles"], h2, acts)
            gate_matrix(nc, first_T, second_T, gate_T, gates, a["u_tiles"], h2, acts)
        acc = p.sb("retrieved", [P, TT, D])
        early_experts(nc, acts, a["v"], gates, acc)
        experts(nc, a["u_tiles"], a["v"], gates, *h2, acc)
        residual(nc, "r2", acc, lat1, g2_row[:], out)


def kernel(**inputs):
    from concourse import bacc
    from concourse.bass_utils import run_bass_kernel_spmd

    arrays = layout(**inputs)
    nc = bacc.Bacc("TRN2", target_bir_lowering=False, num_devices=1)
    a = {name: nc.dram_tensor("in_" + name, array.shape, mybir.dt.from_np(array.dtype),
                               kind="ExternalInput").ap()
         for name, array in arrays.items()}
    out = nc.dram_tensor("out", (SEQ, D), F32, kind="ExternalOutput").ap()
    layer_program(nc, a, out)
    nc.finalize()
    result = run_bass_kernel_spmd(nc, [{"in_" + name: array for name, array in arrays.items()}], core_ids=[0])
    return result.results[0]["out"][None]
```

```python
import numpy as np
from contextlib import ExitStack

import concourse.bass as bass
from concourse import mybir
from concourse.alu_op_type import AluOpType as ALU

ACT = mybir.ActivationFunctionType
AX = mybir.AxisListType
F32 = mybir.dt.float32
F32R = mybir.dt.float32r
BF16 = mybir.dt.bfloat16
I32 = mybir.dt.int32
U32 = mybir.dt.uint32

P = 128
SEQ = 1024
CTX = 256
D = 1024
KT = D // P
TT = SEQ // P
CT = CTX // P
HALF = 512
NB = 512
EPS = 1e-6
HEADS = 4
DK = 256
GRID_W = 64
CONV_W = 31


class Pool:

    def __init__(self, nc, ctx, side="left"):
        self.nc, self.ctx, self.side, self.sems = nc, ctx, side, []
        ctx.callback(self.give_back)

    def give_back(self):
        if self.sems:
            self.nc.clear_and_free_semaphores(self.sems)
            self.nc.all_engine_barrier()

    def sem(self, name):
        self.sems.append(self.nc.alloc_semaphore(name))
        return self.sems[-1]

    def sb(self, name, shape, dt=F32):
        return self.ctx.enter_context(self.nc.sbuf_tensor(name, shape, dt, side=self.side))

    def ps(self, name, shape, dt=F32):
        return self.ctx.enter_context(self.nc.psum_tensor(name, shape, dt))


class Chain:

    def __init__(self, eng, sem, base=0, per_turn=0, i=0):
        self.eng, self.sem, self.base, self.per_turn, self.i, self.taken = eng, sem, base, per_turn, i, 0

    def step(self, instruction):
        self.taken += 1
        instruction.then_inc(self.sem, 1)
        count = self.base + self.taken
        self.eng.wait_ge(self.sem, self.i * self.per_turn + count if self.per_turn else count)


def f32(ap):
    return ap.bitcast(F32)


def split_matmuls(nc, out, pairs, before=lambda n: None):
    last = None
    for n, ((s_hi, s_lo), (m_hi, m_lo)) in enumerate(pairs):
        before(n)
        nc.tensor.matmul(out, s_hi, m_hi, start=(n == 0), stop=False)
        nc.tensor.matmul(out, s_hi, m_lo, start=False, stop=False)
        last = nc.tensor.matmul(out, s_lo, m_hi, start=False, stop=(n == len(pairs) - 1))
    return last


class FirstBlock:
    ON_POOL = (1, 4, 7)

    def __init__(self, nc, p, name, raw, w_hi, w_lo):
        self.nc = nc
        self.raw, self.hi, self.lo = (x[:].rearrange("p (k n) -> p k n", k=KT) for x in (raw, w_hi, w_lo))
        self.loaded = [p.sem(f"{name}_first_loaded{k}") for k in range(KT)]
        self.high = p.sem(name + "_first_high")
        self.low_pool, self.low_dve = p.sem(name + "_first_low_pool"), p.sem(name + "_first_low_dve")

    def load(self, sp, w_block):
        for k in range(KT):
            sp.dma_start(self.raw[:, k, :], w_block.rearrange("p (k n) -> p k n", k=KT)[:, k, :]).then_inc(self.loaded[k], 16)

    def split_high(self, act):
        for k in range(KT):
            act.wait_ge(self.loaded[k], 16)
            self.nc.scalar.activation(self.hi[:, k, :], self.raw[:, k, :], ACT.Copy).then_inc(self.high, 1)

    def split_low(self, engine, wait, on_pool):
        for k in range(KT):
            if (k in self.ON_POOL) == on_pool:
                wait.wait_ge(self.high, k + 1)
                engine.tensor_tensor(self.lo[:, k, :], self.raw[:, k, :], f32(self.hi[:, k, :]),
                                     ALU.subtract).then_inc(self.low_pool if on_pool else self.low_dve, 1)

    def wait(self, eng, k):
        on_pool = k in self.ON_POOL
        before = sum((j in self.ON_POOL) == on_pool for j in range(k + 1))
        eng.wait_ge(self.low_pool if on_pool else self.low_dve, before)

    def wait_all(self, eng):
        self.wait(eng, max(self.ON_POOL))
        self.wait(eng, max(set(range(KT)) - set(self.ON_POOL)))

BLOCKS = ["glu_a", "glu_b", "glu_a", "glu_b", "q", "q", "k", "k",
          "gate_a", "gate_a", "gate_b", "gate_b", "v", "v", "g_ret", "g_ret"]
W_IN_ORDER = [8, 10, 9, 11, 0, 1, 2, 3, 12, 13, 14, 15, 4, 5, 6, 7]
FM_ROWS = 12 * NB


def input_projection(nc, w_blocks, h_hi, h_lo, hc_hi, hc_lo, fm, tm, ctx_kv, conv_w, conv_b, conv):
    with ExitStack() as ctx:
        p = Pool(nc, ctx)
        RING = 4
        raw = p.sb("ip_raw", [P, KT * NB])
        w_hi = [p.sb(f"ip_w_hi{b}", [P, KT * NB], F32R) for b in range(2)]
        w_lo = [p.sb(f"ip_w_lo{b}", [P, KT * NB], F32R) for b in range(2)]
        first = FirstBlock(nc, p, "ip", raw, w_hi[0], w_lo[0])
        stage = p.sb("ip_stage", [P, RING, HALF])
        bank = [p.ps(f"ip_bank{b}", [P, HALF]) for b in range(RING)]

        glu = p.sb("ip_glu", [P, 2, SEQ])
        PAD = CONV_W // 2
        padded = [p.sb(f"ip_padded{b}", [P, SEQ + 2 * PAD]) for b in range(2)]
        convolved = p.sb("ip_convolved", [P, 2, SEQ])
        taps = p.sb("ip_taps", [P, KT, CONV_W])
        conv_bias = p.sb("ip_conv_bias", [P, KT])

        taps_loaded = p.sem("ip_taps_loaded")
        glu_loaded = p.sem("ip_glu_loaded")
        sigmoid_ready = p.sem("ip_sigmoid_ready")
        glu_ready = p.sem("ip_glu_ready")
        conv_chain = p.sem("ip_conv_chain")
        conv_ready = p.sem("ip_conv_ready")
        conv_stored = [p.sem(f"ip_conv_stored{b}") for b in range(2)]
        raw_loaded = p.sem("ip_raw_loaded")
        hi_ready = p.sem("ip_hi_ready")
        lo_ready = p.sem("ip_lo_ready")
        group_done = p.sem("ip_group_done")
        evacuated = p.sem("ip_evacuated")
        stored = [p.sem(f"ip_stored{r}") for r in range(RING)]

        SEGMENTS = [(0, 2, False, False, True), (4, 1, False, False, False), (6, 1, False, True, False),
                    (8, 2, False, False, True), (12, 1, True, True, False), (14, 1, True, False, False)]
        N_BLOCKS = 16
        CONV_FIRST = 4

        def walk(eng, visit):
            group = 0
            for first, pairs, token_major, context, rolled in SEGMENTS:
                per_block = 8 + (CT if context else 0)
                if rolled:
                    with eng.Fori(0, pairs, 1) as i:
                        for b in range(2):
                            visit(first + b, i, b, group + b * per_block, 2 * per_block,
                                  token_major, context, True, True)
                else:
                    for b in range(2):
                        blk = first + b
                        visit(blk, 0, b, group + b * per_block, 0, token_major, context,
                              blk + 1 < N_BLOCKS, blk + 2 < N_BLOCKS)
                group += 2 * pairs * per_block

        block = ctx.enter_context(nc.Block())

        @block.sync
        def _(sp):
            for r in range(RING):
                sp.sem_inc(stored[r], 16)
            sp.sem_inc(raw_loaded, 16)
            sp.sem_inc(hi_ready, 1)
            sp.sem_inc(lo_ready, 1)
            first.load(sp, w_blocks[0])
            sp.dma_start(taps[:], conv_w).then_inc(taps_loaded, 16)
            sp.dma_start(conv_bias[:], conv_b).then_inc(taps_loaded, 16)
            for b in range(2):
                sp.sem_inc(conv_stored[b], 16)
            sp.sem_inc(conv_ready, 2)
            first.wait_all(sp)
            sp.dma_start(raw[:], w_blocks[1]).then_inc(raw_loaded, 16)

            def visit(blk, i, b, group, step, token_major, context, ahead, load):
                if load:
                    sp.wait_ge(lo_ready, blk + 2 + 2 * i)
                    src = w_blocks[bass.ds(blk + 2 + 2 * i, 1)] if step else w_blocks[blk + 2:blk + 3]
                    sp.dma_start(raw[:], src.rearrange("o p n -> (o p) n")).then_inc(raw_loaded, 16)
                tile = blk - CONV_FIRST
                if 0 <= tile < KT:
                    if tile == 0:
                        for r in range(RING):
                            sp.wait_ge(stored[r], 16 * (CONV_FIRST * 8 // RING + 1))
                    else:
                        sp.wait_ge(glu_ready, tile + 2 * i)
                    row = tile * P + (tile // 4) * NB
                    rows = fm[bass.ds(row + 2 * P * i, P + NB), :] if step else fm[row:row + P + NB, :]
                    for j in range(2):
                        sp.dma_start(glu[:, j, :], rows[j * NB:j * NB + P, :]).then_inc(glu_loaded, 16)
                if 0 < tile <= KT:
                    store_tile(tile - 1, i if step else 0, step)
                for g in range(8 + (CT if context else 0)):
                    sp.wait_ge(evacuated, group + g + 1 + RING + step * i)
                    slot = (group + g) % RING
                    if g >= 8:
                        j = (blk - 6) if blk < 8 else (blk - 12 + 2)
                        dst = ctx_kv[2 * j:2 * j + 2, (g - 8) * P:(g - 7) * P, :].rearrange("e t d -> t e d")
                    elif token_major:
                        h = 2 * (blk - 12)
                        dst = tm[h:h + 2, g * P:(g + 1) * P, :].rearrange("e t d -> t e d")
                    else:
                        row = blk * NB + (g // 2) * P
                        cols = slice((g % 2) * HALF, (g % 2 + 1) * HALF)
                        dst = fm[bass.ds(row + 2 * NB * i, P), cols] if step else fm[row:row + P, cols]
                    src = stage[:, slot, :]
                    if g >= 8 or token_major:
                        src = src.rearrange("p (e d) -> p e d", e=2)
                    sp.dma_start(dst, src).then_inc(stored[slot], 16)

            def store_tile(tile, i, step):
                sp.wait_ge(conv_ready, tile + 3 + 2 * i)
                dst = conv[bass.ds(tile * P + 2 * P * i, P), :] if step else conv[tile * P:(tile + 1) * P, :]
                sp.dma_start(dst, convolved[:, tile % 2, :]).then_inc(conv_stored[tile % 2], 16)

            walk(sp, visit)
            for b in range(2):
                sp.wait_ge(conv_stored[b], 16 * (KT // 2 + 1))
            total = 16 * 8 + 4 * CT
            for r in range(RING):
                sp.wait_ge(stored[r], 16 * (total // RING + 1))

        @block.scalar
        def _(act):
            def split(blk, i, b):
                act.wait_ge(raw_loaded, 16 * (blk + 1) + 32 * i)
                nc.scalar.activation(w_hi[b][:], raw[:], ACT.Copy).then_inc(hi_ready, 1)

            first.split_high(act)

            def visit(blk, i, b, group, step, token_major, context, ahead, load):
                if ahead:
                    split(blk + 1, i, 1 - b)
                tile = blk - CONV_FIRST
                for g in range(8 + (CT if context else 0)):
                    if g == 1 and 0 <= tile < KT:
                        act.wait_ge(glu_loaded, 32 * (tile + 1) + 64 * i)
                        nc.scalar.activation(glu[:, 1, :], glu[:, 1, :], ACT.Sigmoid).then_inc(sigmoid_ready, 1)
                    slot = (group + g) % RING
                    act.wait_ge(group_done, group + g + 1 + step * i)
                    act.wait_ge(stored[slot], 16 * ((group + g) // RING + 1) + 16 * (step // RING) * i)
                    nc.scalar.activation(stage[:, slot, :], bank[slot][:], ACT.Copy).then_inc(evacuated, 1)

            walk(act, visit)

        @block.vector
        def _(dve):
            def visit(blk, i, b, group, step, token_major, context, ahead, load):
                tile = blk - CONV_FIRST
                if 0 <= tile < KT:
                    chain = Chain(dve, conv_chain, (CONV_W - 1) * tile, 2 * (CONV_W - 1) if step else 0, i)
                    out = convolved[:, tile % 2, :]
                    tap = taps[:, bass.ds(tile + 2 * i, 1), :] if step else taps[:, tile:tile + 1, :]
                    tap = tap.rearrange("p o w -> p (o w)")
                    bias = conv_bias[:, bass.ds(tile + 2 * i, 1)] if step else conv_bias[:, tile:tile + 1]
                    dve.wait_ge(glu_ready, tile + 1 + 2 * i)
                    dve.wait_ge(conv_stored[tile % 2], 16 * (tile // 2 + 1) + 16 * i)
                    chain.step(nc.vector.tensor_scalar(out, padded[tile % 2][:, 0:SEQ], tap[:, 0:1], bias, ALU.mult, ALU.add))
                    for w in range(1, CONV_W):
                        add = nc.vector.scalar_tensor_tensor(out=out, in0=padded[tile % 2][:, w:w + SEQ], scalar=tap[:, w:w + 1],
                                                             in1=out, op0=ALU.mult, op1=ALU.add)
                        if w < CONV_W - 1:
                            chain.step(add)
                        else:
                            add.then_inc(conv_ready, 1)

            first.split_low(nc.vector, dve, False)
            dve.wait_ge(taps_loaded, 32)
            walk(dve, visit)

        @block.gpsimd
        def _(pool):
            def low_part(blk, i, b):
                pool.wait_ge(hi_ready, blk + 1 + 2 * i)
                nc.gpsimd.tensor_tensor(w_lo[b][:], raw[:], f32(w_hi[b][:]), ALU.subtract).then_inc(lo_ready, 1)

            for b in range(2):
                nc.gpsimd.memset(padded[b][:, 0:PAD], 0.0)
                nc.gpsimd.memset(padded[b][:, SEQ + PAD:], 0.0)
            first.split_low(nc.gpsimd, pool, True)

            def visit(blk, i, b, group, step, token_major, context, ahead, load):
                if ahead:
                    low_part(blk + 1, i, 1 - b)
                tile = blk - CONV_FIRST
                if 0 <= tile < KT:
                    pool.wait_ge(sigmoid_ready, tile + 1 + 2 * i)
                    pool.wait_ge(conv_ready, tile + 1 + 2 * i)
                    nc.gpsimd.tensor_tensor(padded[tile % 2][:, PAD:PAD + SEQ], glu[:, 0, :], glu[:, 1, :],
                                            ALU.mult).then_inc(glu_ready, 1)

            walk(pool, visit)

        @block.tensor
        def _(pe):
            pe.sem_inc(evacuated, RING)

            def visit(blk, i, b, group, step, token_major, context, ahead, load):
                pe.wait_ge(lo_ready, blk + 1 + 2 * i)
                wh = w_hi[b][:].rearrange("p (k n) -> p k n", k=KT)
                wl = w_lo[b][:].rearrange("p (k n) -> p k n", k=KT)
                for g in range(8 + (CT if context else 0)):
                    slot = (group + g) % RING
                    pe.wait_ge(evacuated, group + g + 1 + step * i)
                    if g >= 8:
                        c = slice((g - 8) * P, (g - 7) * P)
                        pairs = [((hc_hi[:, k, c], hc_lo[:, k, c]), (wh[:, k, :], wl[:, k, :])) for k in range(KT)]
                    elif token_major:
                        c = slice(g * P, (g + 1) * P)
                        pairs = [((h_hi[:, k, c], h_lo[:, k, c]), (wh[:, k, :], wl[:, k, :])) for k in range(KT)]
                    else:
                        n = slice((g // 2) * P, (g // 2 + 1) * P)
                        c = slice((g % 2) * HALF, (g % 2 + 1) * HALF)
                        pairs = [((wh[:, k, n], wl[:, k, n]), (h_hi[:, k, c], h_lo[:, k, c])) for k in range(KT)]
                    if blk == 0 and g == 0:
                        split_matmuls(nc, bank[slot][:], pairs, before=lambda k: first.wait(pe, k)).then_inc(group_done, 1)
                    else:
                        split_matmuls(nc, bank[slot][:], pairs).then_inc(group_done, 1)

            walk(pe, visit)


def rsqrt_of_mean(nc, chain, act_sqrt, out, sums, scratch, n):
    v = nc.vector
    mean, root, y2 = scratch
    chain.step(v.tensor_scalar(mean, sums, 1.0 / n, EPS, ALU.mult, ALU.add))
    act_sqrt(root, mean)
    chain.step(v.reciprocal(out, root))
    chain.step(v.tensor_tensor(y2, out, out, ALU.mult))
    chain.step(v.tensor_tensor(y2, y2, mean, ALU.mult))
    chain.step(v.tensor_scalar(y2, y2, -0.5, 1.5, ALU.mult, ALU.add))
    chain.step(v.tensor_tensor(out, out, y2, ALU.mult))

SH1, SC1, G1, SH2, SC2, G2 = range(6)


def conditioning(nc, c_cols, w_mod_blocks, b_mod_cols, gain_cols, mod, rows, ones, ident, sources):
    NBLK = 12
    row_tiles = [(x[:, t, :], dram[:, t, :]) for x, dram in sources for t in range(x.shape[1])]
    TILES = len(row_tiles)
    AHEAD = 3
    with ExitStack() as ctx:
        p = Pool(nc, ctx)
        w = [p.sb(f"cd_w{b}", [P, KT, NB]) for b in range(3)]
        c2 = p.sb("cd_c", [P, KT, 2])
        c2s = p.sb("cd_cs", [P, KT, 2])
        bias = p.sb("cd_bias", [P, 6, KT])
        gain = p.sb("cd_gain", [P, 4, KT])
        lat = p.sb("cd_lat", [P, 6, KT])
        cmod = p.sb("cd_cmod", [P, 2, KT])
        g12 = p.sb("cd_g12", [P, 2, KT])
        diag = p.sb("cd_diag", [P, 2, D])
        row2 = p.sb("cd_row2", [2, 6 * D])
        row_bank = [p.ps(f"cd_row_bank{b}", [2, NB]) for b in range(2)]
        acc = p.ps("cd_acc", [P, 6 * KT, 2])
        spread = [p.ps(f"cd_spread{n}", [P, HALF]) for n in range(4)]
        small_loaded = p.sem("cd_small_loaded")
        w_loaded = [p.sem(f"cd_w_loaded{b}") for b in range(3)]
        w_used = p.sem("cd_w_used")
        silu_ready = p.sem("cd_silu_ready")
        row_copied = p.sem("cd_row_copied")
        turned = p.sem("cd_turned")
        chained = p.sem("cd_chained")
        diag_ready = p.sem("cd_diag_ready")
        spread_done = p.sem("cd_spread_done")
        squares = p.sb("cd_squares", [P, D])
        sums, rstd = p.sb("cd_sums", [P, TILES]), p.sb("cd_rstd", [P, TILES])
        scratch = [p.sb(f"cd_scratch{n}", [P, TILES]) for n in range(3)]
        tile_loaded = [p.sem(f"cd_tile_loaded{t}") for t in range(TILES)]
        summed = p.sem("cd_summed")
        mean_ready, root_ready = p.sem("cd_mean_ready"), p.sem("cd_root_ready")

        def tiles_at(n):
            return range(n - AHEAD, n - AHEAD + 1 if n < NBLK - 1 else TILES) if n >= AHEAD else ()

        block = ctx.enter_context(nc.Block())

        @block.sync
        def _(sp):
            sp.dma_start(c2[:], c_cols).then_inc(small_loaded, 16)
            sp.dma_start(bias[:], b_mod_cols).then_inc(small_loaded, 16)
            sp.dma_start(gain[:], gain_cols).then_inc(small_loaded, 16)
            for n in range(NBLK):
                if n >= 3:
                    sp.wait_ge(w_used, n - 2)
                sp.dma_start(w[n % 3][:].rearrange("p k n -> p (k n)"), w_mod_blocks[n]).then_inc(w_loaded[n % 3], 16)
                for t in (tiles_at(n + 1) if n + 1 < NBLK else ()):
                    sp.dma_start(row_tiles[t][0], row_tiles[t][1]).then_inc(tile_loaded[t], 16)

        @block.scalar
        def _(act):
            act.wait_ge(small_loaded, 48)
            nc.scalar.activation(c2s[:], c2[:], ACT.Silu).then_inc(silu_ready, 1)
            for n in range(NBLK):
                act.wait_ge(w_used, n + 1)
                nc.scalar.activation(row2[:, n * NB:(n + 1) * NB], row_bank[n % 2][:], ACT.Copy).then_inc(row_copied, 1)
                for t in tiles_at(n):
                    act.wait_ge(tile_loaded[t], 16)
                    if t:
                        act.wait_ge(summed, t)
                    nc.scalar.activation(squares[:], row_tiles[t][0], ACT.Square, accum_out=sums[:, t:t + 1]).then_inc(summed, 1)
            act.wait_ge(mean_ready, 1)
            nc.scalar.activation(scratch[1][:], scratch[2][:], ACT.Sqrt).then_inc(root_ready, 1)

        @block.tensor
        def _(pe):
            pe.wait_ge(silu_ready, 1)
            for n in range(NBLK):
                pe.wait_ge(w_loaded[n % 3], 16 * (n // 3 + 1))
                if n >= 2:
                    pe.wait_ge(row_copied, n - 1)
                for k in range(KT):
                    mm = nc.tensor.matmul(row_bank[n % 2][:], c2s[:, k, :], w[n % 3][:, k, :],
                                          start=(k == 0), stop=(k == KT - 1))
                mm.then_inc(w_used, 1)
            pe.wait_ge(row_copied, NBLK)
            for m in range(6 * KT):
                tr = nc.tensor.transpose(acc[:, m, :], row2[:, m * P:(m + 1) * P], ident[0:2, 0:2])
            tr.then_inc(turned, 1)
            pe.wait_ge(diag_ready, 1)
            for n in range(4):
                mm = nc.tensor.matmul(spread[n][:], ones, diag[:, n // 2, (n % 2) * HALF:(n % 2 + 1) * HALF],
                                      start=True, stop=True)
            mm.then_inc(spread_done, 1)

        @block.vector
        def _(dve):
            v = nc.vector
            chain = Chain(dve, chained)

            def act_sqrt(root, mean):
                v.tensor_copy(scratch[2][:], mean).then_inc(mean_ready, 1)
                dve.wait_ge(root_ready, 1)

            dve.wait_ge(summed, TILES)
            rsqrt_of_mean(nc, chain, act_sqrt, rstd[:], sums[:], (scratch[0][:], scratch[1][:], scratch[2][:]), D)
            dve.wait_ge(small_loaded, 48)
            dve.wait_ge(turned, 1)
            parts = acc[:].rearrange("p (m k) c -> p m k c", m=6)
            chain.step(v.tensor_tensor(lat[:], parts[:, :, :, 0], bias[:], ALU.add))
            chain.step(v.tensor_tensor(cmod[:], parts[:, 0:2, :, 1], bias[:, 0:2, :], ALU.add))
            for a, b, source, sh, sc, g in (("a1", "b1", lat, SH1, SC1, 0), ("a2", "b2", lat, SH2, SC2, 2),
                                            ("ac", "bc", cmod, SH1, SC1, 0)):
                chain.step(v.scalar_tensor_tensor(out=mod[a][:], in0=source[:, sc, :], scalar=1.0, in1=gain[:, g, :],
                                                  op0=ALU.add, op1=ALU.mult))
                chain.step(v.tensor_copy(mod[b][:], source[:, sh, :]))
            chain.step(v.tensor_tensor(g12[:, 0, :], lat[:, G1, :], gain[:, 1, :], ALU.mult))
            chain.step(v.tensor_tensor(g12[:, 1, :], lat[:, G2, :], gain[:, 3, :], ALU.mult))
            for m in range(2):
                for k in range(KT):
                    last = v.tensor_scalar(diag[:, m, k * P:(k + 1) * P], ident, g12[:, m, k:k + 1], None, ALU.mult)
            last.then_inc(diag_ready, 1)
            for t, (x, _) in enumerate(row_tiles):
                v.tensor_scalar(x, x, rstd[:, t:t + 1], None, ALU.mult)
            dve.wait_ge(spread_done, 1)
            for m, row in enumerate((rows["g1"], rows["g2"])):
                for half in range(2):
                    v.tensor_copy(row[:, half * HALF:(half + 1) * HALF], spread[2 * m + half][:])


def normalise(nc, name, sources, groups, ident, is_scaled=False):
    with ExitStack() as ctx:
        p = Pool(nc, ctx)
        RING = 4
        tiles = sum(x.shape[1] for x, _ in sources)
        at = [sum(x.shape[1] for x, _ in sources[:n]) for n in range(len(sources))]
        squares = p.sb(name + "_squares", [P, D])
        sums = p.sb(name + "_sums", [P, tiles])
        rstd = p.sb(name + "_rstd", [P, tiles])
        scratch = [p.sb(f"{name}_scratch{n}", [P, tiles]) for n in range(3)]
        value = p.sb(name + "_value", [P, RING, HALF])
        bank = [p.ps(f"{name}_bank{b}", [P, HALF]) for b in range(RING)]
        loaded = [p.sem(f"{name}_loaded{n}") for n in range(len(sources))]
        summed = p.sem(name + "_summed")
        mean_ready = p.sem(name + "_mean_ready")
        root_ready = p.sem(name + "_root_ready")
        chained = p.sem(name + "_chained")
        scaled = p.sem(name + "_scaled")
        turned = p.sem(name + "_turned")
        valued = p.sem(name + "_valued")
        high = p.sem(name + "_high")
        low = p.sem(name + "_low")
        block = ctx.enter_context(nc.Block())

        @block.sync
        def _(sp):
            for n, (x, dram) in enumerate(sources):
                if dram is not None:
                    sp.dma_start(x, dram).then_inc(loaded[n], 16)

        @block.scalar
        def _(act):
            for n, (x, dram) in enumerate(() if is_scaled else sources):
                if dram is not None:
                    act.wait_ge(loaded[n], 16)
                for t in range(x.shape[1]):
                    c = at[n] + t
                    if c:
                        act.wait_ge(summed, c)
                    nc.scalar.activation(squares[:], x[:, t, :], ACT.Square, accum_out=sums[:, c:c + 1]).then_inc(summed, 1)
            if not is_scaled:
                act.wait_ge(mean_ready, 1)
                nc.scalar.activation(scratch[1][:], scratch[0][:], ACT.Sqrt).then_inc(root_ready, 1)
            for g, (_, _, m, _, _, _, hi, _) in enumerate(groups):
                act.wait_ge(valued, g + 1)
                nc.scalar.activation(hi, value[:, g % RING, 0:m * P], ACT.Copy).then_inc(high, 1)

        @block.vector
        def _(dve):
            v = nc.vector
            chain = Chain(dve, chained)

            def act_sqrt(root, mean):
                v.tensor_copy(scratch[2][:], mean).then_inc(mean_ready, 1)
                dve.wait_ge(root_ready, 1)

            if not is_scaled:
                dve.wait_ge(summed, tiles)
                rsqrt_of_mean(nc, chain, act_sqrt, rstd[:], sums[:], (scratch[0][:], scratch[1][:], scratch[2][:]), D)
                for n, (x, _) in enumerate(sources):
                    for t in range(x.shape[1]):
                        v.tensor_scalar(x[:, t, :], x[:, t, :], rstd[:, at[n] + t:at[n] + t + 1], None,
                                        ALU.mult).then_inc(scaled, 1)

            def low_part(g):
                m, lo, hi = groups[g][2], groups[g][7], groups[g][6]
                dve.wait_ge(high, g + 1)
                v.tensor_tensor(lo, value[:, g % RING, 0:m * P], f32(hi), ALU.subtract).then_inc(low, 1)

            for g, (_, _, m, _, a, b, _, _) in enumerate(groups):
                dve.wait_ge(turned, g + 1)
                if g >= RING:
                    dve.wait_ge(low, g - RING + 1)
                v.tensor_scalar(value[:, g % RING, 0:m * P], bank[g % RING][:, 0:m * P], a, b,
                                ALU.mult, ALU.add).then_inc(valued, 1)
                if g >= 1:
                    low_part(g - 1)
            low_part(len(groups) - 1)

        @block.tensor
        def _(pe):
            if not is_scaled:
                pe.wait_ge(scaled, tiles)
            for g, (n, first, m, k, _, _, _, _) in enumerate(groups):
                if g >= RING:
                    pe.wait_ge(valued, g - RING + 1)
                for t in range(m):
                    tr = nc.tensor.transpose(bank[g % RING][:, t * P:(t + 1) * P],
                                             sources[n][0][:, first + t, k * P:(k + 1) * P], ident)
                tr.then_inc(turned, 1)


def constants(nc, ones, ident):
    with ExitStack() as ctx:
        p = Pool(nc, ctx)
        zeroed = p.sem("cs_zeroed")
        block = ctx.enter_context(nc.Block())

        @block.gpsimd
        def _(pool):
            nc.gpsimd.memset(ones[:], 1.0)
            nc.gpsimd.memset(ident[:], 0.0).then_inc(zeroed, 1)
            pool.wait_ge(zeroed, 1)
            nc.gpsimd.affine_select(out=ident[:], in_=ident[:], compare_op=ALU.not_equal, fill=1.0, base=0,
                                    pattern=[[-1, P]], channel_multiplier=1)

CHUNK = 128
NC_ = SEQ // CHUNK
Q_ROW, K_ROW = 4 * NB, 6 * NB

ROTATE_STEPS = 3
COMPLETED = [c for st in range(NC_ // 2, NC_) for c in (st, NC_ - 1 - st)]


def rotate(engine, chain, out, raw, cos_sin, tmp, done):
    cos, sin = cos_sin[:, 0, :], cos_sin[:, 1, :]
    engine.tensor_tensor(out[:, 0, :], raw[:, 0, :], cos, ALU.mult)
    engine.tensor_tensor(out[:, 1, :], raw[:, 0, :], sin, ALU.mult)
    chain.step(engine.tensor_tensor(tmp[:], raw[:, 1, :], sin, ALU.mult))
    chain.step(engine.tensor_tensor(out[:, 0, :], out[:, 0, :], tmp[:], ALU.subtract))
    chain.step(engine.tensor_tensor(tmp[:], raw[:, 1, :], cos, ALU.mult))
    engine.tensor_tensor(out[:, 1, :], out[:, 1, :], tmp[:], ALU.add).then_inc(done, 1)


def retention(nc, fm, tm, ctx_kv, decay_raw, cos_sin, yg_hi, yg_lo, ident):
    with ExitStack() as ctx:
        p = Pool(nc, ctx)
        q_raw = p.sb("rt_q_raw", [P, 2, SEQ])
        k_raw = p.sb("rt_k_raw", [P, 2, SEQ])
        q = p.sb("rt_q", [P, 2, SEQ])
        k = p.sb("rt_k", [P, 2, SEQ])
        v = p.sb("rt_v", [P, NC_, DK])
        gate = p.sb("rt_gate", [P, NC_, DK])
        kc = p.sb("rt_kc", [P, CT, DK])
        vc = p.sb("rt_vc", [P, CT, DK])
        kcd = [p.sb(f"rt_kcd{d}", [P, CT, DK]) for d in range(2)]
        kd = [p.sb(f"rt_kd{d}", [P, NC_, DK]) for d in range(2)]
        state = [p.sb(f"rt_state{d}", [P, 2, DK]) for d in range(2)]
        y = p.sb("rt_y", [P, NC_, DK])
        weights = p.sb("rt_weights", [P, NC_, CHUNK])
        cs = p.sb("rt_cos_sin", [P, 2, SEQ])
        tmp_q = p.sb("rt_tmp_q", [P, SEQ])
        tmp_k = p.sb("rt_tmp_k", [P, SEQ])
        value = p.sb("rt_value", [P, 2, HALF])
        dist = p.sb("rt_dist", [P, 2, CHUNK])
        side = p.sb("rt_side", [P, 2, CHUNK])
        delta = p.sb("rt_delta", [P, CHUNK])
        powers = p.sb("rt_powers", [P, 2, 5])
        power_i = p.sb("rt_power_i", [P, 2, 5], I32)
        delta_i = p.sb("rt_delta_i", [P, CHUNK], I32)
        dec = p.sb("rt_dec", [P, 2, 5])
        dec_all = p.sb("rt_dec_all", [P, HEADS, 2, 5])
        mask_all = p.sb("rt_mask_all", [P, HEADS, 2, CHUNK])
        mask = p.sb("rt_mask", [P, CHUNK])
        raw_all = p.sb("rt_raw_all", [P, 2, HEADS])
        lg = p.sb("rt_lg", [P, 2, HEADS])
        small = [p.sb(f"rt_small{n}", [P, 2, HEADS]) for n in range(6)]
        square = p.sb("rt_square", [P, DK])
        sums = p.sb("rt_sums", [P, NC_])
        rstd = p.sb("rt_rstd", [P, NC_])
        scratch = [p.sb(f"rt_scratch{n}", [P, NC_]) for n in range(3)]

        work = [p.ps(f"rt_work{b}", [P, HALF]) for b in range(2)]
        upd = [p.ps(f"rt_upd{d}", [P, 2, DK]) for d in range(2)]
        cross = [[p.ps(f"rt_cross{d}{b}", [P, DK]) for b in range(2)] for d in range(2)]

        tables_loaded = p.sem("rt_tables_loaded")
        made = p.sem("rt_made")
        decay_loaded = p.sem("rt_decay_loaded")
        q_loaded, k_loaded, kc_loaded, vc_loaded, v_loaded, g_loaded = (
            p.sem(f"rt_{x}_loaded") for x in ("q", "k", "kc", "vc", "v", "g"))
        q_rotated = p.sem("rt_q_rotated")
        k_rotated = p.sem("rt_k_rotated")
        pool_chain = p.sem("rt_pool_chain")
        dve_chain = p.sem("rt_dve_chain")
        lg_exp = p.sem("rt_lg_exp")
        lg_asked = p.sem("rt_lg_asked")
        lg_ready = p.sem("rt_lg_ready")
        decays = p.sem("rt_decays")
        kc_scaled = p.sem("rt_kc_scaled")
        ctx_done = p.sem("rt_ctx_done")
        state_set = p.sem("rt_state_set")
        kt_done, kt_read = p.sem("rt_kt_done"), p.sem("rt_kt_read")
        sc_done, sc_read = p.sem("rt_sc_done"), p.sem("rt_sc_read")
        in_done, in_read = p.sem("rt_in_done"), p.sem("rt_in_read")
        yt_done, yt_read = p.sem("rt_yt_done"), p.sem("rt_yt_read")
        stepped = p.sem("rt_stepped")
        advanced = p.sem("rt_advanced")
        y_summed = p.sem("rt_y_summed")
        squared = p.sem("rt_squared")
        root_asked = p.sem("rt_root_asked")
        root_ready = p.sem("rt_root_ready")
        silu_ready = p.sem("rt_silu_ready")
        gated = p.sem("rt_gated")
        high = p.sem("rt_high")
        low = p.sem("rt_low")

        block = ctx.enter_context(nc.Block())

        @block.sync
        def _(sp):
            sp.sem_inc(q_rotated, 1)
            sp.dma_start(raw_all[:].rearrange("p d h -> p (d h)"),
                         decay_raw.rearrange("(o d) h -> o (d h)", o=1).to_broadcast([P, 2 * HEADS])).then_inc(decay_loaded, 16)
            sp.dma_start(cs[:], cos_sin).then_inc(tables_loaded, 16)
            with sp.Fori(0, HEADS, 1) as i:
                q_row, k_row = sp.snap(i * DK + Q_ROW), sp.snap(i * DK + K_ROW)
                v_head, g_head = sp.snap(i * 1), sp.snap(i + HEADS)
                sp.wait_ge(q_rotated, i + 1)
                sp.dma_start(q_raw[:], fm[bass.ds(q_row, DK), :].rearrange("(j p) t -> p j t", p=P)).then_inc(q_loaded, 16)
                sp.wait_ge(k_rotated, i + 1)
                sp.dma_start(k_raw[:], fm[bass.ds(k_row, DK), :].rearrange("(j p) t -> p j t", p=P)).then_inc(k_loaded, 16)
                sp.wait_ge(ctx_done, i + 1)
                sp.dma_start(kc[:], ctx_kv[bass.ds(i, 1)].rearrange("o (c p) d -> p (o c) d", p=P)).then_inc(kc_loaded, 16)
                sp.dma_start(vc[:], ctx_kv[bass.ds(g_head, 1)].rearrange("o (c p) d -> p (o c) d", p=P)).then_inc(vc_loaded, 16)
                sp.wait_ge(stepped, i * 16 + 16)
                sp.dma_start(v[:], tm[bass.ds(i, 1)].rearrange("o (c p) d -> p (o c) d", p=P)).then_inc(v_loaded, 16)
                sp.wait_ge(gated, NC_ * i + NC_)
                sp.dma_start(gate[:], tm[bass.ds(g_head, 1)].rearrange("o (c p) d -> p (o c) d", p=P)).then_inc(g_loaded, 16)

        @block.gpsimd
        def _(pool):
            g = nc.gpsimd
            pool.sem_inc(k_rotated, 1)
            for d, cols in enumerate((((1, 1), (-1, CHUNK - 1), (0, CHUNK), (-1, CTX - 1), (-1, CTX - 1 - P)),
                                      ((-1, CHUNK), (1, 0), (0, CHUNK), (1, 0), (1, P)))):
                for c, (mult, base) in enumerate(cols):
                    g.iota(power_i[:, d, c:c + 1], pattern=[[0, 1]], base=base, channel_multiplier=mult)
            g.iota(delta_i[:], pattern=[[1, CHUNK]], base=0, channel_multiplier=-1).then_inc(made, 1)
            pool.wait_ge(tables_loaded, 16)
            with pool.Fori(0, HEADS, 1) as i:
                pool.wait_ge(k_loaded, 16 * i + 16)
                chain = Chain(pool, pool_chain, 0, ROTATE_STEPS, i)
                pool.wait_ge(sc_done, i * 2 + 2)
                rotate(g, chain, k, k_raw, cs, tmp_k, k_rotated)

        @block.scalar
        def _(act):
            s = nc.scalar
            act.wait_ge(lg_asked, 1)
            s.activation(small[1][:], small[0][:], ACT.Exp).then_inc(lg_exp, 1)
            act.wait_ge(lg_asked, 2)
            s.activation(small[3][:], small[2][:], ACT.Ln).then_inc(lg_exp, 1)
            act.wait_ge(lg_ready, 1)
            for head in range(HEADS):
                for d in range(2):
                    s.activation(dec_all[:, head, d, :], powers[:, d, :], ACT.Exp, scale=lg[:, d, head:head + 1])
                    last = s.activation(mask_all[:, head, d, :], dist[:, d, :], ACT.Exp, scale=lg[:, d, head:head + 1])
                last.then_inc(decays, 1)
            with act.Fori(0, HEADS, 1) as i:
                act.wait_ge(ctx_done, i + 2)
                for d in range(2):
                    last = s.activation(state[d][:], upd[d][:], ACT.Copy)
                last.then_inc(state_set, 1)
                for n in range(4):
                    act.wait_ge(in_done, 4 * i + n + 1)
                    s.activation(y[:, 2 * n:2 * n + 2, :].rearrange("p c d -> p (c d)"), work[n % 2][:], ACT.Copy).then_inc(in_read, 1)
                act.wait_ge(g_loaded, 16 * i + 16)
                s.activation(gate[:], gate[:], ACT.Silu).then_inc(silu_ready, 1)
                for n, c in enumerate(COMPLETED):
                    act.wait_ge(y_summed, NC_ * i + n + 1)
                    if n:
                        act.wait_ge(squared, NC_ * i + n)
                    s.activation(square[:], y[:, c, :], ACT.Square, accum_out=sums[:, c:c + 1]).then_inc(squared, 1)
                act.wait_ge(root_asked, i + 1)
                s.activation(scratch[1][:], scratch[2][:], ACT.Sqrt).then_inc(root_ready, 1)
                for n in range(4):
                    act.wait_ge(yt_read, 4 * i + 4 + n + 1)
                    s.activation(yg_hi[:, bass.ds(2 * i + n // 2, 1), (n % 2) * HALF:(n % 2 + 1) * HALF].rearrange("p o t -> p (o t)"),
                                 value[:, n % 2, :], ACT.Copy).then_inc(high, 1)

        @block.vector
        def _(dve):
            vv = nc.vector
            chain = Chain(dve, dve_chain)
            dve.wait_ge(made, 1)
            chain.step(vv.tensor_copy(powers[:], power_i[:]))
            chain.step(vv.tensor_copy(delta[:], delta_i[:]))
            chain.step(vv.tensor_scalar(dist[:, 0, :], delta[:], 0.0, None, ALU.max))
            chain.step(vv.tensor_scalar(dist[:, 1, :], delta[:], -1.0, 0.0, ALU.mult, ALU.max))
            chain.step(vv.tensor_scalar(side[:, 0, :], delta[:], 0.0, DK ** -0.5, ALU.is_ge, ALU.mult))
            chain.step(vv.tensor_scalar(side[:, 1, :], delta[:], 0.0, DK ** -0.5, ALU.is_le, ALU.mult))
            dve.wait_ge(tables_loaded, 16)
            dve.wait_ge(decay_loaded, 16)
            x, e, u, ln_u, um1, t5 = raw_all[:], small[1][:], small[2][:], small[3][:], small[4][:], small[5][:]
            chain.step(vv.tensor_scalar(um1, x, -1.0, None, ALU.mult))
            chain.step(vv.tensor_tensor(um1, x, um1, ALU.max))
            vv.tensor_scalar(small[0][:], um1, -1.0, None, ALU.mult).then_inc(lg_asked, 1)
            dve.wait_ge(lg_exp, 1)
            chain.step(vv.tensor_scalar(um1, e, 1.0, None, ALU.add))
            vv.tensor_copy(u, um1).then_inc(lg_asked, 1)
            dve.wait_ge(lg_exp, 2)
            chain.step(vv.tensor_scalar(um1, um1, 1.0, None, ALU.subtract))
            chain.step(vv.tensor_scalar(t5, um1, 0.0, None, ALU.is_equal))
            chain.step(vv.tensor_tensor(um1, um1, t5, ALU.add))
            chain.step(vv.tensor_tensor(ln_u, ln_u, t5, ALU.add))
            chain.step(vv.reciprocal(um1, um1))
            chain.step(vv.tensor_tensor(ln_u, ln_u, e, ALU.mult))
            chain.step(vv.tensor_tensor(ln_u, ln_u, um1, ALU.mult))
            chain.step(vv.tensor_scalar(t5, x, 0.0, None, ALU.max))
            chain.step(vv.tensor_tensor(t5, ln_u, t5, ALU.add))
            vv.tensor_scalar(lg[:], t5, -1.0, None, ALU.mult).then_inc(lg_ready, 1)
            for head in range(HEADS):
                dve.wait_ge(decays, head + 1)
                last = vv.tensor_tensor(mask_all[:, head], mask_all[:, head], side[:], ALU.mult)
            chain.step(last)
            vv.tensor_tensor(mask_all[:, :, 0, :], mask_all[:, :, 0, :], mask_all[:, :, 1, :], ALU.add)
            vv.tensor_scalar(dec_all[:, :, :, 1:2], dec_all[:, :, :, 1:2], DK ** -0.5, None, ALU.mult)
            chain.step(vv.tensor_scalar(dec_all[:, :, :, 3:5], dec_all[:, :, :, 3:5], DK ** -0.5, None, ALU.mult))
            setup = chain.taken
            PER_HEAD = 22
            with dve.Fori(0, HEADS, 1) as i:
                start = Chain(dve, dve_chain, setup, PER_HEAD, i)
                vv.tensor_copy(mask[:], mask_all[:, bass.ds(i, 1), 0, :].rearrange("p o n -> p (o n)"))
                start.step(vv.tensor_copy(dec[:].rearrange("p d n -> p (d n)"),
                                          dec_all[:, bass.ds(i, 1)].rearrange("p o d n -> p (o d n)")))
                dve.wait_ge(kc_loaded, 16 * i + 16)
                for d in range(2):
                    for c in range(CT):
                        last = vv.tensor_scalar(kcd[d][:, c, :], kc[:, c, :], dec[:, d, 3 + c:4 + c], None, ALU.mult)
                last.then_inc(kc_scaled, 1)
                dve.wait_ge(q_loaded, 16 * i + 16)
                rotate(vv, start, q, q_raw, cs, tmp_q, q_rotated)
                for n in range(4):
                    dve.wait_ge(kt_done, 4 * i + n + 1)
                    for d in range(2):
                        last = vv.tensor_scalar(kd[d][:, 2 * n:2 * n + 2, :].rearrange("p c d -> p (c d)"), work[n % 2][:],
                                                dec[:, d, 1:2], None, ALU.mult)
                    last.then_inc(kt_read, 1)
                for n in range(2):
                    dve.wait_ge(sc_done, 2 * i + 2 + n + 1)
                    vv.tensor_tensor(weights[:, 4 * n:4 * n + 4, :], work[n % 2][:].rearrange("p (c n) -> p c n", c=4),
                                     mask[:, None, :].to_broadcast([P, 4, CHUNK]), ALU.mult).then_inc(sc_read, 1)
                dve.wait_ge(state_set, i + 1)
                dve.wait_ge(in_read, 4 * i + 4)
                for st in range(NC_):
                    for d in range(2):
                        c = st if d == 0 else NC_ - 1 - st
                        dve.wait_ge(stepped, 16 * i + 16 + 2 * st + d + 1)
                        vv.scalar_tensor_tensor(out=state[d][:], in0=state[d][:], scalar=dec[:, d, 2:3], in1=upd[d][:],
                                                op0=ALU.mult, op1=ALU.add).then_inc(advanced, 1)
                        add = vv.scalar_tensor_tensor(out=y[:, c, :], in0=cross[d][st % 2][:], scalar=dec[:, d, 0:1],
                                                      in1=y[:, c, :], op0=ALU.mult, op1=ALU.add)
                        if st >= NC_ // 2:
                            add.then_inc(y_summed, 1)
                            dve.wait_ge(y_summed, NC_ * i + COMPLETED.index(c) + 1)
                        else:
                            start.step(add)
                dve.wait_ge(squared, NC_ * i + NC_)

                def act_sqrt(root, mean):
                    vv.tensor_copy(scratch[2][:], mean).then_inc(root_asked, 1)
                    dve.wait_ge(root_ready, i + 1)

                rsqrt_of_mean(nc, start, act_sqrt, rstd[:], sums[:], tuple(x[:] for x in scratch), DK)
                dve.wait_ge(silu_ready, i + 1)
                for c in range(NC_):
                    vv.scalar_tensor_tensor(out=y[:, c, :], in0=y[:, c, :], scalar=rstd[:, c:c + 1], in1=gate[:, c, :],
                                            op0=ALU.mult, op1=ALU.mult).then_inc(gated, 1)
                for n in range(4):
                    dve.wait_ge(yt_done, 4 * i + n + 1)
                    vv.tensor_copy(value[:, n % 2, :], work[n % 2][:]).then_inc(yt_read, 1)
                    dve.wait_ge(high, 4 * i + n + 1)
                    cols = (bass.ds(2 * i + n // 2, 1), slice((n % 2) * HALF, (n % 2 + 1) * HALF))
                    start.step(vv.tensor_tensor(yg_lo[:, cols[0], cols[1]].rearrange("p o t -> p (o t)"), value[:, n % 2, :],
                                                f32(yg_hi[:, cols[0], cols[1]].rearrange("p o t -> p (o t)")), ALU.subtract))
                assert start.taken == PER_HEAD, start.taken

        @block.tensor
        def _(pe):
            mm_ = nc.tensor.matmul
            pe.sem_inc(ctx_done, 1)
            pe.sem_inc(sc_done, 2)
            pe.sem_inc(stepped, 16)
            pe.sem_inc(gated, NC_)
            pe.sem_inc(yt_read, 4)
            with pe.Fori(0, HEADS, 1) as i:
                pe.wait_ge(kc_scaled, i + 1)
                pe.wait_ge(vc_loaded, 16 * i + 16)
                for d in range(2):
                    for j in range(2):
                        for c in range(CT):
                            mm = mm_(upd[d][:, j, :], kcd[d][:, c, j * P:(j + 1) * P], vc[:, c, :],
                                     start=(c == 0), stop=(c == CT - 1))
                mm.then_inc(ctx_done, 1)
                pe.wait_ge(k_rotated, i + 2)
                for n in range(4):
                    if n >= 2:
                        pe.wait_ge(kt_read, 4 * i + n - 1)
                    else:
                        pe.wait_ge(yt_read, 4 * i + 4)
                    for c in range(2):
                        for j in range(2):
                            tr = nc.tensor.transpose(work[n % 2][:, c * DK + j * P:c * DK + (j + 1) * P],
                                                     k[:, j, (2 * n + c) * CHUNK:(2 * n + c + 1) * CHUNK], ident)
                    tr.then_inc(kt_done, 1)
                pe.wait_ge(q_rotated, i + 2)
                for n in range(2):
                    pe.wait_ge(kt_read, 4 * i + n + 3)
                    for c in range(4):
                        cols = slice((4 * n + c) * CHUNK, (4 * n + c + 1) * CHUNK)
                        for j in range(2):
                            mm = mm_(work[n % 2][:, c * CHUNK:(c + 1) * CHUNK], k[:, j, cols], q[:, j, cols],
                                     start=(j == 0), stop=(j == 1))
                    mm.then_inc(sc_done, 1)
                pe.wait_ge(v_loaded, 16 * i + 16)
                for n in range(4):
                    if n < 2:
                        pe.wait_ge(sc_read, 2 * i + n + 1)
                    else:
                        pe.wait_ge(in_read, 4 * i + n - 1)
                    if n == 0:
                        pe.wait_ge(sc_read, 2 * i + 2)
                    for c in range(2):
                        mm = mm_(work[n % 2][:, c * DK:(c + 1) * DK], weights[:, 2 * n + c, :], v[:, 2 * n + c, :],
                                 start=True, stop=True)
                    mm.then_inc(in_done, 1)
                pe.wait_ge(state_set, i + 1)
                for st in range(NC_):
                    for d in range(2):
                        c = st if d == 0 else NC_ - 1 - st
                        if st:
                            pe.wait_ge(advanced, 16 * i + 2 * (st - 1) + d + 1)
                        for j in range(2):
                            mm_(cross[d][st % 2][:], q[:, j, c * CHUNK:(c + 1) * CHUNK], state[d][:, j, :],
                                start=(j == 0), stop=(j == 1))
                        for j in range(2):
                            mm = mm_(upd[d][:, j, :], kd[d][:, c, j * P:(j + 1) * P], v[:, c, :], start=True, stop=True)
                        mm.then_inc(stepped, 1)
                for n in range(4):
                    pe.wait_ge(gated, NC_ * i + NC_ + 4 * (n % 2) + 4)
                    if n >= 2:
                        pe.wait_ge(yt_read, 4 * i + 4 + n - 1)
                    for c in range(4):
                        tr = nc.tensor.transpose(work[n % 2][:, c * P:(c + 1) * P],
                                                 y[:, 4 * (n % 2) + c, (n // 2) * P:(n // 2 + 1) * P], ident)
                    tr.then_inc(yt_done, 1)


class Residual:

    def __init__(self, nc, p, name, y, base_dram, row, out_dram, base, square, again=False):
        self.nc, self.y, self.row, self.base, self.square, self.again = nc, y, row, base, square, again
        self.base_dram, self.out_dram = (x.rearrange("(t p) d -> p t d", p=P) for x in (base_dram, out_dram))
        columns = ("sums", "rstd", "mean", "root", "asked")
        self.col = [{c: p.sb(f"{name}_{c}{n}", [P, TT]) for c in columns} for n in range(2)]
        self.loaded = [p.sem(f"{name}_loaded{b}") for b in range(2)]
        self.summed = [p.sem(f"{name}_summed{n}") for n in range(2)]
        self.root_asked = [p.sem(f"{name}_root_asked{n}") for n in range(2)]
        self.root_ready = [p.sem(f"{name}_root_ready{n}") for n in range(2)]
        self.chained = p.sem(name + "_chained")
        self.weighted = p.sem(name + "_weighted")
        self.added = p.sem(name + "_added")
        self.stored = [p.sem(f"{name}_stored{b}") for b in range(2)]
        self.chain = None

    def load(self, sp, t):
        if t >= 2:
            sp.wait_ge(self.added, t - 1)
        sp.dma_start(self.base[t % 2], self.base_dram[:, t, :]).then_inc(self.loaded[t % 2], 16)

    def store(self, sp, t):
        sp.wait_ge(self.added, t + 1)
        sp.dma_start(self.out_dram[:, t, :], self.y[:, t, :]).then_inc(self.stored[t % 2], 16)

    def last_stores(self, sp):
        for b in range(2):
            sp.wait_ge(self.stored[b], 16 * (TT // 2))

    def sum_squares(self, act, t, n=0):
        if n:
            act.wait_ge(self.added, t + 1)
        if t + n:
            act.wait_ge(self.summed[0], t + n)
        if self.again and t + n > 1:
            act.wait_ge(self.summed[1], t + n - 1)
        self.nc.scalar.activation(self.square, self.y[:, t, :], ACT.Square,
                                  accum_out=self.col[n]["sums"][:, t:t + 1]).then_inc(self.summed[n], 1)

    def root(self, act, t, n=0):
        act.wait_ge(self.root_asked[n], t + 1)
        col = self.col[n]
        self.nc.scalar.activation(col["root"][:, t:t + 1], col["asked"][:, t:t + 1], ACT.Sqrt).then_inc(self.root_ready[n], 1)

    def rstd(self, dve, t, n):
        if self.chain is None:
            self.chain = Chain(dve, self.chained)
        col = {c: x[:, t:t + 1] for c, x in self.col[n].items()}
        dve.wait_ge(self.summed[n], t + 1)

        def act_sqrt(root, mean):
            self.nc.vector.tensor_copy(col["asked"], mean).then_inc(self.root_asked[n], 1)
            dve.wait_ge(self.root_ready[n], t + 1)

        rsqrt_of_mean(self.nc, self.chain, act_sqrt, col["rstd"], col["sums"], (col["mean"], col["root"], col["asked"]), D)
        return col["rstd"]

    def weigh(self, dve, t):
        rstd = self.rstd(dve, t, 0)
        self.nc.vector.scalar_tensor_tensor(out=self.y[:, t, :], in0=self.y[:, t, :], scalar=rstd, in1=self.row,
                                            op0=ALU.mult, op1=ALU.mult).then_inc(self.weighted, 1)

    def add(self, pool, t):
        pool.wait_ge(self.weighted, t + 1)
        pool.wait_ge(self.loaded[t % 2], 16 * (t // 2 + 1))
        self.nc.gpsimd.tensor_tensor(self.y[:, t, :], self.y[:, t, :], self.base[t % 2], ALU.add).then_inc(self.added, 1)

    def scale(self, dve, t):
        rstd = self.rstd(dve, t, 1)
        dve.wait_ge(self.stored[t % 2], 16 * (t // 2 + 1))
        self.nc.vector.tensor_scalar(self.y[:, t, :], self.y[:, t, :], rstd, None, ALU.mult)


def project(nc, name, w_blocks, n_blocks, a_hi, a_lo, token_major, gate_rows, result, add, residual=None):
    with ExitStack() as ctx:
        p = Pool(nc, ctx)
        RING = 4
        GROUPS = 8 * n_blocks
        raw = p.sb(name + "_raw", [P, KT * NB])
        w_hi = [p.sb(f"{name}_w_hi{b}", [P, KT * NB], F32R) for b in range(2)]
        w_lo = [p.sb(f"{name}_w_lo{b}", [P, KT * NB], F32R) for b in range(2)]
        first = FirstBlock(nc, p, name, raw, w_hi[0], w_lo[0])
        gate = p.sb(name + "_gate", [P, RING, HALF]) if gate_rows is not None else None
        bank = [p.ps(f"{name}_bank{b}", [P, HALF]) for b in range(RING)]
        raw_loaded = p.sem(name + "_raw_loaded")
        hi_ready = p.sem(name + "_hi_ready")
        lo_ready = p.sem(name + "_lo_ready")
        gate_loaded = [p.sem(f"{name}_gate_loaded{r}") for r in range(RING)]
        gate_ready = p.sem(name + "_gate_ready")
        group_done = p.sem(name + "_group_done")
        multiplied = p.sem(name + "_multiplied")
        evacuated = p.sem(name + "_evacuated")
        LAST = GROUPS - 8
        if residual:
            base = [p.sb(f"{name}_base{b}", [P, D])[:] for b in range(2)]
            finish = Residual(nc, p, name + "_finish", result, residual[0], residual[1], residual[2], base,
                              p.sb(name + "_square", [P, D])[:], again=True)
        block = ctx.enter_context(nc.Block())

        def place(g):
            blk, r = g // 8, g % 8
            if token_major:
                return result[:, r, blk * NB:(blk + 1) * NB]
            tile = blk * 4 + r // 2
            return result[:, tile, (r % 2) * HALF:(r % 2 + 1) * HALF]

        @block.sync
        def _(sp):
            sp.sem_inc(raw_loaded, 16)
            sp.sem_inc(hi_ready, 1)
            sp.sem_inc(lo_ready, 1)
            first.load(sp, w_blocks[0])
            for g in range(GROUPS):
                if g % 8 == 4 and g // 8 + 1 < n_blocks:
                    if g == 4:
                        first.wait_all(sp)
                    sp.wait_ge(lo_ready, g // 8 + 1)
                    sp.dma_start(raw[:], w_blocks[g // 8 + 1]).then_inc(raw_loaded, 16)
                if gate_rows is not None:
                    if g >= RING:
                        sp.wait_ge(evacuated, g - RING + 1)
                    tile, half = (g // 8) * 4 + g % 8 // 2, g % 2
                    sp.dma_start(gate[:, g % RING, :],
                                 gate_rows[tile * P:(tile + 1) * P, half * HALF:(half + 1) * HALF]).then_inc(gate_loaded[g % RING], 16)
            if residual:
                finish.load(sp, 0)
                finish.load(sp, 1)
                for t in range(TT):
                    finish.store(sp, t)
                    if t + 2 < TT:
                        finish.load(sp, t + 2)
                finish.last_stores(sp)

        @block.scalar
        def _(act):
            def high_part(blk):
                act.wait_ge(raw_loaded, 16 * (blk + 1))
                nc.scalar.activation(w_hi[blk % 2][:], raw[:], ACT.Copy).then_inc(hi_ready, 1)

            first.split_high(act)
            for g in range(GROUPS):
                if g % 8 == 6 and g // 8 + 1 < n_blocks:
                    high_part(g // 8 + 1)
                if gate_rows is not None:
                    act.wait_ge(gate_loaded[g % RING], 16 * (g // RING + 1))
                    nc.scalar.activation(gate[:, g % RING, :], gate[:, g % RING, :], ACT.Sigmoid).then_inc(gate_ready, 1)
                else:
                    act.wait_ge(group_done, g + 1)
                    nc.scalar.activation(place(g), bank[g % RING][:], ACT.Copy).then_inc(evacuated, 1)
                if residual and g >= LAST:
                    act.wait_ge(evacuated, g + 1)
                    finish.sum_squares(act, g - LAST)
                    finish.root(act, g - LAST)
                    if g > LAST:
                        finish.sum_squares(act, g - LAST - 1, 1)
                        finish.root(act, g - LAST - 1, 1)
            if residual:
                finish.sum_squares(act, TT - 1, 1)
                finish.root(act, TT - 1, 1)

        @block.gpsimd
        def _(pool):
            first.split_low(nc.gpsimd, pool, True)
            for blk in range(1, n_blocks):
                pool.wait_ge(hi_ready, blk + 1)
                nc.gpsimd.tensor_tensor(w_lo[blk % 2][:], raw[:], f32(w_hi[blk % 2][:]), ALU.subtract).then_inc(lo_ready, 1)
            if residual:
                for t in range(TT):
                    finish.add(pool, t)

        @block.vector
        def _(dve):
            first.split_low(nc.vector, dve, False)
            if residual:
                for t in range(TT):
                    finish.weigh(dve, t)
                    if t:
                        finish.scale(dve, t - 1)
                finish.scale(dve, TT - 1)
            if gate_rows is None:
                return
            for g in range(GROUPS):
                dve.wait_ge(group_done, g + 1)
                dve.wait_ge(gate_ready, g + 1)
                if add:
                    nc.vector.tensor_tensor(gate[:, g % RING, :], bank[g % RING][:], gate[:, g % RING, :], ALU.mult).then_inc(multiplied, 1)
                    dve.wait_ge(multiplied, g + 1)
                    nc.vector.tensor_tensor(place(g), place(g), gate[:, g % RING, :], ALU.add).then_inc(evacuated, 1)
                else:
                    nc.vector.tensor_tensor(place(g), bank[g % RING][:], gate[:, g % RING, :], ALU.mult).then_inc(evacuated, 1)

        @block.tensor
        def _(pe):
            for g in range(GROUPS):
                blk, r = g // 8, g % 8
                if r == 0:
                    pe.wait_ge(lo_ready, blk + 1)
                wh = w_hi[blk % 2][:].rearrange("p (k n) -> p k n", k=KT)
                wl = w_lo[blk % 2][:].rearrange("p (k n) -> p k n", k=KT)
                if g >= RING:
                    pe.wait_ge(evacuated, g - RING + 1)
                if token_major:
                    c = slice(r * P, (r + 1) * P)
                    pairs = [((a_hi[:, k, c], a_lo[:, k, c]), (wh[:, k, :], wl[:, k, :])) for k in range(KT)]
                else:
                    n = slice((r // 2) * P, (r // 2 + 1) * P)
                    c = slice((r % 2) * HALF, (r % 2 + 1) * HALF)
                    pairs = [((wh[:, k, n], wl[:, k, n]), (a_hi[:, k, c], a_lo[:, k, c])) for k in range(KT)]
                if g == 0:
                    split_matmuls(nc, bank[0][:], pairs, before=lambda k: first.wait(pe, k)).then_inc(group_done, 1)
                else:
                    split_matmuls(nc, bank[g % RING][:], pairs).then_inc(group_done, 1)


def split_tile(nc, name, x, hi, lo):
    with ExitStack() as ctx:
        p = Pool(nc, ctx)
        high = p.sem(name + "_high")
        low = p.sem(name + "_low")
        block = ctx.enter_context(nc.Block())

        @block.scalar
        def _(act):
            for k in range(KT):
                nc.scalar.activation(hi[:, k, :], x[:, k, :], ACT.Copy).then_inc(high, 1)

        @block.vector
        def _(dve):
            for k in range(KT):
                dve.wait_ge(high, k + 1)
                nc.vector.tensor_tensor(lo[:, k, :], x[:, k, :], f32(hi[:, k, :]), ALU.subtract)


def conv_norm(nc, conv, gain_cols, bias_cols, u_hi, u_lo, ones):
    with ExitStack() as ctx:
        p = Pool(nc, ctx)
        x = p.sb("cn_x", [P, KT, SEQ])
        square = p.sb("cn_square", [P, 2, SEQ])
        var = p.sb("cn_var", [P, SEQ])
        root = p.sb("cn_root", [P, SEQ])
        rstd = p.sb("cn_rstd", [P, SEQ])
        gain = p.sb("cn_gain", [P, KT])
        bias = p.sb("cn_bias", [P, KT])
        mean_bank = [p.ps(f"cn_mean{h}", [P, HALF]) for h in range(2)]
        var_bank = [p.ps(f"cn_var_bank{h}", [P, HALF]) for h in range(2)]
        loaded = [p.sem(f"cn_loaded{k}") for k in range(KT)]
        cols_loaded = p.sem("cn_cols_loaded")
        tiles_added = p.sem("cn_tiles_added")
        mean_done = p.sem("cn_mean_done")
        centred = p.sem("cn_centred")
        squared = p.sem("cn_squared")
        var_done = p.sem("cn_var_done")
        square_read = p.sem("cn_square_read")
        root_asked = p.sem("cn_root_asked")
        root_ready = p.sem("cn_root_ready")
        chained = p.sem("cn_chained")
        scaled = p.sem("cn_scaled")
        silued = p.sem("cn_silued")
        high = p.sem("cn_high")
        ON_POOL = (0, 2, 4, 6)
        block = ctx.enter_context(nc.Block())

        @block.sync
        def _(sp):
            for k in range(KT):
                sp.dma_start(x[:, k, :], conv[k * P:(k + 1) * P, :]).then_inc(loaded[k], 16)
            sp.dma_start(gain[:], gain_cols).then_inc(cols_loaded, 16)
            sp.dma_start(bias[:], bias_cols).then_inc(cols_loaded, 16)

        @block.tensor
        def _(pe):
            pe.wait_ge(tiles_added, 1)
            for h in range(2):
                mm = nc.tensor.matmul(mean_bank[h][:], ones, var[:, h * HALF:(h + 1) * HALF], start=True, stop=True)
            mm.then_inc(mean_done, 1)
            for k in range(KT):
                pe.wait_ge(squared, k + 1)
                for h in range(2):
                    mm = nc.tensor.matmul(var_bank[h][:], ones, square[:, k % 2, h * HALF:(h + 1) * HALF],
                                          start=(k == 0), stop=(k == KT - 1))
                mm.then_inc(square_read, 1)

        @block.vector
        def _(dve):
            v = nc.vector
            chain = Chain(dve, chained)
            for k in range(KT):
                dve.wait_ge(loaded[k], 16)
                if k:
                    added = v.tensor_tensor(var[:], x[:, 0, :] if k == 1 else var[:], x[:, k, :], ALU.add)
                if 0 < k < KT - 1:
                    chain.step(added)
            added.then_inc(tiles_added, 1)
            dve.wait_ge(mean_done, 1)
            for k in range(KT):
                for h in range(2):
                    cols = slice(h * HALF, (h + 1) * HALF)
                    v.scalar_tensor_tensor(out=x[:, k, cols], in0=mean_bank[h][:], scalar=-1.0 / D, in1=x[:, k, cols],
                                           op0=ALU.mult, op1=ALU.add).then_inc(centred, 1)
            dve.wait_ge(square_read, KT)
            for h in range(2):
                chain.step(v.tensor_scalar(var[:, h * HALF:(h + 1) * HALF], var_bank[h][:], 1.0 / D, EPS, ALU.mult, ALU.add))
            v.tensor_copy(rstd[:, 0:1], var[:, 0:1]).then_inc(root_asked, 1)
            dve.wait_ge(root_ready, 1)
            chain.step(v.reciprocal(rstd[:], root[:]))
            chain.step(v.tensor_tensor(root[:], rstd[:], rstd[:], ALU.mult))
            chain.step(v.tensor_tensor(root[:], root[:], var[:], ALU.mult))
            chain.step(v.tensor_scalar(root[:], root[:], -0.5, 1.5, ALU.mult, ALU.add))
            chain.step(v.tensor_tensor(rstd[:], rstd[:], root[:], ALU.mult))
            for k in range(KT):
                v.tensor_tensor(x[:, k, :], x[:, k, :], rstd[:], ALU.mult).then_inc(scaled, 1)
            for k in range(KT):
                if k not in ON_POOL:
                    dve.wait_ge(high, k + 1)
                    v.tensor_tensor(u_lo[:, k, :], x[:, k, :], f32(u_hi[:, k, :]), ALU.subtract)

        @block.gpsimd
        def _(pool):
            for k in ON_POOL:
                pool.wait_ge(high, k + 1)
                nc.gpsimd.tensor_tensor(u_lo[:, k, :], x[:, k, :], f32(u_hi[:, k, :]), ALU.subtract)

        @block.scalar
        def _(act):
            s = nc.scalar
            for k in range(KT):
                act.wait_ge(centred, 2 * (k + 1))
                if k >= 2:
                    act.wait_ge(square_read, k - 1)
                s.activation(square[:, k % 2, :], x[:, k, :], ACT.Square).then_inc(squared, 1)
            act.wait_ge(root_asked, 1)
            s.activation(root[:], var[:], ACT.Sqrt).then_inc(root_ready, 1)
            act.wait_ge(cols_loaded, 32)
            for k in range(KT):
                act.wait_ge(scaled, k + 1)
                s.activation(x[:, k, :], x[:, k, :], ACT.Silu, bias=bias[:, k:k + 1], scale=gain[:, k:k + 1]).then_inc(silued, 1)
                act.wait_ge(silued, k + 1)
                s.activation(u_hi[:, k, :], x[:, k, :], ACT.Copy).then_inc(high, 1)

PEER_HEADS = 8
N_KEYS = 128
TOPK = 16
SIDES = 2 * PEER_HEADS
CAND = TOPK * TOPK
NEG = -3.0e38


def query_scores(nc, wq_blocks, keys, h_hi, h_lo, scores):
    with ExitStack() as ctx:
        p = Pool(nc, ctx)
        RING = 4
        BLKS = 4
        raw = p.sb("qs_raw", [P, KT * NB])
        w_hi = [p.sb(f"qs_w_hi{b}", [P, KT * NB], F32R) for b in range(2)]
        w_lo = [p.sb(f"qs_w_lo{b}", [P, KT * NB], F32R) for b in range(2)]
        first = FirstBlock(nc, p, "qs", raw, w_hi[0], w_lo[0])
        key = p.sb("qs_key", [P, SIDES, N_KEYS])
        q = p.sb("qs_q", [P, RING, HALF])
        stage = p.sb("qs_stage", [P, RING, 4, N_KEYS])
        q_bank = [p.ps(f"qs_q_bank{b}", [P, HALF]) for b in range(RING)]
        s_bank = [p.ps(f"qs_s_bank{b}", [P, 4, N_KEYS]) for b in range(RING)]
        keys_loaded = p.sem("qs_keys_loaded")
        raw_loaded = p.sem("qs_raw_loaded")
        hi_ready = p.sem("qs_hi_ready")
        lo_ready = p.sem("qs_lo_ready")
        q_done, q_read = p.sem("qs_q_done"), p.sem("qs_q_read")
        s_done, s_read = p.sem("qs_s_done"), p.sem("qs_s_read")
        stored = [p.sem(f"qs_stored{r}") for r in range(RING)]
        block = ctx.enter_context(nc.Block())

        @block.sync
        def _(sp):
            sp.sem_inc(raw_loaded, 16)
            sp.sem_inc(hi_ready, 1)
            sp.sem_inc(lo_ready, 1)
            first.load(sp, wq_blocks[0])
            sp.dma_start(key[:], keys).then_inc(keys_loaded, 16)
            for g in range(8 * BLKS):
                if g % 8 == 0 and g // 8 + 1 < BLKS:
                    if g == 0:
                        first.wait_all(sp)
                    sp.wait_ge(lo_ready, g // 8 + 1)
                    sp.dma_start(raw[:], wq_blocks[g // 8 + 1]).then_inc(raw_loaded, 16)
                side, half = g // 2, g % 2
                sp.wait_ge(s_read, g + 1)
                dst = scores.rearrange("(t p) (s n) -> s p t n", p=P, n=N_KEYS)[side, :, half * 4:half * 4 + 4, :]
                sp.dma_start(dst, stage[:, g % RING, :, :]).then_inc(stored[g % RING], 16)
            for r in range(RING):
                sp.wait_ge(stored[r], 16 * (8 * BLKS // RING))

        @block.scalar
        def _(act):
            def high_part(blk):
                act.wait_ge(raw_loaded, 16 * (blk + 1))
                nc.scalar.activation(w_hi[blk % 2][:], raw[:], ACT.Copy).then_inc(hi_ready, 1)

            first.split_high(act)
            for g in range(8 * BLKS):
                if g % 8 == 2 and g // 8 + 1 < BLKS:
                    high_part(g // 8 + 1)
                act.wait_ge(q_done, g + 1)
                if g >= RING:
                    act.wait_ge(s_done, g - RING + 1)
                nc.scalar.activation(q[:, g % RING, :], q_bank[g % RING][:], ACT.Copy).then_inc(q_read, 1)

        @block.gpsimd
        def _(pool):
            first.split_low(nc.gpsimd, pool, True)
            for blk in range(1, BLKS):
                pool.wait_ge(hi_ready, blk + 1)
                nc.gpsimd.tensor_tensor(w_lo[blk % 2][:], raw[:], f32(w_hi[blk % 2][:]), ALU.subtract).then_inc(lo_ready, 1)

        @block.vector
        def _(dve):
            first.split_low(nc.vector, dve, False)
            for g in range(8 * BLKS):
                dve.wait_ge(s_done, g + 1)
                if g >= RING:
                    dve.wait_ge(stored[g % RING], 16 * (g // RING))
                nc.vector.tensor_copy(stage[:, g % RING, :, :], s_bank[g % RING][:]).then_inc(s_read, 1)

        @block.tensor
        def _(pe):
            def score(g):
                side = g // 2
                pe.wait_ge(q_read, g + 1)
                if g >= RING:
                    pe.wait_ge(s_read, g - RING + 1)
                for t in range(4):
                    mm = nc.tensor.matmul(s_bank[g % RING][:, t, :], q[:, g % RING, t * P:(t + 1) * P], key[:, side, :],
                                          start=True, stop=True)
                mm.then_inc(s_done, 1)

            for g in range(8 * BLKS):
                blk, r = g // 8, g % 8
                if r == 0:
                    pe.wait_ge(lo_ready, blk + 1)
                wh = w_hi[blk % 2][:].rearrange("p (k n) -> p k n", k=KT)
                wl = w_lo[blk % 2][:].rearrange("p (k n) -> p k n", k=KT)
                if g >= RING:
                    pe.wait_ge(q_read, g - RING + 1)
                n = slice((r // 2) * P, (r // 2 + 1) * P)
                c = slice((r % 2) * HALF, (r % 2 + 1) * HALF)
                pairs = [((wh[:, k, n], wl[:, k, n]), (h_hi[:, k, c], h_lo[:, k, c])) for k in range(KT)]
                if g == 0:
                    split_matmuls(nc, q_bank[0][:], pairs, before=lambda k: first.wait(pe, k)).then_inc(q_done, 1)
                else:
                    split_matmuls(nc, q_bank[g % RING][:], pairs).then_inc(q_done, 1)
                if g == 1:
                    pe.wait_ge(keys_loaded, 16)
                if g:
                    score(g - 1)
            score(8 * BLKS - 1)

SPAN = 64
SLABS = SEQ // SPAN
EARLY_BESIDE_TOP = 40
EARLY_BESIDE_GATES = 48
EARLY = EARLY_BESIDE_TOP + EARLY_BESIDE_GATES
GELU = ACT.Gelu_apprx_tanh


class EarlyProducts:

    def __init__(self, nc, p, name, u_tiles, h, acts, first_tile, tiles, per_turn):
        self.nc, self.u_tiles, self.h, self.acts = nc, u_tiles, h, acts
        self.first_tile, self.tiles, self.per_turn = first_tile, tiles, per_turn
        self.u_raw = p.sb(name + "_u_raw", [P, KT, P])
        self.u_hi = [p.sb(f"{name}_u_hi{b}", [P, KT, P], F32R) for b in range(2)]
        self.u_lo = [p.sb(f"{name}_u_lo{b}", [P, KT, P], F32R) for b in range(2)]
        self.value = [p.sb(f"{name}_value{b}", [P, SEQ]) for b in range(2)]
        self.bank = [p.ps(f"{name}_bank{b}", [P, HALF]) for b in range(4)]
        self.u_loaded = p.sem(name + "_u_loaded")
        self.u_hi_ready = p.sem(name + "_u_hi_ready")
        self.u_lo_ready = p.sem(name + "_u_lo_ready")
        self.u_done = p.sem(name + "_u_done")
        self.gelu_done = p.sem(name + "_gelu_done")
        self.stored = [p.sem(f"{name}_stored{b}") for b in range(2)]

    def credit(self, sp):
        sp.sem_inc(self.u_lo_ready, 1)
        sp.sem_inc(self.u_done, 4)
        sp.sem_inc(self.gelu_done, 4)
        for b in range(2):
            sp.sem_inc(self.stored[b], 16)

    def tile(self, dram, n, i):
        at = i * self.per_turn + (self.first_tile + n)
        return dram[at:at + 1] if isinstance(i, int) else dram[bass.ds(at, 1)]

    def load_u(self, sp, n, i=0):
        sp.wait_ge(self.u_lo_ready, self.per_turn * i + n + 1)
        src = self.tile(self.u_tiles, n, i).rearrange("o p (k n) -> (o p) k n", k=KT)
        sp.dma_start(self.u_raw[:], src).then_inc(self.u_loaded, 16)

    def store(self, sp, n, i=0):
        sp.wait_ge(self.gelu_done, 2 * self.per_turn * i + 2 * n + 2 + 4)
        dst = self.tile(self.acts, n, i).rearrange("o p t -> (o p) t")
        sp.dma_start(dst, self.value[n % 2][:]).then_inc(self.stored[n % 2], 16)

    def last_stores(self, sp):
        for b in range(2):
            sp.wait_ge(self.stored[b], 16 * (self.tiles // 2 + 1))

    def high_u(self, act, n, i=0):
        act.wait_ge(self.u_loaded, 16 * self.per_turn * i + 16 * (n + 1))
        act.wait_ge(self.u_done, 2 * self.per_turn * i + 2 * n + 2)
        self.nc.scalar.activation(self.u_hi[n % 2][:], self.u_raw[:], ACT.Copy).then_inc(self.u_hi_ready, 1)

    def low_u(self, pool, n, i=0):
        pool.wait_ge(self.u_hi_ready, self.per_turn * i + n + 1)
        self.nc.gpsimd.tensor_tensor(self.u_lo[n % 2][:], self.u_raw[:], f32(self.u_hi[n % 2][:]),
                                     ALU.subtract).then_inc(self.u_lo_ready, 1)

    def product(self, pe, g, k, i=0):
        n, half, cols = g // 2, g % 2, slice((g % 2) * HALF, (g % 2 + 1) * HALF)
        if k == 0:
            pe.wait_ge(self.u_lo_ready, self.per_turn * i + n + 2)
            pe.wait_ge(self.gelu_done, 2 * self.per_turn * i + g + 1)
        mm, bank, (h_hi, h_lo) = self.nc.tensor.matmul, self.bank[g % 4], self.h
        mm(bank[:], self.u_hi[n % 2][:, k, :], h_hi[:, k, cols], start=(k == 0), stop=False)
        mm(bank[:], self.u_hi[n % 2][:, k, :], h_lo[:, k, cols], start=False, stop=False)
        last = mm(bank[:], self.u_lo[n % 2][:, k, :], h_hi[:, k, cols], start=False, stop=(k == KT - 1))
        if k == KT - 1:
            last.then_inc(self.u_done, 1)

    def gelu(self, act, g, i=0):
        n, half = g // 2, g % 2
        act.wait_ge(self.u_done, 2 * self.per_turn * i + g + 1 + 4)
        if half == 0:
            act.wait_ge(self.stored[n % 2], 8 * self.per_turn * i + 16 * (n // 2 + 1))
        self.nc.scalar.activation(self.value[n % 2][:, half * HALF:(half + 1) * HALF], self.bank[g % 4][:],
                                  GELU).then_inc(self.gelu_done, 1)


def top_experts(nc, scores, first_T, second_T, gate_T, ident, u_tiles, h, acts):
    PER_TOKENS = EARLY_BESIDE_TOP // TT
    BODY = 2 * PER_TOKENS
    BODIES = TT // 2
    with ExitStack() as ctx:
        p = Pool(nc, ctx)
        s = p.sb("te_s", [P, SIDES, N_KEYS])
        s2 = p.sb("te_s2", [P, SIDES, N_KEYS])
        top = p.sb("te_top", [P, SIDES, TOPK])
        top_i = p.sb("te_top_i", [P, SIDES, TOPK], U32)
        top_f = p.sb("te_top_f", [P, SIDES, TOPK])
        cand = p.sb("te_cand", [P, PEER_HEADS, CAND])
        cand2 = p.sb("te_cand2", [P, PEER_HEADS, CAND])
        best = p.sb("te_best", [P, PEER_HEADS, TOPK])
        sel = p.sb("te_sel", [P, PEER_HEADS * TOPK], U32)
        part_i = p.sb("te_part_i", [P, 2, PEER_HEADS * TOPK], U32)
        part = p.sb("te_part", [P, 2, PEER_HEADS * TOPK])
        hit = [p.sb(f"te_hit{d}", [P, PEER_HEADS * TOPK, TOPK]) for d in range(2)]
        found = p.sb("te_found", [P, 3, PEER_HEADS * TOPK])
        shifted = p.sb("te_shifted", [P, PEER_HEADS, TOPK])
        sums = p.sb("te_sums", [P, PEER_HEADS])
        ranks_i = p.sb("te_ranks_i", [P, TOPK], I32)
        ranks = p.sb("te_ranks", [P, TOPK])
        pad = p.sb("te_pad", [P, 1])
        bank = p.ps("te_bank", [P, 3, P])
        loaded = p.sem("te_loaded")
        made = p.sem("te_made")
        chain_sem = p.sem("te_chain")
        keys_taken = p.sem("te_keys_taken")
        exp_asked = p.sem("te_exp_asked")
        exp_ready = p.sem("te_exp_ready")
        parted = p.sem("te_parted")
        compared = p.sem("te_compared")
        second_hit = p.sem("te_second_hit")
        found_ready = p.sem("te_found_ready")
        turned = p.sem("te_turned")
        kept = p.sem("te_kept")
        early = EarlyProducts(nc, p, "te_early", u_tiles, h, acts, 0, EARLY_BESIDE_TOP, BODY)
        block = ctx.enter_context(nc.Block())

        def walk(eng, body):
            with eng.Fori(0, BODIES - 1, 1) as i:
                body(i, True)
            body(BODIES - 1, False)

        @block.sync
        def _(sp):
            early.credit(sp)
            s_rows = s[:].rearrange("p s n -> p (s n)")
            sp.dma_start(s_rows, scores[0:P, :]).then_inc(loaded, 16)
            early.load_u(sp, 0)
            early.load_u(sp, 1)

            def body(i, more):
                rows = []
                for t in range(2):
                    at = i * (2 * P) + (t + 1) * P
                    rows.append(slice(at, at + P) if isinstance(i, int) else bass.ds(sp.snap(at), P))
                for n in range(BODY):
                    if more or n + 2 < BODY:
                        early.load_u(sp, n + 2, i)
                    early.store(sp, n, i)
                    t = n // PER_TOKENS
                    if n % PER_TOKENS == 2 and (more or t == 0):
                        sp.wait_ge(keys_taken, 2 * i + t + 1)
                        sp.dma_start(s_rows, scores[rows[t], :]).then_inc(loaded, 16)

            walk(sp, body)
            early.last_stores(sp)

        def compare(side):
            pt = part[:, side, :]
            return nc.vector.tensor_tensor(hit[side][:], pt[:, :, None].to_broadcast([P, PEER_HEADS * TOPK, TOPK]),
                                           ranks[:, None, :].to_broadcast([P, PEER_HEADS * TOPK, TOPK]), ALU.is_equal)

        def weigh(engine, side):
            idx = top_f[:].rearrange("p (h e) k -> p h e k", e=2)[:, :, side, :]
            view = hit[side][:].rearrange("p (h k) a -> p h k a", h=PEER_HEADS)
            return engine.tensor_tensor(view, view, idx[:, :, None, :].to_broadcast([P, PEER_HEADS, TOPK, TOPK]), ALU.mult)

        @block.gpsimd
        def _(pool):
            nc.gpsimd.iota(ranks_i[:], pattern=[[1, TOPK]], base=0, channel_multiplier=0).then_inc(made, 1)
            pool.wait_ge(made, 1)
            nc.gpsimd.tensor_copy(ranks[:], ranks_i[:]).then_inc(made, 1)
            pool.wait_ge(made, 2)
            early.low_u(pool, 0)
            early.low_u(pool, 1)

            def body(i, more):
                for n in range(BODY):
                    if more or n + 2 < BODY:
                        early.low_u(pool, n + 2, i)
                    if n % PER_TOKENS == 3:
                        pool.wait_ge(compared, 2 * i + n // PER_TOKENS + 1)
                        weigh(nc.gpsimd, 1).then_inc(second_hit, 1)

            walk(pool, body)

        @block.scalar
        def _(act):
            act.sem_inc(kept, 1)
            early.high_u(act, 0)
            early.high_u(act, 1)

            def body(i, more):
                for n in range(BODY):
                    t = n // PER_TOKENS
                    early.gelu(act, 2 * n, i)
                    early.gelu(act, 2 * n + 1, i)
                    if more or n + 2 < BODY:
                        early.high_u(act, n + 2, i)
                    if n % PER_TOKENS == 3:
                        act.wait_ge(exp_asked, 2 * i + t + 1)
                        nc.scalar.activation(shifted[:], shifted[:], ACT.Exp).then_inc(exp_ready, 1)
                    if n % PER_TOKENS == 4:
                        act.wait_ge(turned, 2 * i + t + 1)
                        for m, dst in enumerate((first_T, second_T, gate_T)):
                            at = i * (2 * P) + t * P
                            cols = slice(at, at + P) if isinstance(i, int) else bass.ds(at, P)
                            copied = nc.scalar.activation(dst[:, cols], bank[:, m, :], ACT.Copy)
                        copied.then_inc(kept, 1)

            walk(act, body)

        @block.tensor
        def _(pe):
            with pe.Fori(0, BODIES, 1) as i:
                for n in range(BODY):
                    for half in range(2):
                        for k in range(KT):
                            early.product(pe, 2 * n + half, k, i)
                    if n % PER_TOKENS == PER_TOKENS - 1:
                        t = n // PER_TOKENS
                        pe.wait_ge(found_ready, 2 * i + t + 1)
                        pe.wait_ge(kept, 2 * i + t + 1)
                        for m in range(3):
                            tr = nc.tensor.transpose(bank[:, m, :], found[:, m, :], ident)
                        tr.then_inc(turned, 1)

        @block.vector
        def _(dve):
            v = nc.vector
            STEPS = 13
            dve.wait_ge(made, 2)

            def take_wait():
                v.memset(pad[:], 0.0)

            with dve.Fori(0, TT, 1) as i:
                chain = Chain(dve, chain_sem, 0, STEPS, i)
                dve.wait_ge(loaded, 16 * i + 16)
                take_wait()
                for c in range(SIDES):
                    last = v.max(top[:, c, 0:8], s[:, c, :])
                chain.step(last)
                take_wait()
                for c in range(SIDES):
                    last = v.match_replace(s2[:, c, :], top[:, c, 0:8], s[:, c, :], NEG)
                chain.step(last)
                take_wait()
                for c in range(SIDES):
                    last = v.max(top[:, c, 8:16], s2[:, c, :])
                chain.step(last)
                take_wait()
                for c in range(SIDES):
                    v.max_index(top_i[:, c, 8:16], top[:, c, 8:16], s2[:, c, :])
                    last = v.max_index(top_i[:, c, 0:8], top[:, c, 0:8], s[:, c, :])
                last.then_inc(keys_taken, 1)
                dve.wait_ge(keys_taken, i + 1)
                v.tensor_copy(top_f[:], top_i[:])
                pairs = top[:].rearrange("p (h e) k -> p h e k", e=2)
                chain.step(v.tensor_tensor(cand[:].rearrange("p h (a b) -> p h a b", a=TOPK),
                                           pairs[:, :, 0, :, None].to_broadcast([P, PEER_HEADS, TOPK, TOPK]),
                                           pairs[:, :, 1, None, :].to_broadcast([P, PEER_HEADS, TOPK, TOPK]), ALU.add))
                take_wait()
                for h in range(PEER_HEADS):
                    last = v.max(best[:, h, 0:8], cand[:, h, :])
                chain.step(last)
                take_wait()
                for h in range(PEER_HEADS):
                    last = v.match_replace(cand2[:, h, :], best[:, h, 0:8], cand[:, h, :], NEG)
                chain.step(last)
                take_wait()
                for h in range(PEER_HEADS):
                    last = v.max(best[:, h, 8:16], cand2[:, h, :])
                chain.step(last)
                v.tensor_tensor(shifted[:], best[:], best[:, :, 0:1].to_broadcast([P, PEER_HEADS, TOPK]),
                                ALU.subtract).then_inc(exp_asked, 1)
                for h in range(PEER_HEADS):
                    v.max_index(sel[:, h * TOPK + 8:h * TOPK + 16], best[:, h, 8:16], cand2[:, h, :])
                    last = v.max_index(sel[:, h * TOPK:h * TOPK + 8], best[:, h, 0:8], cand[:, h, :])
                chain.step(last)
                v.tensor_scalar(part_i[:, 0, :], sel[:], 4, None, ALU.logical_shift_right)
                chain.step(v.tensor_scalar(part_i[:, 1, :], sel[:], TOPK - 1, None, ALU.bitwise_and))
                v.tensor_copy(part[:], part_i[:]).then_inc(parted, 1)
                dve.wait_ge(parted, i + 1)
                compare(1).then_inc(compared, 1)
                chain.step(compare(0))
                chain.step(weigh(v, 0))
                dve.wait_ge(kept, i + 1)
                v.tensor_reduce(found[:, 0, :], hit[0][:], AX.X, ALU.add)
                dve.wait_ge(second_hit, i + 1)
                v.tensor_reduce(found[:, 1, :], hit[1][:], AX.X, ALU.add)
                dve.wait_ge(exp_ready, i + 1)
                chain.step(v.tensor_reduce(sums[:], shifted[:], AX.X, ALU.add))
                chain.step(v.reciprocal(sums[:], sums[:]))
                v.tensor_tensor(found[:, 2, :].rearrange("p (h k) -> p h k", h=PEER_HEADS), shifted[:],
                                sums[:, :, None].to_broadcast([P, PEER_HEADS, TOPK]), ALU.mult).then_inc(found_ready, 1)
                assert chain.taken == STEPS, chain.taken


def gate_matrix(nc, first_T, second_T, gate_T, g_dram, u_tiles, h, acts):
    TURN = 8
    QUAD = 4
    QUADS = TURN // QUAD
    PER_SLAB = SPAN // QUAD
    BODY = 2 * SPAN // TURN
    BODIES = SLABS // 2
    TILES = EARLY_BESIDE_GATES // BODIES
    UNITS = 2 * KT * TILES

    def turn_of(unit):
        return unit * (BODY - 2) // UNITS
    with ExitStack() as ctx:
        p = Pool(nc, ctx)
        iota_i = p.sb("gm_iota_i", [P, P], I32)
        iota = p.sb("gm_iota", [P, P])
        weight_hi = p.sb("gm_weight_hi", [P, SEQ], F32R)
        weight_lo = gate_T
        hot_i = [p.sb(f"gm_hot_i{b}", [P, TURN, P], BF16) for b in range(2)]
        hot_j = [p.sb(f"gm_hot_j{b}", [P, TURN, P], F32R) for b in range(2)]
        hot_w = [p.sb(f"gm_hot_w{b}", [P, TURN, 2, P], F32R) for b in range(2)]
        slab = [p.sb(f"gm_slab{b}", [P, P, SPAN]) for b in range(2)]
        bank = [p.ps(f"gm_bank{b}", [P, QUAD, 2, P]) for b in range(2)]
        made = p.sem("gm_made")
        weights_ready = p.sem("gm_weights_ready")
        i_ready = p.sem("gm_i_ready")
        hi_ready = p.sem("gm_hi_ready")
        lo_ready = p.sem("gm_lo_ready")
        quad_done = p.sem("gm_quad_done")
        high_kept = p.sem("gm_high_kept")
        quad_read = p.sem("gm_quad_read")
        stored = [p.sem(f"gm_stored{b}") for b in range(2)]
        early = EarlyProducts(nc, p, "gm_early", u_tiles, h, acts, EARLY_BESIDE_TOP, EARLY_BESIDE_GATES, TILES)
        block = ctx.enter_context(nc.Block())

        def walk(eng, body):
            with eng.Fori(0, BODIES - 1, 1) as i:
                body(i, True)
            body(BODIES - 1, False)

        def rows_of(x, t0):
            return x[:, bass.ds(t0, TURN)][:, :, None].to_broadcast([P, TURN, P])

        iota_rows = iota[:, None, :].to_broadcast([P, TURN, P])

        @block.sync
        def _(sp):
            early.credit(sp)
            early.load_u(sp, 0)
            early.load_u(sp, 1)

            def body(i, more):
                for b in range(2):
                    for n in range(b * TILES // 2, (b + 1) * TILES // 2):
                        if more or n + 2 < TILES:
                            early.load_u(sp, n + 2, i)
                        early.store(sp, n, i)
                    sp.wait_ge(quad_read, 2 * PER_SLAB * i + (b + 1) * PER_SLAB + 2)
                    at = i * 2 + b
                    dst = g_dram[at:at + 1] if isinstance(i, int) else g_dram[bass.ds(at, 1)]
                    sp.dma_start(dst.rearrange("s j i t -> (s j) i t"), slab[b][:]).then_inc(stored[b], 16)

            walk(sp, body)
            early.last_stores(sp)
            for b in range(2):
                sp.wait_ge(stored[b], 16 * (BODIES + 1))

        @block.gpsimd
        def _(pool):
            pool.sem_inc(lo_ready, 2)
            nc.gpsimd.iota(iota_i[:], pattern=[[1, P]], base=0, channel_multiplier=0).then_inc(made, 1)
            pool.wait_ge(made, 1)
            nc.gpsimd.tensor_copy(iota[:], iota_i[:]).then_inc(made, 1)
            early.low_u(pool, 0)
            pool.wait_ge(weights_ready, 2)
            ends = [turn_of(2 * KT * (n + 1) - 1) for n in range(TILES)]

            def body(i, more):
                for turn in range(BODY):
                    b = turn % 2
                    pool.wait_ge(i_ready, BODY * i + turn + 1)
                    pool.wait_ge(quad_done, QUADS * BODY * i + QUADS * (turn + 1))
                    nc.gpsimd.tensor_tensor(hot_w[b][:, :, 1, :], hot_i[b][:], rows_of(weight_lo, i * (BODY * TURN) + turn * TURN),
                                            ALU.mult).then_inc(lo_ready, 1)
                    if turn == 1:
                        early.low_u(pool, 1, i)
                    if turn - 2 in ends[:-1] and (more or ends.index(turn - 2) + 2 < TILES):
                        early.low_u(pool, ends.index(turn - 2) + 2, i)

            walk(pool, body)

        @block.vector
        def _(dve):
            v = nc.vector
            dve.wait_ge(made, 2)
            dve.wait_ge(weights_ready, 1)
            v.tensor_tensor(weight_lo[:], weight_lo[:], f32(weight_hi[:]), ALU.subtract).then_inc(weights_ready, 1)
            dve.wait_ge(weights_ready, 2)

            def make(turn, i):
                b, t0 = turn % 2, i * (BODY * TURN) + turn * TURN
                dve.wait_ge(lo_ready, BODY * i + turn + 1)
                v.tensor_tensor(hot_i[b][:], rows_of(first_T, t0), iota_rows, ALU.is_equal).then_inc(i_ready, 1)
                dve.wait_ge(quad_done, QUADS * BODY * i + QUADS * (turn + 1))
                v.tensor_tensor(hot_j[b][:], rows_of(second_T, t0), iota_rows, ALU.is_equal)
                dve.wait_ge(i_ready, BODY * i + turn + 1)
                v.tensor_tensor(hot_w[b][:, :, 0, :], hot_i[b][:], rows_of(f32(weight_hi[:]), t0), ALU.mult).then_inc(hi_ready, 1)

            def gather(turn, i):
                b = 2 * turn // BODY
                for q in range(turn * QUADS, (turn + 1) * QUADS):
                    n = q % PER_SLAB
                    dve.wait_ge(high_kept, 2 * PER_SLAB * i + q + 1)
                    out = slab[b][:, :, n * QUAD:(n + 1) * QUAD].rearrange("p i t -> p t i")
                    v.tensor_tensor(out, bank[q % 2][:, :, 1, :], out, ALU.add).then_inc(quad_read, 1)

            def body(i, more):
                for turn in range(BODY):
                    if more or turn + 1 < BODY:
                        make(turn + 1, i)
                    gather(turn, i)

            make(0, 0)
            walk(dve, body)

        @block.scalar
        def _(act):
            for b in range(2):
                act.sem_inc(stored[b], 16)
            act.sem_inc(quad_read, 2)
            nc.scalar.activation(weight_hi[:], gate_T[:], ACT.Copy).then_inc(weights_ready, 1)
            early.high_u(act, 0)
            early.high_u(act, 1)

            def body(i, more):
                unit = 0
                for turn in range(BODY):
                    b = 2 * turn // BODY
                    if turn % (BODY // 2) == 0:
                        act.wait_ge(stored[b], 16 * i + 16)
                    for q in range(turn * QUADS, (turn + 1) * QUADS):
                        n = q % PER_SLAB
                        act.wait_ge(quad_done, 2 * PER_SLAB * i + q + 1 + 2 * QUADS)
                        nc.scalar.activation(slab[b][:, :, n * QUAD:(n + 1) * QUAD].rearrange("p i t -> p t i"),
                                             bank[q % 2][:, :, 0, :], ACT.Copy).then_inc(high_kept, 1)
                    while unit < UNITS and turn_of(unit) == turn:
                        unit += 1
                        if unit % KT == 0:
                            early.gelu(act, unit // KT - 1, i)
                        if unit % (2 * KT) == 0 and (more or unit // (2 * KT) + 1 < TILES):
                            early.high_u(act, unit // (2 * KT) + 1, i)

            walk(act, body)

        @block.tensor
        def _(pe):
            pe.sem_inc(quad_done, 2 * QUADS)
            with pe.Fori(0, BODIES, 1) as i:
                unit = 0
                for turn in range(BODY):
                    b = turn % 2
                    pe.wait_ge(hi_ready, BODY * i + turn + 1)
                    pe.wait_ge(lo_ready, BODY * i + turn + 1 + 2)
                    for n in range(QUADS):
                        q = turn * QUADS + n
                        pe.wait_ge(quad_read, i * (BODY * QUADS) + q + 1)
                        for c in range(QUAD):
                            t = n * QUAD + c
                            mm = nc.tensor.matmul(bank[q % 2][:, c, :, :], hot_j[b][:, t, :], hot_w[b][:, t, :, :], start=True, stop=True)
                        mm.then_inc(quad_done, 1)
                    while unit < UNITS and turn_of(unit) == turn:
                        early.product(pe, unit // KT, unit % KT, i)
                        unit += 1


class SecondProducts:

    def __init__(self, nc, p, name, acc):
        self.nc, self.acc = nc, acc
        self.v_hi = [p.sb(f"{name}_v_hi{b}", [P, D], F32R) for b in range(4)]
        self.v_lo = [p.sb(f"{name}_v_lo{b}", [P, D], F32R) for b in range(4)]
        self.w_hi = [p.sb(f"{name}_w_hi{b}", [P, SEQ], F32R) for b in range(4)]
        self.w_lo = [p.sb(f"{name}_w_lo{b}", [P, SEQ], F32R) for b in range(4)]
        self.bank = [p.ps(f"{name}_v_bank{b}", [P, HALF]) for b in range(4)]
        self.v_lo_ready = p.sem(name + "_v_lo_ready")
        self.w_lo_ready = p.sem(name + "_w_lo_ready")
        self.done = p.sem(name + "_v_done")
        self.added = p.sem(name + "_added")

    def product(self, pe, r, n, i):
        if n == 0:
            pe.wait_ge(self.w_lo_ready, 8 * i + 4 * r + 4 + 4)
            pe.wait_ge(self.v_lo_ready, 4 * i + 2 * r + 2 + 2)
        pe.wait_ge(self.added, 32 * i + 16 * r + n + 13)
        rows = slice((n // 2) * P, (n // 2 + 1) * P)
        cols = slice((n % 2) * HALF, (n % 2 + 1) * HALF)
        mm_, bank = self.nc.tensor.matmul, self.bank[n % 4][:]
        for c in range(2):
            b = (2 * r + c) % 4
            mm_(bank, self.w_hi[b][:, rows], self.v_hi[b][:, cols], start=(c == 0), stop=False)
            mm_(bank, self.w_hi[b][:, rows], self.v_lo[b][:, cols], start=False, stop=False)
            mm = mm_(bank, self.w_lo[b][:, rows], self.v_hi[b][:, cols], start=False, stop=(c == 1))
        mm.then_inc(self.done, 1)

    def add(self, dve, r, n, i):
        out = self.acc[:, n // 2, (n % 2) * HALF:(n % 2 + 1) * HALF]
        dve.wait_ge(self.done, 32 * i + 16 * r + n + 1 + 32)
        dve.wait_ge(self.added, 32 * i + 16 * r + n + 1)
        self.nc.vector.tensor_tensor(out, self.bank[n % 4][:], out, ALU.add).then_inc(self.added, 1)


def half_gates(g_dram, pair, half):
    slabs = slice(half * SLABS // 2, (half + 1) * SLABS // 2)
    at = slice(2 * pair, 2 * pair + 2) if isinstance(pair, int) else bass.ds(2 * pair, 2)
    return g_dram[slabs, :, at, :].rearrange("s j i t -> j s (i t)")


def early_experts(nc, acts, v_dram, g_dram, acc):
    PAIRS = EARLY // 2
    with ExitStack() as ctx:
        p = Pool(nc, ctx)
        sp_ = SecondProducts(nc, p, "ee", acc)
        v_raw = [p.sb(f"ee_v_raw{b}", [P, D]) for b in range(2)]
        value = [p.sb(f"ee_value{b}", [P, SEQ]) for b in range(2)]
        gates = p.sb("ee_gates", [P, SLABS, 2, SPAN])
        v_loaded, act_loaded = ([p.sem(f"ee_{x}_loaded{b}") for b in range(2)] for x in ("v", "act"))
        g_loaded = [p.sem(f"ee_g_loaded{half}") for half in range(2)]
        v_hi_ready, w_hi_ready = p.sem("ee_v_hi_ready"), p.sem("ee_w_hi_ready")
        gated = p.sem("ee_gated")
        block = ctx.enter_context(nc.Block())

        def walk(eng, visit):
            with eng.Fori(0, PAIRS // 2, 1) as i:
                visit(0, i)
                visit(1, i)

        @block.sync
        def _(sp):
            sp.sem_inc(sp_.v_lo_ready, 2)
            sp.sem_inc(sp_.w_lo_ready, 4)
            sp.sem_inc(gated, 4)

            def visit(r, i):
                pair = i * 2 + r
                for c in range(2):
                    e = 2 * r + c
                    sp.wait_ge(sp_.v_lo_ready, 4 * i + e + 1)
                    sp.dma_start(v_raw[c][:], v_dram[bass.ds(i * (4 * P) + e * P, P), :]).then_inc(v_loaded[c], 16)
                for c in range(2):
                    e = 2 * r + c
                    sp.wait_ge(gated, 8 * i + 4 * r + c + 3)
                    half = gates[:, c * SLABS // 2:(c + 1) * SLABS // 2].rearrange("p s i t -> p s (i t)")
                    sp.dma_start(half, half_gates(g_dram, pair, c)).then_inc(g_loaded[c], 16)
                    sp.wait_ge(sp_.w_lo_ready, 8 * i + 2 * e + 2)
                    sp.dma_start(value[c][:], acts[bass.ds(i * 4 + e, 1)].rearrange("o p t -> (o p) t")).then_inc(act_loaded[c], 16)

            walk(sp, visit)

        @block.scalar
        def _(act):
            s = nc.scalar

            def visit(r, i):
                for c in range(2):
                    e = 2 * r + c
                    act.wait_ge(sp_.done, 32 * i + 16 * (r + 1))
                    act.wait_ge(v_loaded[c], 32 * i + 16 * (r + 1))
                    s.activation(sp_.v_hi[e][:], v_raw[c][:], ACT.Copy).then_inc(v_hi_ready, 1)
                    for half in range(2):
                        cols = slice(half * HALF, (half + 1) * HALF)
                        act.wait_ge(gated, 8 * i + 2 * e + half + 1 + 4)
                        s.activation(sp_.w_hi[e][:, cols], value[c][:, cols], ACT.Copy).then_inc(w_hi_ready, 1)

            walk(act, visit)

        @block.gpsimd
        def _(pool):
            sub = nc.gpsimd.tensor_tensor

            def visit(r, i):
                for c in range(2):
                    e = 2 * r + c
                    pool.wait_ge(v_hi_ready, 4 * i + e + 1)
                    sub(sp_.v_lo[e][:], v_raw[c][:], f32(sp_.v_hi[e][:]), ALU.subtract).then_inc(sp_.v_lo_ready, 1)
                    for half in range(2):
                        cols = slice(half * HALF, (half + 1) * HALF)
                        pool.wait_ge(w_hi_ready, 8 * i + 2 * e + half + 1)
                        sub(sp_.w_lo[e][:, cols], value[c][:, cols], f32(sp_.w_hi[e][:, cols]),
                            ALU.subtract).then_inc(sp_.w_lo_ready, 1)

            walk(pool, visit)

        @block.vector
        def _(dve):
            dve.sem_inc(sp_.done, 32)
            nc.vector.memset(acc[:], 0.0).then_inc(sp_.added, 16)

            def gate(g, i):
                c, half = (g // 2) % 2, g % 2
                dve.wait_ge(act_loaded[c], 32 * i + 16 * (g // 4 + 1))
                dve.wait_ge(g_loaded[half], 32 * i + 16 * (g // 4 + 1))
                out = value[c][:, half * HALF:(half + 1) * HALF].rearrange("p (s t) -> p s t", t=SPAN)
                nc.vector.tensor_tensor(out, out, gates[:, half * SLABS // 2:(half + 1) * SLABS // 2, c, :],
                                        ALU.mult).then_inc(gated, 1)

            def visit(r, i, more=True):
                for n in range(16):
                    if n % 4 == 0 and more:
                        gate(4 * (r + 1) + n // 4, i)
                    sp_.add(dve, r, n, i)

            for g in range(4):
                gate(g, 0)
            with dve.Fori(0, PAIRS // 2 - 1, 1) as i:
                visit(0, i)
                visit(1, i)
            visit(0, PAIRS // 2 - 1)
            visit(1, PAIRS // 2 - 1, more=False)

        @block.tensor
        def _(pe):
            def visit(r, i):
                for n in range(16):
                    sp_.product(pe, r, n, i)

            walk(pe, visit)


def experts(nc, u_tiles, v_dram, g_dram, h_hi, h_lo, acc, base_dram, row, out_dram):
    PAIRS = (N_KEYS - EARLY) // 2
    LAG = 4
    with ExitStack() as ctx:
        p = Pool(nc, ctx)
        sp_ = SecondProducts(nc, p, "ex", acc)
        u_raw = p.sb("ex_u_raw", [P, KT, P])
        v_raw = p.sb("ex_v_raw", [P, D])
        u_hi = [p.sb(f"ex_u_hi{b}", [P, KT, P], F32R) for b in range(2)]
        u_lo = [p.sb(f"ex_u_lo{b}", [P, KT, P], F32R) for b in range(2)]
        gates = p.sb("ex_gates", [P, SLABS, 2, SPAN])
        value = p.sb("ex_value", [P, 2, HALF])
        u_bank = [p.ps(f"ex_u_bank{b}", [P, HALF]) for b in range(4)]
        u_loaded, v_loaded = p.sem("ex_u_loaded"), p.sem("ex_v_loaded")
        g_loaded = [p.sem(f"ex_g_loaded{half}") for half in range(2)]
        u_hi_ready, v_hi_ready = p.sem("ex_u_hi_ready"), p.sem("ex_v_hi_ready")
        u_lo_ready = p.sem("ex_u_lo_ready")
        u_done = p.sem("ex_u_done")
        gelu_done = p.sem("ex_gelu_done")
        gated = p.sem("ex_gated")
        w_hi_ready = p.sem("ex_w_hi_ready")
        finish = Residual(nc, p, "ex_finish", acc, base_dram, row, out_dram,
                          [u_raw[:].rearrange("p k n -> p (k n)"), v_raw[:]], value[:].rearrange("p a n -> p (a n)"))
        block = ctx.enter_context(nc.Block())

        def walk(eng, visit):
            visit(0, 0)
            visit(1, 0)
            with eng.Fori(0, (PAIRS - 4) // 2, 1) as i:
                visit(2, i)
                visit(3, i)
            visit(PAIRS - 2, 0)
            visit(PAIRS - 1, 0)

        def lagged(step, r, n, i):
            if n >= LAG and r >= 1:
                step(r - 1, n - LAG, i)
            elif n < LAG and r >= 2:
                step(r - 2, n - LAG + 16, i)

        def lagged_rest(step, then=None):
            for n in range(16 - LAG, 16):
                step(PAIRS - 2, n, 0)
            for n in range(16):
                step(PAIRS - 1, n, 0)
                if then is not None and n % 2 and n > 1:
                    then(n // 2 - 1)

        @block.sync
        def _(sp):
            sp.sem_inc(u_lo_ready, 1)
            sp.sem_inc(sp_.v_lo_ready, 2)
            sp.sem_inc(sp_.w_lo_ready, 4)

            def load_u(e, i):
                sp.wait_ge(u_lo_ready, 4 * i + e + 1)
                at = i * 4 + (EARLY + e)
                src = u_tiles[at:at + 1] if isinstance(i, int) else u_tiles[bass.ds(at, 1)]
                sp.dma_start(u_raw[:], src.rearrange("o p (k n) -> (o p) k n", k=KT)).then_inc(u_loaded, 16)

            def load_v(e, i):
                sp.wait_ge(sp_.v_lo_ready, 4 * i + e + 2)
                at = i * (4 * P) + (EARLY + e) * P
                src = v_dram[at:at + P, :] if isinstance(i, int) else v_dram[bass.ds(at, P), :]
                sp.dma_start(v_raw[:], src).then_inc(v_loaded, 16)

            def load_g(r, half, i):
                sp.wait_ge(gated, 8 * i + 4 * r + half + 3)
                place = gates[:, half * SLABS // 2:(half + 1) * SLABS // 2].rearrange("p s i t -> p s (i t)")
                sp.dma_start(place, half_gates(g_dram, i * 2 + (EARLY // 2 + r), half)).then_inc(g_loaded[half], 16)

            load_u(0, 0)
            load_u(1, 0)
            load_g(0, 0, 0)
            load_g(0, 1, 0)

            def visit(r, i):
                for e in (2 * r, 2 * r + 1):
                    load_v(e, i)
                    if r < PAIRS - 1:
                        load_u(e + 2, i)
                if r < PAIRS - 1:
                    load_g(r + 1, 0, i)
                    load_g(r + 1, 1, i)

            walk(sp, visit)
            sp.wait_ge(u_lo_ready, 2 * PAIRS + 1)
            finish.load(sp, 0)
            sp.wait_ge(sp_.v_lo_ready, 2 * PAIRS + 2)
            finish.load(sp, 1)
            for t in range(TT):
                finish.store(sp, t)
                if t + 2 < TT:
                    finish.load(sp, t + 2)
            finish.last_stores(sp)

        @block.scalar
        def _(act):
            s = nc.scalar
            act.sem_inc(gelu_done, 4)

            def high_u(e, i):
                act.wait_ge(u_loaded, 64 * i + 16 * (e + 1))
                act.wait_ge(u_done, 8 * i + 2 * e + 2)
                s.activation(u_hi[e % 2][:], u_raw[:], ACT.Copy).then_inc(u_hi_ready, 1)

            high_u(0, 0)
            high_u(1, 0)

            def visit(r, i):
                for e in (2 * r, 2 * r + 1):
                    for half in range(2):
                        g = 2 * e + half
                        act.wait_ge(u_done, 8 * i + g + 1 + 4)
                        act.wait_ge(sp_.w_lo_ready, 8 * i + g + 1 + 2)
                        s.activation(value[:, g % 2, :], u_bank[g % 4][:], ACT.Gelu_apprx_tanh).then_inc(gelu_done, 1)
                        act.wait_ge(gated, 8 * i + g + 1 + 4)
                        act.wait_ge(sp_.done, 32 * i + 16 * (r + 1))
                        s.activation(sp_.w_hi[e % 4][:, half * HALF:(half + 1) * HALF], value[:, g % 2, :], ACT.Copy).then_inc(w_hi_ready, 1)
                    if r < PAIRS - 1:
                        high_u(e + 2, i)
                    act.wait_ge(v_loaded, 64 * i + 16 * (e + 1))
                    s.activation(sp_.v_hi[e % 4][:], v_raw[:], ACT.Copy).then_inc(v_hi_ready, 1)

            walk(act, visit)
            act.wait_ge(sp_.w_lo_ready, 4 * PAIRS + 4)
            for t in range(TT):
                act.wait_ge(sp_.added, 16 * PAIRS + 2 * t + 2)
                finish.sum_squares(act, t)
                finish.root(act, t)

        @block.gpsimd
        def _(pool):
            g_ = nc.gpsimd

            def low_u(e, i):
                pool.wait_ge(u_hi_ready, 4 * i + e + 1)
                g_.tensor_tensor(u_lo[e % 2][:], u_raw[:], f32(u_hi[e % 2][:]), ALU.subtract).then_inc(u_lo_ready, 1)

            low_u(0, 0)
            low_u(1, 0)

            def visit(r, i):
                for e in (2 * r, 2 * r + 1):
                    for half in range(2):
                        g = 2 * e + half
                        cols = slice(half * HALF, (half + 1) * HALF)
                        pool.wait_ge(w_hi_ready, 8 * i + g + 1)
                        g_.tensor_tensor(sp_.w_lo[e % 4][:, cols], value[:, g % 2, :], f32(sp_.w_hi[e % 4][:, cols]),
                                         ALU.subtract).then_inc(sp_.w_lo_ready, 1)
                    if r < PAIRS - 1:
                        low_u(e + 2, i)
                    pool.wait_ge(v_hi_ready, 4 * i + e + 1)
                    g_.tensor_tensor(sp_.v_lo[e % 4][:], v_raw[:], f32(sp_.v_hi[e % 4][:]), ALU.subtract).then_inc(sp_.v_lo_ready, 1)

            walk(pool, visit)
            for t in range(TT):
                finish.add(pool, t)

        @block.vector
        def _(dve):
            v = nc.vector
            dve.sem_inc(gated, 4)
            dve.sem_inc(sp_.added, 16)

            def gate(g, i):
                e, half = g // 2, g % 2
                dve.wait_ge(gelu_done, 8 * i + g + 1 + 4)
                dve.wait_ge(g_loaded[half], 32 * i + 16 * (e // 2 + 1))
                out = value[:, g % 2, :].rearrange("p (s t) -> p s t", t=SPAN)
                v.tensor_tensor(out, out, gates[:, half * SLABS // 2:(half + 1) * SLABS // 2, e % 2, :],
                                ALU.mult).then_inc(gated, 1)

            def add(r, n, i):
                sp_.add(dve, r, n, i)

            def visit(r, i):
                for n in range(16):
                    lagged(add, r, n, i)
                    if n % 4 == 3:
                        gate(4 * r + n // 4, i)

            walk(dve, visit)
            lagged_rest(add, lambda t: finish.weigh(dve, t))
            finish.weigh(dve, TT - 1)

        @block.tensor
        def _(pe):
            pe.sem_inc(u_done, 4)
            pe.sem_inc(sp_.done, 32)
            mm_ = nc.tensor.matmul

            def first(r, n, i):
                e, half = 2 * r + n // 8, (n // 4) % 2
                g = 2 * e + half
                if n % 8 == 0:
                    pe.wait_ge(u_lo_ready, 4 * i + e + 2)
                if n % 4 == 0:
                    pe.wait_ge(gelu_done, 8 * i + g + 1)
                cols = slice(half * HALF, (half + 1) * HALF)
                uh, ul = u_hi[e % 2], u_lo[e % 2]
                for k in (2 * (n % 4), 2 * (n % 4) + 1):
                    mm_(u_bank[g % 4][:], uh[:, k, :], h_hi[:, k, cols], start=(k == 0), stop=False)
                    mm_(u_bank[g % 4][:], uh[:, k, :], h_lo[:, k, cols], start=False, stop=False)
                    mm = mm_(u_bank[g % 4][:], ul[:, k, :], h_hi[:, k, cols], start=False, stop=(k == KT - 1))
                if n % 4 == 3:
                    mm.then_inc(u_done, 1)

            def second(r, n, i):
                sp_.product(pe, r, n, i)

            def visit(r, i):
                for n in range(16):
                    first(r, n, i)
                    lagged(second, r, n, i)

            walk(pe, visit)
            lagged_rest(second)


def cols(v):
    v = v.reshape(-1, KT, P)
    return np.ascontiguousarray(v.transpose(2, 0, 1))


def column_blocks(w, width=NB):
    n = w.shape[1] // width
    return np.ascontiguousarray(w.reshape(KT, P, n, width).transpose(2, 1, 0, 3)).reshape(n, P, KT * width)


def rotary_tables():
    rows = np.repeat(np.arange(SEQ // GRID_W, dtype=np.float32), GRID_W)
    columns = np.tile(np.arange(GRID_W, dtype=np.float32), SEQ // GRID_W)
    quarter = DK // 4
    inv = (np.float32(10000.0) ** (-np.arange(quarter, dtype=np.float32) / np.float32(quarter))).astype(np.float32)
    ang = np.concatenate([rows[:, None] * inv, columns[:, None] * inv], axis=-1)
    return np.ascontiguousarray(np.stack([np.cos(ang).T, np.sin(ang).T], axis=1).astype(np.float32))


def layout(x, c, ctx, c_ctx, w_mod, b_mod, norm_gain, w_in, ret_decay_raw, w_ret_o, conv_w, conv_b,
           conv_norm_g, conv_norm_b, w_conv_o, w_out, peer_wq, peer_keys, peer_u, peer_v):
    return {
        "x": x[0], "ctx": ctx[0],
        "c_cols": np.ascontiguousarray(np.stack([c[0], c_ctx], -1).reshape(KT, P, 2).transpose(1, 0, 2)),
        "w_mod": column_blocks(w_mod[0]), "b_mod": cols(b_mod[0]), "gain": cols(norm_gain[0]),
        "w_in": np.ascontiguousarray(column_blocks(w_in[0])[W_IN_ORDER]),
        "decay": ret_decay_raw[0], "rotary": rotary_tables(),
        "w_ret_o": column_blocks(w_ret_o[0]), "w_conv_o": column_blocks(w_conv_o[0]), "w_out": column_blocks(w_out[0]),
        "conv_w": np.ascontiguousarray(conv_w[0].T.reshape(KT, P, CONV_W).transpose(1, 0, 2)),
        "w_query": column_blocks(peer_wq[0]),
        "keys": np.ascontiguousarray(peer_keys[0].reshape(SIDES, N_KEYS, P).transpose(2, 0, 1)),
        "u_tiles": np.ascontiguousarray(peer_u[0].reshape(N_KEYS, N_KEYS, KT, P).transpose(0, 3, 2, 1)).reshape(N_KEYS, P, D),
        "v": peer_v[0],
        "conv_b": cols(conv_b[0])[:, 0], "conv_norm_g": cols(conv_norm_g[0])[:, 0], "conv_norm_b": cols(conv_norm_b[0])[:, 0],
    }


def scratch(nc, name, shape):
    return nc.dram_tensor(name, shape, F32, kind="Internal").ap()


def mixer_program(nc, a, lat1, keep, ones, ident, mod, rows, x, cx, x_scope):
    fm = scratch(nc, "proj_fm", [FM_ROWS, SEQ])
    tm = scratch(nc, "proj_tm", [2 * HEADS, SEQ, DK])
    ctx_kv = scratch(nc, "ctx_kv", [2 * HEADS, CTX, DK])
    conv = scratch(nc, "conv_out", [D, SEQ])

    with ExitStack() as s:
        p = Pool(nc, s)
        h_hi, h_lo = p.sb("h_hi", [P, KT, SEQ], F32R), p.sb("h_lo", [P, KT, SEQ], F32R)
        hc_hi, hc_lo = p.sb("hc_hi", [P, KT, CTX], F32R), p.sb("hc_lo", [P, KT, CTX], F32R)
        groups = [(1, 0, CT, k, mod["ac"][:, k:k + 1], mod["bc"][:, k:k + 1], hc_hi[:, k, :], hc_lo[:, k, :])
                  for k in range(KT)]
        groups += latent_groups(mod["a1"], mod["b1"], h_hi, h_lo)
        normalise(nc, "n1", [(x[:], None), (cx[:], None)], groups, ident, is_scaled=True)
        x_scope.close()
        input_projection(nc, a["w_in"], h_hi, h_lo, hc_hi, hc_lo, fm, tm, ctx_kv, a["conv_w"], a["conv_b"], conv)

    with ExitStack() as s:
        p = Pool(nc, s)
        with ExitStack() as s2:
            q = Pool(nc, s2, "right")
            yg_hi, yg_lo = q.sb("yg_hi", [P, KT, SEQ], F32R), q.sb("yg_lo", [P, KT, SEQ], F32R)
            retention(nc, fm, tm, ctx_kv, a["decay"], a["rotary"], yg_hi, yg_lo, ident)
            merged = p.sb("merged", [P, KT, SEQ])
            project(nc, "pa", a["w_ret_o"], 2, yg_hi, yg_lo, False, fm[8 * NB:10 * NB, :], merged, False)
        with ExitStack() as s2:
            q = Pool(nc, s2, "right")
            u_hi, u_lo = q.sb("u_hi", [P, KT, SEQ], F32R), q.sb("u_lo", [P, KT, SEQ], F32R)
            conv_norm(nc, conv, a["conv_norm_g"], a["conv_norm_b"], u_hi, u_lo, ones)
            project(nc, "pb", a["w_conv_o"], 2, u_hi, u_lo, False, fm[10 * NB:12 * NB, :], merged, True)
        with ExitStack() as s2:
            q = Pool(nc, s2, "right")
            m_hi, m_lo = q.sb("m_hi", [P, KT, SEQ], F32R), q.sb("m_lo", [P, KT, SEQ], F32R)
            split_tile(nc, "ms", merged, m_hi, m_lo)
            project(nc, "po", a["w_out"], 2, m_hi, m_lo, True, None, merged, False,
                    residual=(a["x"], rows["g1"][:], lat1))
        h2 = Pool(nc, keep, "right")
        hi, lo = h2.sb("h2_hi", [P, KT, SEQ], F32R), h2.sb("h2_lo", [P, KT, SEQ], F32R)
        normalise(nc, "n2", [(merged[:], None)], latent_groups(mod["a2"], mod["b2"], hi, lo), ident,
                  is_scaled=True)
    return hi, lo


def latent_groups(a, b, hi, lo):
    return [(0, 4 * half, 4, k, a[:, k:k + 1], b[:, k:k + 1], hi[:, k, half * HALF:(half + 1) * HALF],
             lo[:, k, half * HALF:(half + 1) * HALF]) for k in range(KT) for half in range(2)]


def layer_program(nc, a, out):
    lat1 = scratch(nc, "lat1", [SEQ, D])
    scores = scratch(nc, "scores", [SEQ, SIDES * N_KEYS])
    gates = scratch(nc, "gates", [SLABS, N_KEYS, N_KEYS, SPAN])
    acts = scratch(nc, "acts", [EARLY, P, SEQ])
    with ExitStack() as keep:
        p = Pool(nc, keep)
        ones, ident = p.sb("ones", [P, P]), p.sb("ident", [P, P])
        mod = {k: p.sb("mod_" + k, [P, KT]) for k in ("a1", "b1", "a2", "b2", "ac", "bc")}
        g2_row = p.sb("row_g2", [P, D])
        constants(nc, ones, ident)
        with ExitStack() as s:
            rows = {"g1": Pool(nc, s).sb("row_g1", [P, D]), "g2": g2_row}
            x_scope = s.enter_context(ExitStack())
            q = Pool(nc, x_scope, "right")
            x, cx = q.sb("x", [P, TT, D]), q.sb("cx", [P, CT, D])
            sources = [(sb[:], a[name].rearrange("(t p) d -> p t d", p=P)) for sb, name in ((x, "x"), (cx, "ctx"))]
            conditioning(nc, a["c_cols"], a["w_mod"], a["b_mod"], a["gain"], mod, rows, ones[:], ident[:], sources)
            h2 = mixer_program(nc, a, lat1, keep, ones[:], ident[:], mod, rows, x, cx, x_scope)
        query_scores(nc, a["w_query"], a["keys"], *h2, scores)
        with ExitStack() as s:
            q = Pool(nc, s)
            first_T, second_T, gate_T = (q.sb(n, [P, SEQ]) for n in ("first_T", "second_T", "gate_T"))
            top_experts(nc, scores, first_T, second_T, gate_T, ident[:], a["u_tiles"], h2, acts)
            gate_matrix(nc, first_T, second_T, gate_T, gates, a["u_tiles"], h2, acts)
        acc = p.sb("retrieved", [P, TT, D])
        early_experts(nc, acts, a["v"], gates, acc)
        experts(nc, a["u_tiles"], a["v"], gates, *h2, acc, lat1, g2_row[:], out)


def kernel(**inputs):
    from concourse import bacc
    from concourse.bass_utils import run_bass_kernel_spmd

    arrays = layout(**inputs)
    nc = bacc.Bacc("TRN2", target_bir_lowering=False, num_devices=1)
    a = {name: nc.dram_tensor("in_" + name, array.shape, mybir.dt.from_np(array.dtype),
                               kind="ExternalInput").ap()
         for name, array in arrays.items()}
    out = nc.dram_tensor("out", (SEQ, D), F32, kind="ExternalOutput").ap()
    layer_program(nc, a, out)
    nc.finalize()
    result = run_bass_kernel_spmd(nc, [{"in_" + name: array for name, array in arrays.items()}], core_ids=[0])
    return result.results[0]["out"][None]
```
